# Optimizing a Trainium2 kernel written in Bass

```python
import math
import jax, jax.numpy as jnp
from jax import lax
import numpy as np

D_MODEL = 1024
BATCH = 1
SEQ = 256
DEPTH = 1

HEAD_DIM = 64
DIL_GROUPS = ((128, 1), (512, 4), (2048, 16))
DIL_HEADS = 4
DIL_WIDTH = len(DIL_GROUPS) * DIL_HEADS * HEAD_DIM
DIL_OUT = DIL_HEADS * HEAD_DIM
SWA_Q_HEADS = 16
SWA_KV_HEADS = 2
SWA_REP = SWA_Q_HEADS // SWA_KV_HEADS
SWA_WINDOW = 128
SWA_Q_WIDTH = SWA_Q_HEADS * HEAD_DIM
SWA_KV_WIDTH = SWA_KV_HEADS * HEAD_DIM
N_ALIBI_HEADS = SWA_Q_HEADS + len(DIL_GROUPS) * DIL_HEADS
ATTN_BLOCK = 128
SPLIT_SIZES = (DIL_WIDTH, DIL_WIDTH, DIL_WIDTH, SWA_Q_WIDTH, SWA_KV_WIDTH, SWA_KV_WIDTH, D_MODEL, D_MODEL)
SPLIT_POINTS = tuple(sum(SPLIT_SIZES[:i + 1]) for i in range(len(SPLIT_SIZES) - 1))
IN_COLS = sum(SPLIT_SIZES)
N_EXPERTS = 32
TOP_K = 4
D_FF = 1024
SWIGLU_LIMIT = 7.0
SWIGLU_ALPHA = 1.702
MOE_BLOCK = 128
LN_EPS = 1e-5
DEEPNORM_ALPHA = (2 * DEPTH) ** 0.25
DEEPNORM_BETA = (8 * DEPTH) ** -0.25
NEG_INF = -1e30


def layer_norm(x, g, b):
    xf = x.astype(jnp.float32)
    mu = jnp.mean(xf, axis=-1, keepdims=True)
    var = jnp.mean(jnp.square(xf - mu), axis=-1, keepdims=True)
    y = (xf - mu) * lax.rsqrt(var + LN_EPS) * g.astype(jnp.float32) + b.astype(jnp.float32)
    return y.astype(x.dtype)

def alibi_slopes():
    h = jnp.arange(1, N_ALIBI_HEADS + 1, dtype=jnp.float32)
    return jnp.exp2(-8.0 * h / N_ALIBI_HEADS)

def banded_attention(q, k, v, slopes, max_diff, dist_scale, sinks):
    n, g, r, L, hd = q.shape
    nb = -(-L // ATTN_BLOCK)
    pad = nb * ATTN_BLOCK - L
    q = jnp.pad(q, ((0, 0), (0, 0), (0, 0), (0, pad), (0, 0)))
    k = jnp.pad(k, ((0, 0), (0, 0), (ATTN_BLOCK, pad), (0, 0)))
    v = jnp.pad(v, ((0, 0), (0, 0), (ATTN_BLOCK, pad), (0, 0)))
    qb = q.reshape(n, g, r, nb, ATTN_BLOCK, hd)
    kb = k.reshape(n, g, nb + 1, ATTN_BLOCK, hd)
    vb = v.reshape(n, g, nb + 1, ATTN_BLOCK, hd)
    kw = jnp.concatenate([kb[:, :, :-1], kb[:, :, 1:]], axis=3)
    vw = jnp.concatenate([vb[:, :, :-1], vb[:, :, 1:]], axis=3)
    s = jnp.einsum('ngrbqd,ngbkd->ngrbqk', qb, kw, preferred_element_type=jnp.float32) * (hd ** -0.5)
    qi = jnp.arange(ATTN_BLOCK)[:, None]
    kj = jnp.arange(2 * ATTN_BLOCK)[None, :]
    diff = qi - kj + ATTN_BLOCK
    kpos = jnp.arange(nb)[:, None, None] * ATTN_BLOCK - ATTN_BLOCK + kj[None]
    valid = (diff >= 0) & (diff <= max_diff) & (kpos >= 0)
    bias = -slopes.astype(jnp.float32)[:, :, None, None, None] * (dist_scale * diff).astype(jnp.float32)
    s = jnp.where(valid, s + bias, NEG_INF)
    m = jnp.max(s, axis=-1)
    if sinks is not None:
        sink = sinks.astype(jnp.float32)[:, :, None, None]
        m = jnp.maximum(m, sink)
    p = jnp.exp(s - m[..., None])
    denom = jnp.sum(p, axis=-1)
    if sinks is not None:
        denom = denom + jnp.exp(sink - m)
    o = jnp.einsum('ngrbqk,ngbkd->ngrbqd', p.astype(v.dtype), vw, preferred_element_type=jnp.float32)
    o = o / denom[..., None]
    lse = m + jnp.log(denom)
    o = o.reshape(n, g, r, nb * ATTN_BLOCK, hd)[:, :, :, :L]
    lse = lse.reshape(n, g, r, nb * ATTN_BLOCK)[:, :, :, :L]
    return o.astype(q.dtype), lse

def dilated_attention(q, k, v, slopes_a):
    b, S, _ = q.shape
    q = q.reshape(b, S, len(DIL_GROUPS), DIL_HEADS, HEAD_DIM)
    k = k.reshape(b, S, len(DIL_GROUPS), DIL_HEADS, HEAD_DIM)
    v = v.reshape(b, S, len(DIL_GROUPS), DIL_HEADS, HEAD_DIM)
    outs, lses = [], []
    for gi, (window, dil) in enumerate(DIL_GROUPS):
        L = S // dil

        def to_sub(t):
            t = t[:, :, gi].reshape(b, L, dil, DIL_HEADS, HEAD_DIM)
            return t.transpose(0, 2, 3, 1, 4).reshape(b * dil, DIL_HEADS, L, HEAD_DIM)

        qs, ks, vs = to_sub(q), to_sub(k), to_sub(v)
        o, lse = banded_attention(qs[:, :, None], ks, vs, slopes_a[gi][:, None],
                                  max_diff=window // dil, dist_scale=dil, sinks=None)
        o = o[:, :, 0].reshape(b, dil, DIL_HEADS, L, HEAD_DIM).transpose(0, 3, 1, 2, 4).reshape(b, S, DIL_HEADS, HEAD_DIM)
        lse = lse[:, :, 0].reshape(b, dil, DIL_HEADS, L).transpose(0, 3, 1, 2).reshape(b, S, DIL_HEADS)
        outs.append(o)
        lses.append(lse)
    w = jax.nn.softmax(jnp.stack(lses, axis=0), axis=0)
    o = jnp.einsum('gbsh,gbshd->bshd', w, jnp.stack(outs, axis=0).astype(jnp.float32))
    return o.reshape(b, S, DIL_OUT).astype(q.dtype)

def swa_sink_attention(q, k, v, slopes_b, sinks):
    b, S, _ = q.shape
    q = q.reshape(b, S, SWA_KV_HEADS, SWA_REP, HEAD_DIM).transpose(0, 2, 3, 1, 4)
    k = k.reshape(b, S, SWA_KV_HEADS, HEAD_DIM).transpose(0, 2, 1, 3)
    v = v.reshape(b, S, SWA_KV_HEADS, HEAD_DIM).transpose(0, 2, 1, 3)
    o, _ = banded_attention(q, k, v, slopes_b, max_diff=SWA_WINDOW - 1, dist_scale=1, sinks=sinks)
    return o.transpose(0, 3, 1, 2, 4).reshape(b, S, SWA_Q_WIDTH)

def token_mixer(x, w_in, sinks, w_proj_a, w_proj_b, w_out, slopes):
    h = jnp.einsum('bsd,dc->bsc', x, w_in)
    a_q, a_k, a_v, b_q, b_k, b_v, g_a, g_b = jnp.split(h, SPLIT_POINTS, axis=-1)
    slopes_b = slopes[:SWA_Q_HEADS].reshape(SWA_KV_HEADS, SWA_REP)
    slopes_a = slopes[SWA_Q_HEADS:].reshape(len(DIL_GROUPS), DIL_HEADS)
    out_a = dilated_attention(a_q, a_k, a_v, slopes_a)
    out_b = swa_sink_attention(b_q, b_k, b_v, slopes_b, sinks.reshape(SWA_KV_HEADS, SWA_REP))
    merged = (jax.nn.sigmoid(g_a) * jnp.einsum('bsc,cd->bsd', out_a, w_proj_a)
              + jax.nn.sigmoid(g_b) * jnp.einsum('bsc,cd->bsd', out_b, w_proj_b))
    return jnp.einsum('bsd,de->bse', merged, w_out)

def moe_ffn(y, router_w, router_b, w_gate, b_gate, w_up, b_up, w_down, b_down):
    b, S, D = y.shape
    n_tok = b * S
    yf = y.reshape(n_tok, D)
    logits = (yf @ router_w + router_b).astype(jnp.float32)
    top_val, top_idx = lax.top_k(logits, TOP_K)
    gates = jax.nn.softmax(top_val, axis=-1)
    n_assign = n_tok * TOP_K
    flat_e = top_idx.reshape(-1)
    order = jnp.argsort(flat_e)
    sorted_e = flat_e[order]
    tok = order // TOP_K
    counts = jnp.zeros((N_EXPERTS,), jnp.int32).at[flat_e].add(1)
    padded = (counts + MOE_BLOCK - 1) // MOE_BLOCK * MOE_BLOCK
    p_end = jnp.cumsum(padded)
    p_start = p_end - padded
    u_start = jnp.cumsum(counts) - counts
    dest = p_start[sorted_e] + jnp.arange(n_assign, dtype=jnp.int32) - u_start[sorted_e]
    n_blocks = -(-n_assign // MOE_BLOCK) + N_EXPERTS
    rows = n_blocks * MOE_BLOCK
    xs = jnp.zeros((rows, D), y.dtype).at[dest].set(yf[tok])
    block_e = jnp.minimum(jnp.searchsorted(p_end, jnp.arange(n_blocks, dtype=jnp.int32) * MOE_BLOCK, side='right'),
                          N_EXPERTS - 1).astype(jnp.int32)

    def expert_block(args):
        xb, e = args
        gt = xb @ w_gate[e] + b_gate[e]
        up = xb @ w_up[e] + b_up[e]
        gt = jnp.minimum(gt, SWIGLU_LIMIT)
        up = jnp.clip(up, -SWIGLU_LIMIT, SWIGLU_LIMIT)
        hdn = gt * jax.nn.sigmoid(SWIGLU_ALPHA * gt) * (up + 1.0)
        return hdn @ w_down[e] + b_down[e]

    ys = lax.map(expert_block, (xs.reshape(n_blocks, MOE_BLOCK, D), block_e)).reshape(rows, D)
    contrib = ys[dest] * gates.reshape(-1)[order][:, None].astype(ys.dtype)
    out = jax.ops.segment_sum(contrib, tok, num_segments=n_tok)
    return out.reshape(b, S, D)

def first_inputs(seed: int = 0) -> dict:
    key = jax.random.key(seed)
    ks = jax.random.split(key, 20)
    f32 = jnp.float32
    beta = DEEPNORM_BETA
    col_scale = jnp.concatenate([
        jnp.ones((2 * DIL_WIDTH,), f32), jnp.full((DIL_WIDTH,), beta, f32),
        jnp.ones((SWA_Q_WIDTH + SWA_KV_WIDTH,), f32), jnp.full((SWA_KV_WIDTH,), beta, f32),
        jnp.ones((2 * D_MODEL,), f32)])
    nrm = lambda k, shape: jax.random.normal(k, shape, f32)
    return {
        "x": nrm(ks[0], (BATCH, SEQ, D_MODEL)),
        "w_in": nrm(ks[1], (DEPTH, D_MODEL, IN_COLS)) * (D_MODEL ** -0.5) * col_scale,
        "sinks": 0.5 * nrm(ks[2], (DEPTH, SWA_Q_HEADS)),
        "w_proj_a": nrm(ks[3], (DEPTH, DIL_OUT, D_MODEL)) * (DIL_OUT ** -0.5),
        "w_proj_b": nrm(ks[4], (DEPTH, SWA_Q_WIDTH, D_MODEL)) * (SWA_Q_WIDTH ** -0.5),
        "w_out": nrm(ks[5], (DEPTH, D_MODEL, D_MODEL)) * (D_MODEL ** -0.5) * beta,
        "ln1_g": 1.0 + 0.05 * nrm(ks[6], (DEPTH, D_MODEL)),
        "ln1_b": 0.02 * nrm(ks[7], (DEPTH, D_MODEL)),
        "router_w": nrm(ks[8], (DEPTH, D_MODEL, N_EXPERTS)) * (D_MODEL ** -0.5),
        "router_b": 0.01 * nrm(ks[9], (DEPTH, N_EXPERTS)),
        "w_gate": nrm(ks[10], (DEPTH, N_EXPERTS, D_MODEL, D_FF)) * (D_MODEL ** -0.5),
        "b_gate": 0.02 * nrm(ks[11], (DEPTH, N_EXPERTS, D_FF)),
        "w_up": nrm(ks[12], (DEPTH, N_EXPERTS, D_MODEL, D_FF)) * (D_MODEL ** -0.5),
        "b_up": 0.02 * nrm(ks[13], (DEPTH, N_EXPERTS, D_FF)),
        "w_down": nrm(ks[14], (DEPTH, N_EXPERTS, D_FF, D_MODEL)) * (D_FF ** -0.5) * beta,
        "b_down": 0.02 * nrm(ks[15], (DEPTH, N_EXPERTS, D_MODEL)),
        "ln2_g": 1.0 + 0.05 * nrm(ks[16], (DEPTH, D_MODEL)),
        "ln2_b": 0.02 * nrm(ks[17], (DEPTH, D_MODEL)),
    }

def first_block(x, w_in, sinks, w_proj_a, w_proj_b, w_out, ln1_g, ln1_b, router_w, router_b,
              w_gate, b_gate, w_up, b_up, w_down, b_down, ln2_g, ln2_b):
    slopes = alibi_slopes()
    for l in range(DEPTH):
        mix = token_mixer(x, w_in[l], sinks[l], w_proj_a[l], w_proj_b[l], w_out[l], slopes)
        x = layer_norm(DEEPNORM_ALPHA * x + mix, ln1_g[l], ln1_b[l])
        ffn = moe_ffn(x, router_w[l], router_b[l], w_gate[l], b_gate[l], w_up[l], b_up[l], w_down[l], b_down[l])
        x = layer_norm(DEEPNORM_ALPHA * x + ffn, ln2_g[l], ln2_b[l])
    return x


DEPTH_2 = 2

GRID_W = 64
CTX_LEN = 256
N_MIXERS = 2
N_A_LAYERS = (DEPTH_2 + N_MIXERS - 1) // N_MIXERS
N_B_LAYERS = DEPTH_2 // N_MIXERS
DN_ALPHA = (2.0 * DEPTH_2) ** 0.25
DN_BETA = (8.0 * DEPTH_2) ** -0.25
CHUNK = 128
ROWS_PER_CHUNK = CHUNK // GRID_W
A_WIDTH = D_MODEL
A_HEADS = 8
A_GROUP = A_WIDTH // A_HEADS
GLA_HEADS = 4
GLA_DK = D_MODEL // 2 // GLA_HEADS
GLA_DV = D_MODEL // GLA_HEADS
GLA_QK = GLA_HEADS * GLA_DK
GLA_V = GLA_HEADS * GLA_DV
GLA_GATE_RANK = 16
GLA_TAU = 16.0
GLA_CHUNK = 64
GLA_IN = 2 * GLA_QK + 2 * GLA_V + 2 * GLA_GATE_RANK
PEER_HEADS = 8
PEER_NKEYS = 128
PEER_EXPERTS = PEER_NKEYS * PEER_NKEYS
PEER_QDIM = 128
PEER_HALF = PEER_QDIM // 2
PEER_TOPK = 16
PEER_BLOCK = 128


def layer_norm_2(x, g, b):
    xf = x.astype(jnp.float32)
    mu = jnp.mean(xf, axis=-1, keepdims=True)
    var = jnp.mean(jnp.square(xf - mu), axis=-1, keepdims=True)
    y = (xf - mu) * lax.rsqrt(var + LN_EPS)
    return (y * g + b).astype(x.dtype)

def chunk_mlp(h, n_chunks, w_in, norm_g, norm_b, w_s, b_s, w_out):
    bsz, t, _ = h.shape
    z = jax.nn.gelu(h @ w_in)
    u, v = jnp.split(z, 2, axis=-1)
    v = layer_norm_2(v, norm_g, norm_b)
    vb = v.reshape(bsz, n_chunks, CHUNK, A_HEADS, A_GROUP)
    s = jnp.einsum('hpq,bnqhc->bnphc', w_s, vb) + b_s.T[None, None, :, :, None]
    return (u * s.reshape(bsz, t, A_WIDTH)) @ w_out

def gla_chunked(q, k, v, g, s0):
    bsz, t, h, dk = q.shape
    dv = v.shape[-1]
    n = t // GLA_CHUNK
    f32 = jnp.float32
    q = q.astype(f32).reshape(bsz, n, GLA_CHUNK, h, dk)
    k = k.astype(f32).reshape(bsz, n, GLA_CHUNK, h, dk)
    v = v.astype(f32).reshape(bsz, n, GLA_CHUNK, h, dv)
    b = jnp.cumsum(g.astype(f32).reshape(bsz, n, GLA_CHUNK, h, dk), axis=2)
    b_end = b[:, :, -1:]
    q_in = q * jnp.exp(b)
    k_in = k * jnp.exp(-b)
    k_end = k * jnp.exp(b_end - b)
    att = jnp.einsum('bnihd,bnjhd->bnhij', q_in, k_in)
    mask = jnp.tril(jnp.ones((GLA_CHUNK, GLA_CHUNK), dtype=bool))
    att = jnp.where(mask, att, 0.0)
    o_intra = jnp.einsum('bnhij,bnjhe->bnihe', att, v)

    def step(state, inp):
        qc, kc, vc, dc = inp
        o = jnp.einsum('bihd,bhde->bihe', qc, state)
        state = dc[..., None] * state + jnp.einsum('bjhd,bjhe->bhde', kc, vc)
        return state, o

    xs = (jnp.moveaxis(q_in, 1, 0), jnp.moveaxis(k_end, 1, 0), jnp.moveaxis(v, 1, 0),
          jnp.moveaxis(jnp.exp(b_end[:, :, 0]), 1, 0))
    s_fin, o_inter = lax.scan(step, s0.astype(f32), xs)
    o = o_intra + jnp.moveaxis(o_inter, 0, 1)
    return o.reshape(bsz, t, h, dv), s_fin

def gla_reverse(q, k, v, g, s0):
    o, s_fin = gla_chunked(jnp.flip(q, 1), jnp.flip(k, 1), jnp.flip(v, 1), jnp.flip(g, 1), s0)
    return jnp.flip(o, 1), s_fin

def gla_project(h, w_in, w_gate, gate_bias):
    bsz, t, _ = h.shape
    z = h @ w_in
    q, k, v, r, gl = jnp.split(z, [GLA_QK, 2 * GLA_QK, 2 * GLA_QK + GLA_V, 2 * GLA_QK + 2 * GLA_V], axis=-1)
    q = q.reshape(bsz, t, GLA_HEADS, GLA_DK) * (GLA_DK ** -0.5)
    k = k.reshape(bsz, t, GLA_HEADS, GLA_DK)
    v = v.reshape(bsz, t, GLA_HEADS, GLA_DV)
    gl = gl.reshape(bsz, t, 2, GLA_GATE_RANK)
    zg = (jnp.einsum('btjr,jrd->btjd', gl, w_gate) + gate_bias).astype(jnp.float32)
    glog = (jax.nn.log_sigmoid(zg) / GLA_TAU).reshape(bsz, t, 2, GLA_HEADS, GLA_DK)
    return q, k, v, r, glog

def gla_readout(o, r, gn_g, w_out):
    bsz, t = o.shape[:2]
    mu = jnp.mean(o, axis=-1, keepdims=True)
    var = jnp.mean(jnp.square(o - mu), axis=-1, keepdims=True)
    y = ((o - mu) * lax.rsqrt(var + LN_EPS)).reshape(bsz, t, GLA_V) * gn_g
    return (y.astype(r.dtype) * jax.nn.silu(r)) @ w_out

def gla_mixer(h_lat, h_ctx, w_in, w_gate, gate_bias, gn_g, w_out, need_ctx_out):
    qc, kc, vc, rc, gc = gla_project(h_ctx, w_in, w_gate, gate_bias)
    ql, kl, vl, rl, gll = gla_project(h_lat, w_in, w_gate, gate_bias)
    s0 = jnp.zeros((h_ctx.shape[0], GLA_HEADS, GLA_DK, GLA_DV), jnp.float32)
    o_cf, s_f = gla_chunked(qc, kc, vc, gc[:, :, 0], s0)
    o_cb, s_b = gla_reverse(qc, kc, vc, gc[:, :, 1], s0)
    o_lf, _ = gla_chunked(ql, kl, vl, gll[:, :, 0], s_f)
    o_lb, _ = gla_reverse(ql, kl, vl, gll[:, :, 1], s_b)
    out_lat = gla_readout(o_lf + o_lb, rl, gn_g, w_out)
    out_ctx = gla_readout(o_cf + o_cb, rc, gn_g, w_out) if need_ctx_out else None
    return out_lat, out_ctx

def peer_ffn(h, w_q, sub_keys, u_tab, v_tab):
    bsz, t, d = h.shape
    blocks = h.reshape(-1, PEER_BLOCK, d)

    def one_block(xb):
        q = (xb @ w_q).reshape(PEER_BLOCK, PEER_HEADS, 2, PEER_HALF)
        s = jnp.einsum('thpd,pkd->thpk', q, sub_keys).astype(jnp.float32)
        s1, i1 = lax.top_k(s[:, :, 0], PEER_TOPK)
        s2, i2 = lax.top_k(s[:, :, 1], PEER_TOPK)
        cand_s = (s1[..., :, None] + s2[..., None, :]).reshape(PEER_BLOCK, PEER_HEADS, PEER_TOPK * PEER_TOPK)
        cand_i = (i1[..., :, None] * PEER_NKEYS + i2[..., None, :]).reshape(PEER_BLOCK, PEER_HEADS, PEER_TOPK * PEER_TOPK)
        top_s, pos = lax.top_k(cand_s, PEER_TOPK)
        idx = jnp.take_along_axis(cand_i, pos, axis=-1)
        wts = jax.nn.softmax(top_s, axis=-1).astype(xb.dtype)
        act = jax.nn.gelu(jnp.einsum('thkd,td->thk', u_tab[idx], xb)) * wts
        return jnp.einsum('thk,thkd->td', act, v_tab[idx])

    return lax.map(one_block, blocks).reshape(bsz, t, d)

def second_inputs(seed: int = 0) -> dict:
    key = jax.random.key(seed)
    ks = jax.random.split(key, 24)
    f32 = jnp.float32

    def nrm(k, shape, s):
        return jax.random.normal(k, shape, f32) * s

    d = D_MODEL
    return {
        "x": nrm(ks[0], (BATCH, SEQ, d), 1.0),
        "c": nrm(ks[1], (BATCH, d), 1.0),
        "ctx": nrm(ks[2], (BATCH, CTX_LEN, d), 1.0),
        "c_ctx": nrm(ks[3], (d,), 1.0),
        "w_mod": nrm(ks[4], (DEPTH_2, d, 6 * d), 0.5 * d ** -0.5),
        "b_mod": nrm(ks[5], (DEPTH_2, 6 * d), 0.01),
        "ln_g": 1.0 + nrm(ks[6], (DEPTH_2, 2, d), 0.01),
        "ln_b": nrm(ks[7], (DEPTH_2, 2, d), 0.01),
        "a_w_in": nrm(ks[8], (N_A_LAYERS, d, 2 * A_WIDTH), d ** -0.5),
        "a_norm_g": 1.0 + nrm(ks[9], (N_A_LAYERS, A_WIDTH), 0.01),
        "a_norm_b": nrm(ks[10], (N_A_LAYERS, A_WIDTH), 0.01),
        "a_w_s": nrm(ks[11], (N_A_LAYERS, A_HEADS, CHUNK, CHUNK), CHUNK ** -0.5),
        "a_b_s": 1.0 + nrm(ks[12], (N_A_LAYERS, A_HEADS, CHUNK), 0.01),
        "a_w_out": nrm(ks[13], (N_A_LAYERS, A_WIDTH, d), DN_BETA * A_WIDTH ** -0.5),
        "b_w_in": nrm(ks[14], (N_B_LAYERS, d, GLA_IN), d ** -0.5),
        "b_w_gate": nrm(ks[15], (N_B_LAYERS, 2, GLA_GATE_RANK, GLA_QK), GLA_GATE_RANK ** -0.5),
        "b_gate_bias": nrm(ks[16], (N_B_LAYERS, 2, GLA_QK), 0.01),
        "b_gn_g": 1.0 + nrm(ks[17], (N_B_LAYERS, GLA_V), 0.01),
        "b_w_out": nrm(ks[18], (N_B_LAYERS, GLA_V, d), DN_BETA * GLA_V ** -0.5),
        "p_w_q": nrm(ks[19], (DEPTH_2, d, PEER_HEADS * PEER_QDIM), d ** -0.5),
        "p_keys": nrm(ks[20], (DEPTH_2, 2, PEER_NKEYS, PEER_HALF), PEER_HALF ** -0.5),
        "p_u": nrm(ks[21], (DEPTH_2, PEER_EXPERTS, d), d ** -0.5),
        "p_v": nrm(ks[22], (DEPTH_2, PEER_EXPERTS, d), DN_BETA),
    }

def second_block(x, c, ctx, c_ctx, w_mod, b_mod, ln_g, ln_b,
              a_w_in, a_norm_g, a_norm_b, a_w_s, a_b_s, a_w_out,
              b_w_in, b_w_gate, b_gate_bias, b_gn_g, b_w_out,
              p_w_q, p_keys, p_u, p_v):
    bsz, seq, d = x.shape
    rows = seq // GRID_W
    lat_chunks = rows // ROWS_PER_CHUNK
    ctx_chunks = ctx.shape[1] // CHUNK
    sc = jax.nn.silu(c)
    sc_ctx = jax.nn.silu(c_ctx)
    for i in range(DEPTH_2):
        last = i == DEPTH_2 - 1
        m = (sc @ w_mod[i] + b_mod[i]).reshape(bsz, 6, d)
        mc = (sc_ctx @ w_mod[i] + b_mod[i]).reshape(6, d)
        sh1, s1, g1, sh2, s2, g2 = [m[:, j, None, :] for j in range(6)]
        sh1c, s1c, g1c, sh2c, s2c, g2c = [mc[j] for j in range(6)]
        h_lat = x * (1.0 + s1) + sh1
        if i % N_MIXERS == 0:
            j = i // N_MIXERS
            prm = (a_w_in[j], a_norm_g[j], a_norm_b[j], a_w_s[j], a_b_s[j], a_w_out[j])
            mix_lat = chunk_mlp(h_lat, lat_chunks, *prm)
            mix_ctx = None if last else chunk_mlp(ctx * (1.0 + s1c) + sh1c, ctx_chunks, *prm)
        else:
            j = i // N_MIXERS
            h_ctx = ctx * (1.0 + s1c) + sh1c
            mix_lat, mix_ctx = gla_mixer(h_lat, h_ctx, b_w_in[j], b_w_gate[j], b_gate_bias[j],
                                         b_gn_g[j], b_w_out[j], not last)
        x = layer_norm_2(DN_ALPHA * x + g1 * mix_lat, ln_g[i, 0], ln_b[i, 0])
        ffn_lat = peer_ffn(x * (1.0 + s2) + sh2, p_w_q[i], p_keys[i], p_u[i], p_v[i])
        x = layer_norm_2(DN_ALPHA * x + g2 * ffn_lat, ln_g[i, 1], ln_b[i, 1])
        if not last:
            ctx = layer_norm_2(DN_ALPHA * ctx + g1c * mix_ctx, ln_g[i, 0], ln_b[i, 0])
            ffn_ctx = peer_ffn(ctx * (1.0 + s2c) + sh2c, p_w_q[i], p_keys[i], p_u[i], p_v[i])
            ctx = layer_norm_2(DN_ALPHA * ctx + g2c * ffn_ctx, ln_g[i, 1], ln_b[i, 1])
    return x


def setup_inputs(seed=0):
    out = dict(first_inputs(seed))
    for name, value in second_inputs(seed + 1).items():
        if name != "x":
            out[name + "_2"] = value
    return out


def reference(
    x, w_in, sinks, w_proj_a, w_proj_b, w_out, ln1_g, ln1_b, router_w, router_b, w_gate, b_gate,
    w_up, b_up, w_down, b_down, ln2_g, ln2_b, c_2, ctx_2, c_ctx_2, w_mod_2, b_mod_2, ln_g_2,
    ln_b_2, a_w_in_2, a_norm_g_2, a_norm_b_2, a_w_s_2, a_b_s_2, a_w_out_2, b_w_in_2, b_w_gate_2,
    b_gate_bias_2, b_gn_g_2, b_w_out_2, p_w_q_2, p_keys_2, p_u_2, p_v_2,
):
    x = first_block(
        x, w_in, sinks, w_proj_a, w_proj_b, w_out, ln1_g, ln1_b, router_w, router_b, w_gate,
        b_gate, w_up, b_up, w_down, b_down, ln2_g, ln2_b,
    )
    return second_block(
        x, c_2, ctx_2, c_ctx_2, w_mod_2, b_mod_2, ln_g_2, ln_b_2, a_w_in_2, a_norm_g_2,
        a_norm_b_2, a_w_s_2, a_b_s_2, a_w_out_2, b_w_in_2, b_w_gate_2, b_gate_bias_2, b_gn_g_2,
        b_w_out_2, p_w_q_2, p_keys_2, p_u_2, p_v_2,
    )


_drawn_inputs = setup_inputs


def setup_inputs(seed=0):
    import zlib

    import numpy as np

    out = dict(_drawn_inputs(seed))
    spreads = {}
    factors = {'sinks': 4.695,
     'b_gate': 6.561,
     'b_up': 8.0,
     'b_down': 4.538,
     'ctx_2': 4.363,
     'c_ctx_2': 5.753,
     'b_mod_2': 4.662,
     'a_norm_g_2': 27.799,
     'a_norm_b_2': 30.034,
     'a_b_s_2': 35.668,
     'b_w_gate_2': 4.322,
     'b_gate_bias_2': 8.0,
     'b_gn_g_2': 64.0}
    for name, (base, spread) in spreads.items():
        noise = np.random.default_rng([zlib.crc32(name.encode()), seed]).standard_normal(out[name].shape)
        drawn = base * np.exp(spread * noise) if base else spread * noise
        out[name] = __import__('jax').numpy.asarray(drawn.astype(out[name].dtype))
    for name, factor in factors.items():
        out[name] = (out[name] * factor).astype(out[name].dtype)
    return out
```

```python
from contextlib import ExitStack

import numpy as np
import concourse.bass as bass
from concourse import mybir

F32 = mybir.dt.float32
U32 = mybir.dt.uint32
I32 = mybir.dt.int32
ALU = mybir.AluOpType
ACT = mybir.ActivationFunctionType
AX = mybir.AxisListType

P = 128
D = 1024
KT = D // P
T = 256
TT = T // P
HD = 64
EPS = 1e-5
DIL_HEADS, DIL_GROUPS, SWA_PAIRS = 4, 3, 8
N_SLOPES = 28
SLOPES = [float(np.float32(2.0 ** (-8.0 * (h + 1) / N_SLOPES))) for h in range(N_SLOPES)]
Q_A, K_A, Q_B, K_B, V_T, GATE = 0, 6, 12, 20, 21, 28
V_COLS = 896
N_IN = 11
ALPHA1 = 2.0 ** 0.25
FAR = -1e34
NE, TOPK, SLOTS = 32, 4, 64
PASSES = T // SLOTS
PER_EXPERT = 6
LIMIT, SW_ALPHA = 7.0, 1.702
ALPHA2 = 4.0 ** 0.25
PH, PK, NKEY = 8, 16, 128
GH, DK, DV, RANK, TAU = 4, 128, 256, 16, 16.0
CH = 64
LOWEST = -3.0e38
SLOT = KT * 512
NSLOT = 6


class Marks:

    def __init__(self, nc, ctx):
        self.nc, self.ctx, self.sems, self.n, self.spare = nc, ctx, {}, {}, []

    def __call__(self, name):
        if name not in self.sems:
            self.sems[name] = self.spare.pop() if self.spare else self.ctx.enter_context(self.nc.semaphore(name))
        return self.sems[name]

    def retire(self, kept):
        names = [n for n in self.sems if not n.startswith(kept)]
        with self.nc.Block() as block:

            @block.sync
            def _(sp):
                for name in names:
                    sp.sem_clear(self.sems[name])

        for name in names:
            self.spare.append(self.sems.pop(name))
            self.n.pop(name, None)

    def up(self, ins, name, by=1):
        ins.then_inc(self(name), by)
        self.n[name] = self.n.get(name, 0) + by
        return self.n[name]


class Chain:

    def __init__(self, marks, eng, name):
        self.marks, self.eng, self.name = marks, eng, name

    def __call__(self, ins, name=None):
        name = name or self.name
        value = self.marks.up(ins, name)
        self.eng.wait_ge(self.marks(name), value)


class Banks:

    def __init__(self, marks):
        self.marks, self.used = marks, [0] * 8

    def plan(self, names, banks):
        table = {}
        for i, name in enumerate(names):
            bank = banks[i % len(banks)]
            table[name] = (bank, self.used[bank])
            self.used[bank] += 1
        return table

    def wait_free(self, pe, where):
        bank, nth = where
        if nth:
            pe.wait_ge(self.marks(f"bank_free{bank}"), nth)

    def fill(self, ins, where):
        ins.then_inc(self.marks(f"bank_full{where[0]}"), 1)

    def wait_full(self, eng, where):
        eng.wait_ge(self.marks(f"bank_full{where[0]}"), where[1] + 1)

    def free(self, ins, where):
        ins.then_inc(self.marks(f"bank_free{where[0]}"), 1)

    def free_chained(self, eng, ins, where):
        ins.then_inc(self.marks(f"bank_free{where[0]}"), 1)
        eng.wait_ge(self.marks(f"bank_free{where[0]}"), where[1] + 1)


class Ring:

    def __init__(self, marks, mem, chunks):
        self.marks, self.mem, self.chunks, self.sent = marks, mem, chunks, 0
        self.at = {}
        for n, (name, _, _) in enumerate(chunks):
            self.at.setdefault(name, n)

    def load(self, sp, end):
        for n in range(self.sent, min(end, len(self.chunks))):
            slot, nth = n % NSLOT, n // NSLOT
            _, src, size = self.chunks[n]
            if nth:
                sp.wait_ge(self.marks(f"chunk_used{slot}"), nth)
            sp.dma_start(self.mem[:, slot, 0:size], src).then_inc(self.marks(f"chunk_in{slot}"), 16)
        self.sent = max(self.sent, min(end, len(self.chunks)))

    def upto(self, name, count):
        return self.at[name] + count + NSLOT

    def wait(self, pe, name, i=0):
        n = self.at[name] + i
        pe.wait_ge(self.marks(f"chunk_in{n % NSLOT}"), 16 * (n // NSLOT + 1))
        return self.mem[:, n % NSLOT, :].rearrange("p (k j) -> p k j", k=KT)

    def used(self, ins, name, i=0):
        ins.then_inc(self.marks(f"chunk_used{(self.at[name] + i) % NSLOT}"), 1)


def products(nc, out, pairs):
    for i, (lhs, rhs) in enumerate(pairs):
        last = nc.tensor.matmul(out, lhs, rhs, start=i == 0, stop=i == len(pairs) - 1)
    return last


class Memory:

    def __init__(self, nc, ctx):
        def sb(name, shape, dtype=F32):
            return ctx.enter_context(nc.sbuf_tensor("sb_" + name, shape, dtype))

        self.ring = sb("ring", [P, NSLOT, SLOT])
        self.arena = sb("arena", [P, 16384])
        self.H = sb("H", [P, 4, D])
        self.X = sb("X", [P, 4, D])
        self.consts = sb("consts", [P, CONST_COLS])
        self.idx = sb("idx", [P, 4 * P + PK], U32)
        self.wts = sb("wts", [P, 4 * P])
        self.diag = [sb(f"diag{i}", [P, P])[:, :] for i in range(4)]
        self.cur_idx = sb("cur_idx", [P, 2 * PK], U32)
        self.dots = sb("dots", [P, PK])
        self.act = sb("act", [P, PK])
        self.stats = sb("stats", [P, 64])
        self.count = sb("count", [1, 2], I32)
        self.norms, self.rows_sent = 0, 0
        self.ps = ctx.enter_context(nc.psum_tensor("ps", [P, 8, 512], F32))

    def const(self, name):
        a, n = CONST_AT[name]
        return self.consts[:, a:a + n]

    def part(self, start, *dims):
        size = int(np.prod(dims))
        flat = self.arena[:, start:start + size]
        names = "abcd"[:len(dims)]
        if len(dims) == 1:
            return flat
        return flat.rearrange(f"p ({' '.join(names)}) -> p {' '.join(names)}",
                              **{n: d for n, d in zip(names, dims)})


def constants():
    j, i = np.arange(P)[:, None], np.arange(P)[None, :]
    same = (j // CH) == (i // CH)
    parts = {
        "ident": (j == i),
        "upto": (j <= i),
        "ones": np.ones((P, P)),
        "fwd": (j <= i) & same,
        "bwd": (j >= i) & same,
        "after": (j > i) & same,
        "before": (j < i) & same,
        "chunk": j // CH == np.arange(2)[None, :],
        "iota": np.broadcast_to(np.arange(CH), (P, CH)),
        "zero": np.zeros((P, P)),
    }
    return parts


CONST_AT, CONST_COLS = {}, 0
for _name, _a in constants().items():
    CONST_AT[_name] = (CONST_COLS, _a.shape[1])
    CONST_COLS += _a.shape[1]


def distances():
    out = np.full((P, 4, 384), FAR, np.float32)
    for block, (at, nk) in enumerate(((0, 128), (128, 256))):
        i, j = block * P + np.arange(P)[:, None], np.arange(nk)[None, :]
        d = i - j
        seen = [(d >= 0) & (d <= 127), (d >= 0) & (d <= 128), (d >= 0) & (d % 4 == 0), (d >= 0) & (d % 16 == 0)]
        for kind, s in enumerate(seen):
            out[:, kind, at:at + nk] = np.where(s, -d, FAR)
    return out



def attention(nc, d, m, M, banks, ring):
    qk = m.part(0, 21, T)
    v = m.part(5376, TT, V_COLS)
    gates = m.part(7168, 16, T)
    oT = m.part(11264, 10, T)
    pT = m.part(13824, 2, 6, P)
    tmp = m.part(15360, 2, T)
    rows = m.H[:, :, :].rearrange("p a b -> p (a b)")
    xT = rows[:, 0:2048].rearrange("p (k t) -> p k t", k=KT)
    sc = rows[:, 2048:2048 + 2 * 772].rearrange("p (u c) -> p u c", u=2)
    spare = m.X[:, 2:4, :].rearrange("p a b -> p (a b)")
    dist = spare[:, 0:1536].rearrange("p (k c) -> p k c", k=4)
    sinks = spare[:, 1536:1552]
    X = m.X
    ident = m.const("ident")

    units = [("dil", h, b) for b in range(TT) for h in range(DIL_HEADS)]
    units += [("swa", t, b) for b in range(TT) for t in range(SWA_PAIRS)]

    def blocks(unit):
        return (DIL_GROUPS if unit[0] == "dil" else 2), unit[2] + 1

    proj = [("qk", n) for n in range(10)] + [("kb", 0)] + [("v", i) for i in range(4)]
    proj += [("gate", n) for n in range(8)]
    gp = banks.plan(proj, [0, 1, 2, 3])
    go = banks.plan([("o", u) for u in range(len(units))], [6, 7])
    gm = banks.plan([("m", i) for i in range(KT)], [0, 1, 2, 3])
    gx = banks.plan([("x", i) for i in range(4)], [4, 5, 6, 7])

    with nc.Block() as block:

        @block.sync
        def _(sp):
            sp.dma_start(xT, d["xT"]).then_inc(M("xT_in"), 16)
            ring.load(sp, 2)
            sp.dma_start(m.consts[:, :], d["consts"]).then_inc(M("consts_in"), 16)
            sp.dma_start(dist, d["dist"]).then_inc(M("dist_in"), 16)
            sp.dma_start(sinks, d["sinks"].to_broadcast([P, 16])).then_inc(M("dist_in"), 16)
            sp.dma_start(X[:, 0:TT, :], d["x"].rearrange("(t p) c -> p t c", p=P)).then_inc(M("x_in"), 16)
            ring.load(sp, ring.upto("w_out", 2))

        @block.tensor
        def _(pe):
            pe.wait_ge(M("xT_in"), 16)

            def channel_tile(chunk, j, out):
                return products(nc, out, [(w[:, k, j * P:(j + 1) * P], xT[:, k, :]) for k in range(KT)])

            w = ring.wait(pe, "w_in", 0)
            for n in range(10):
                if n and n % 2 == 0:
                    w = ring.wait(pe, "w_in", n // 2)
                where = gp["qk", n]
                banks.wait_free(pe, where)
                channel_tile(w, 2 * (n % 2), m.ps[:, where[0], 0:T])
                last = channel_tile(w, 2 * (n % 2) + 1, m.ps[:, where[0], T:2 * T])
                banks.fill(last, where)
                if n % 2:
                    pe.wait_ge(M(f"bank_full{where[0]}"), where[1] + 1)
                    pe.sem_inc(M(f"chunk_used{(ring.at['w_in'] + n // 2) % NSLOT}"), 1)
            w = ring.wait(pe, "w_in", 5)
            where = gp["kb", 0]
            banks.wait_free(pe, where)
            banks.fill(channel_tile(w, 0, m.ps[:, where[0], 0:T]), where)
            for i in range(4):
                t, piece = i % 2, i // 2
                if i == 2:
                    w = ring.wait(pe, "w_in", 6)
                cols = slice(P, 512) if piece == 0 else slice(0, 512)
                where = gp["v", i]
                banks.wait_free(pe, where)
                last = products(nc, m.ps[:, where[0], 0:cols.stop - cols.start],
                                [(xT[:, k, t * P:(t + 1) * P], w[:, k, cols]) for k in range(KT)])
                banks.fill(last, where)
                if t:
                    pe.wait_ge(M(f"bank_full{where[0]}"), where[1] + 1)
                    pe.sem_inc(M(f"chunk_used{(ring.at['w_in'] + 5 + piece) % NSLOT}"), 1)
            for n in range(8):
                if n % 2 == 0:
                    w = ring.wait(pe, "w_in", 7 + n // 2)
                where = gp["gate", n]
                banks.wait_free(pe, where)
                channel_tile(w, 2 * (n % 2), m.ps[:, where[0], 0:T])
                last = channel_tile(w, 2 * (n % 2) + 1, m.ps[:, where[0], T:2 * T])
                banks.fill(last, where)
                if n % 2:
                    pe.wait_ge(M(f"bank_full{where[0]}"), where[1] + 1)
                    pe.sem_inc(M(f"chunk_used{(ring.at['w_in'] + 7 + n // 2) % NSLOT}"), 1)

            def scores(u):
                kind, h, b = units[u]
                nk = P * (b + 1)
                out = m.ps[:, 2 * (u % 2):2 * (u % 2) + 2, :].rearrange("p a b -> p (a b)")
                if u >= 2:
                    pe.wait_ge(M("scores_read"), u - 1)
                for g in range(blocks(units[u])[0]):
                    if kind == "dil":
                        rows_ = slice((h % 2) * HD, (h % 2) * HD + HD)
                        qt, kt = Q_A + 2 * g + h // 2, K_A + 2 * g + h // 2
                    else:
                        rows_ = slice(g * HD, (g + 1) * HD)
                        qt, kt = Q_B + h, K_B
                    at = g * nk if kind == "dil" else g * 512
                    last = nc.tensor.matmul(out[:, at:at + nk], qk[rows_, qt, b * P:(b + 1) * P],
                                            qk[rows_, kt, 0:nk], start=True, stop=True)
                last.then_inc(M("scores_done"), 1)

            pe.wait_ge(M("qkv_ready"), 15)
            pe.wait_ge(M("consts_in"), 16)
            pe.wait_ge(M("gates_ready"), 8)
            scores(0)
            scores(1)
            for u, unit in enumerate(units):
                n_seg, nb = blocks(unit)
                turned = m.ps[:, 4:6, :].rearrange("p a b -> p (a b)")
                pe.wait_ge(M("probs_ready"), u + 1)
                if u:
                    pe.wait_ge(M("probsT_ready"), u)
                stride = nb * P + (1 if unit[0] == "swa" else 0)
                for g in range(n_seg):
                    for kb in range(nb):
                        at = g * stride + kb * P
                        i = g * nb + kb
                        last = nc.tensor.transpose(turned[:, i * P:(i + 1) * P], sc[:, u % 2, at:at + P], ident)
                last.then_inc(M("probsT_done"), 1)
                if u + 2 < len(units):
                    scores(u + 2)
                pe.wait_ge(M("probsT_ready"), u + 1)
                where = go["o", u]
                banks.wait_free(pe, where)
                kind, h, b = unit
                for g in range(n_seg):
                    for kb in range(nb):
                        i = g * nb + kb
                        if kind == "dil":
                            rows_ = slice((h % 2) * HD, (h % 2) * HD + HD)
                            col, start, stop = g * 256 + h * HD, i == 0, i == n_seg * nb - 1
                        else:
                            rows_ = slice(g * HD, (g + 1) * HD)
                            col, start, stop = 768 + g * HD, kb == 0, kb == nb - 1
                        last = nc.tensor.matmul(m.ps[rows_, where[0], 0:P], v[:, kb, col:col + HD],
                                                pT[:, u % 2, i, :], start=start, stop=stop)
                banks.fill(last, where)

            wa = ring.wait(pe, "w_proj_a", 0)
            wa = ring.mem[:, ring.at["w_proj_a"] % NSLOT, 0:2048].rearrange("p (k j) -> p k j", k=2)
            pe.wait_ge(M("o_ready"), len(units))
            for i in range(KT):
                if i % 4 == 0:
                    wb = ring.wait(pe, "w_proj_b", i // 4)
                where = gm["m", i]
                banks.wait_free(pe, where)
                products(nc, m.ps[:, where[0], 0:T], [(wa[:, k, i * P:(i + 1) * P], oT[:, k, :]) for k in range(2)])
                j = i % 4
                last = products(nc, m.ps[:, where[0], T:2 * T],
                                [(wb[:, k, j * P:(j + 1) * P], oT[:, 2 + k, :]) for k in range(KT)])
                banks.fill(last, where)
                if j == 3:
                    pe.wait_ge(M(f"bank_full{where[0]}"), where[1] + 1)
                    pe.sem_inc(M(f"chunk_used{(ring.at['w_proj_b'] + i // 4) % NSLOT}"), 1)
                    if i == KT - 1:
                        pe.sem_inc(M(f"chunk_used{ring.at['w_proj_a'] % NSLOT}"), 1)
            pe.wait_ge(M("merged_ready"), KT)
            for i in range(4):
                half, t = i // 2, i % 2
                w = ring.wait(pe, "w_out", half)
                where = gx["x", i]
                banks.wait_free(pe, where)
                last = products(nc, m.ps[:, where[0], :], [(gates[:, k, t * P:(t + 1) * P], w[:, k, :]) for k in range(KT)])
                banks.fill(last, where)
                if t:
                    pe.wait_ge(M(f"bank_full{where[0]}"), where[1] + 1)
                    pe.sem_inc(M(f"chunk_used{(ring.at['w_out'] + half) % NSLOT}"), 1)

        @block.scalar
        def _(act):
            for n in range(10):
                where = gp["qk", n]
                banks.wait_full(act, where)
                is_q = n < 3 or n >= 6
                ins = nc.scalar.activation(qk[:, 2 * n:2 * n + 2, :].rearrange("p a b -> p (a b)"), m.ps[:, where[0], :],
                                           ACT.Copy, scale=HD ** -0.5 if is_q else 1.0)
                banks.free_chained(act, ins, where)
                act.sem_inc(M("qkv_ready"), 1)
            where = gp["kb", 0]
            banks.wait_full(act, where)
            banks.free_chained(act, nc.scalar.activation(qk[:, K_B, :], m.ps[:, where[0], 0:T], ACT.Copy), where)
            act.sem_inc(M("qkv_ready"), 1)
            for i in range(4):
                t, piece = i % 2, i // 2
                where = gp["v", i]
                banks.wait_full(act, where)
                dst = v[:, t, 0:384] if piece == 0 else v[:, t, 384:V_COLS]
                banks.free_chained(act, nc.scalar.activation(dst, m.ps[:, where[0], 0:384 if piece == 0 else 512], ACT.Copy), where)
                act.sem_inc(M("qkv_ready"), 1)
            for n in range(8):
                where = gp["gate", n]
                banks.wait_full(act, where)
                ins = nc.scalar.activation(gates[:, 2 * n:2 * n + 2, :].rearrange("p a b -> p (a b)"), m.ps[:, where[0], :], ACT.Sigmoid)
                banks.free_chained(act, ins, where)
                act.sem_inc(M("gates_ready"), 1)

            def exps(u):
                kind, h, b = units[u]
                nk = P * (b + 1)
                act.wait_ge(M("max_ready"), u + 1)
                n, width = (1, 3 * nk) if kind == "dil" else (2, nk + 1)
                for s in range(n):
                    part = sc[:, u % 2, s * width:(s + 1) * width]
                    ins = nc.scalar.activation(part, part, ACT.Exp, bias=m.stats[:, 4 + 2 * (u % 2) + s:5 + 2 * (u % 2) + s],
                                               accum_out=m.stats[:, 8 + 2 * (u % 2) + s:9 + 2 * (u % 2) + s])
                ins.then_inc(M("exp_done"), 1)

            def turn(u):
                n_seg, nb = blocks(units[u])
                act.wait_ge(M("probsT_done"), u + 1)
                if u >= 2:
                    banks.wait_full(act, go["o", u - 2])
                n = n_seg * nb * P
                nc.scalar.activation(pT[:, u % 2, :, :].rearrange("p a b -> p (a b)")[:, 0:n],
                                     m.ps[:, 4:6, :].rearrange("p a b -> p (a b)")[:, 0:n], ACT.Copy)\
                    .then_inc(M("probsT_ready"), 1)

            exps(0)
            for u in range(len(units)):
                if u + 1 < len(units):
                    exps(u + 1)
                turn(u)

        @block.vector
        def _(dve):
            step = Chain(M, dve, "dve_step")
            dve.wait_ge(M("dist_in"), 32)

            def biased(u):
                kind, h, b = units[u]
                nk = P * (b + 1)
                dve.wait_ge(M("scores_done"), u + 1)
                if u >= 2:
                    dve.wait_ge(M("probsT_done"), u - 1)
                scores_ = m.ps[:, 2 * (u % 2):2 * (u % 2) + 2, :].rearrange("p a b -> p (a b)")
                at = 0 if b == 0 else P
                n_seg = blocks(units[u])[0]
                for g in range(n_seg):
                    if kind == "dil":
                        kindd, slope, col, src = 1 + g, SLOPES[16 + 4 * g + h], g * nk, g * nk
                    else:
                        kindd, slope, col, src = 0, SLOPES[8 * g + h], g * (nk + 1), g * 512
                        nc.vector.tensor_copy(sc[:, u % 2, col + nk:col + nk + 1], sinks[:, 8 * g + h:8 * g + h + 1]).then_inc(M("sink_set"), 1)
                    last = nc.vector.scalar_tensor_tensor(
                        out=sc[:, u % 2, col:col + nk], in0=dist[:, kindd, at:at + nk], scalar=slope,
                        in1=scores_[:, src:src + nk], op0=ALU.mult, op1=ALU.add)
                last.then_inc(M("scores_read"), 1)
                dve.wait_ge(M("scores_read"), u + 1)
                n, width = (1, 3 * nk) if kind == "dil" else (2, nk + 1)
                step(nc.vector.tensor_reduce(m.stats[:, 0:n], sc[:, u % 2, 0:n * width].rearrange("p (s c) -> p s c", s=n),
                                             axis=AX.X, op=ALU.max))
                nc.vector.tensor_scalar(m.stats[:, 4 + 2 * (u % 2):4 + 2 * (u % 2) + n], m.stats[:, 0:n], -1.0, None, ALU.mult)\
                    .then_inc(M("max_ready"), 1)
                dve.wait_ge(M("max_ready"), u + 1)

            def normal(u):
                kind, h, b = units[u]
                nk = P * (b + 1)
                dve.wait_ge(M("exp_done"), u + 1)
                n, width = (1, 3 * nk) if kind == "dil" else (2, nk + 1)
                den = m.stats[:, 8 + 2 * (u % 2):8 + 2 * (u % 2) + n]
                step(nc.vector.reciprocal(m.stats[:, 12:12 + n], den))
                p3 = sc[:, u % 2, 0:n * width].rearrange("p (s c) -> p s c", s=n)
                nc.vector.tensor_tensor(p3, p3, m.stats[:, 12:12 + n].rearrange("p (s c) -> p s c", c=1).to_broadcast([P, n, width]),
                                        ALU.mult).then_inc(M("probs_ready"), 1)
                dve.wait_ge(M("probs_ready"), u + 1)

            def out_of(u):
                kind, h, b = units[u]
                where = go["o", u]
                banks.wait_full(dve, where)
                if kind == "dil":
                    rows_, tile = slice((h % 2) * HD, (h % 2) * HD + HD), h // 2
                else:
                    rows_, tile = slice(0, P), 2 + h
                ins = nc.vector.tensor_copy(oT[rows_, tile, b * P:(b + 1) * P], m.ps[rows_, where[0], 0:P])
                banks.free_chained(dve, ins, where)
                dve.sem_inc(M("o_ready"), 1)

            biased(0)
            for u in range(len(units)):
                if u + 1 < len(units):
                    biased(u + 1)
                normal(u)
                if u:
                    out_of(u - 1)
            out_of(len(units) - 1)
            dve.wait_ge(M("gates_ready"), 8)
            both = m.part(7168, 2, KT, T)
            for i in range(KT):
                where = gm["m", i]
                banks.wait_full(dve, where)
                ins = nc.vector.tensor_tensor(tmp, m.ps[:, where[0], :].rearrange("p (a b) -> p a b", a=2), both[:, :, i, :], ALU.mult)
                banks.free_chained(dve, ins, where)
                nc.vector.tensor_tensor(gates[:, i, :], tmp[:, 0, :], tmp[:, 1, :], ALU.add).then_inc(M("merged_ready"), 1)
                dve.wait_ge(M("merged_ready"), i + 1)
            dve.wait_ge(M("x_in"), 16)
            for i in range(4):
                half, t = i // 2, i % 2
                where = gx["x", i]
                banks.wait_full(dve, where)
                part = X[:, t, half * 512:(half + 1) * 512]
                ins = nc.vector.scalar_tensor_tensor(out=part, in0=part, scalar=ALPHA1, in1=m.ps[:, where[0], :], op0=ALU.mult, op1=ALU.add)
                banks.free_chained(dve, ins, where)



LN = {"sum": (16, 28), "mv": (28, 30), "var": (30, 31), "std": (31, 32), "rstd": (32, 33)}


def stat(m, name):
    a, b = LN[name]
    return m.stats[:, a:b]


def norm_dve(nc, dve, step, m, M, x, n, out=None):
    out = x if out is None else out
    width = x.shape[-1]
    pieces = max(1, width // 512)
    for i in range(pieces):
        piece = x[:, i * 512:(i + 1) * 512] if pieces > 1 else x
        step(nc.vector.bn_stats(m.stats[:, 16 + 6 * i:22 + 6 * i], piece))
    step(nc.vector.bn_aggr(stat(m, "mv"), m.stats[:, 16:16 + 6 * pieces]))
    step(nc.vector.tensor_scalar(stat(m, "var"), m.stats[:, 29:30], EPS, None, ALU.add), "variance_ready")
    dve.wait_ge(M("std_ready"), n)
    step(nc.vector.reciprocal(stat(m, "rstd"), stat(m, "std")))
    step(nc.vector.tensor_scalar(out, x, m.stats[:, 28:29], stat(m, "rstd"), ALU.subtract, ALU.mult))


def norm_act(nc, act, m, M, n):
    act.wait_ge(M("variance_ready"), n)
    nc.scalar.activation(stat(m, "std"), stat(m, "var"), ACT.Sqrt).then_inc(M("std_ready"), 1)


def row(m, i):
    return m.part(12288, 4, D)[:, i, :]


def load_rows(sp, M, m, sources):
    for i, src in enumerate(sources):
        sp.dma_start(row(m, i), src.to_broadcast([P, D])).then_inc(M("rows_in"), 16)
    m.rows_sent += 16 * len(sources)



class Experts:

    def __init__(self, m):
        self.yT = m.part(0, KT, T)
        self.router = m.part(4096, KT, NE)
        self.router_b = m.part(4352, NE)
        self.logits = m.part(4384, TT, NE)
        self.gates = m.part(4448, TT, NE)
        self.chosen = m.part(4512, TT, NE)
        self.place = m.part(4576, TT, NE + 1)
        self.onehot = m.part(4672, NE)
        self.top = m.part(4704, TT, 8)
        self.top_i = m.part(4720, TT, 8)
        self.top_at = m.arena[:, 4736:4744].bitcast(U32)
        self.exp = m.part(4752, 8)
        self.gatesT = m.part(4800, T)
        self.total = m.part(5056, NE + 2)
        self.b_gate = m.part(5120, NE * KT, 1)
        self.b_up = m.part(5376, NE * KT, 1)
        self.b_down = m.part(5632, D)
        self.pick = m.part(6656, TT, SLOTS)
        self.weigh = m.part(6784, TT, SLOTS)
        self.weighT = m.part(6912, T)
        self.xe = m.part(7168, KT, SLOTS)
        self.g = m.part(7680, KT, SLOTS)
        self.sig = m.part(8192, KT, SLOTS)
        self.u = m.part(8704, KT, SLOTS)
        self.h = m.part(9216, KT, SLOTS)
        self.ye = m.part(9728, D)


def route(nc, d, m, M, banks, ring):
    x = Experts(m)
    n0 = m.norms
    m.norms += TT
    turn = banks.plan([("t", i) for i in range(4)], [4, 5, 6, 7])
    small = banks.plan([("logit", t) for t in range(TT)] + [("place", t) for t in range(TT)] + ["total", "gT"], [0, 1, 2, 3])
    with nc.Block() as block:

        @block.sync
        def _(sp):
            load_rows(sp, M, m, [d["lns"][i:i + 1, :] for i in range(4)])
            for dst, src in ((x.router, d["router_w"]), (x.router_b[0:1, :], d["router_b"]), (x.b_gate[:, :, 0], d["b_gate"]),
                             (x.b_up[:, :, 0], d["b_up"]), (x.b_down[0:NE, :], d["b_down"])):
                sp.dma_start(dst, src).then_inc(M("router_in"), 16)
            ring.load(sp, ring.at["moe"] + NSLOT)

        @block.tensor
        def _(pe):
            ident = m.const("ident")
            for i in range(4):
                t, half = i // 2, i % 2
                where = turn["t", i]
                banks.wait_free(pe, where)
                pe.wait_ge(M("y_ready"), t + 1)
                for k in range(4):
                    c = (4 * half + k) * P
                    last = nc.tensor.transpose(m.ps[:, where[0], k * P:(k + 1) * P], m.X[:, t, c:c + P], ident)
                banks.fill(last, where)
            pe.wait_ge(M("router_in"), 5 * 16)
            pe.wait_ge(M("yT_ready"), 4)
            for t in range(TT):
                where = small["logit", t]
                banks.wait_free(pe, where)
                pairs = [(x.yT[:, k, t * P:(t + 1) * P], x.router[:, k, :]) for k in range(KT)]
                pairs.append((m.const("ones")[0:1, :], x.router_b[0:1, :]))
                banks.fill(products(nc, m.ps[:, where[0], 0:NE], pairs), where)
            pe.wait_ge(M("gates_known"), TT)
            for t in range(TT):
                where = small["place", t]
                banks.wait_free(pe, where)
                pairs = [(m.const("ones"), x.chosen[:, s, :]) for s in range(t)] + [(m.const("upto"), x.chosen[:, t, :])]
                banks.fill(products(nc, m.ps[:, where[0], 0:NE], pairs), where)
            where = small["total"]
            banks.wait_free(pe, where)
            banks.fill(products(nc, m.ps[0:1, where[0], 0:NE], [(m.const("ones")[:, 0:1], x.chosen[:, t, :]) for t in range(TT)]), where)
            where = small["gT"]
            banks.wait_free(pe, where)
            for t in range(TT):
                last = nc.tensor.transpose(m.ps[0:NE, where[0], t * P:(t + 1) * P], x.gates[:, t, :], ident)
            banks.fill(last, where)

        @block.scalar
        def _(act):
            for t in range(TT):
                norm_act(nc, act, m, M, n0 + t + 1)
            for i in range(4):
                t, half = i // 2, i % 2
                where = turn["t", i]
                banks.wait_full(act, where)
                ins = nc.scalar.activation(x.yT[:, 4 * half:4 * half + 4, t * P:(t + 1) * P],
                                           m.ps[:, where[0], :].rearrange("p (k c) -> p k c", k=4), ACT.Copy)
                banks.free_chained(act, ins, where)
                act.sem_inc(M("yT_ready"), 1)
            for t in range(TT):
                act.wait_ge(M("top_ready"), t + 1)
                nc.scalar.activation(x.exp[:, 0:TOPK], x.exp[:, 0:TOPK], ACT.Exp).then_inc(M("top_exp"), 1)

        @block.vector
        def _(dve):
            step = Chain(M, dve, "dve_step")
            dve.wait_ge(M("rows_in"), m.rows_sent)
            for t in range(TT):
                X = m.X[:, t, :]
                norm_dve(nc, dve, step, m, M, X, n0 + t + 1)
                step(nc.vector.tensor_tensor(X, X, row(m, 0), ALU.mult))
                step(nc.vector.tensor_tensor(X, X, row(m, 1), ALU.add), "y_ready")
            iota = m.const("iota")[:, 0:NE]
            for t in range(TT):
                where = small["logit", t]
                banks.wait_full(dve, where)
                banks.free_chained(dve, nc.vector.tensor_copy(x.logits[:, t, :], m.ps[:, where[0], 0:NE]), where)
                top = x.top[:, t, :]
                step(nc.vector.max(top, x.logits[:, t, :]))
                step(nc.vector.max_index(x.top_at, top, x.logits[:, t, :]))
                step(nc.vector.tensor_copy(x.top_i[:, t, :], x.top_at))
                step(nc.vector.tensor_scalar(x.exp[:, 0:TOPK], top[:, 0:TOPK], top[:, 0:1], None, ALU.subtract), "top_ready")
                dve.wait_ge(M("top_exp"), t + 1)
                step(nc.vector.tensor_reduce(x.exp[:, 4:5], x.exp[:, 0:TOPK], axis=AX.X, op=ALU.add))
                step(nc.vector.reciprocal(x.exp[:, 5:6], x.exp[:, 4:5]))
                step(nc.vector.tensor_scalar(x.exp[:, 0:TOPK], x.exp[:, 0:TOPK], x.exp[:, 5:6], None, ALU.mult))
                for k in range(TOPK):
                    at, gate = x.top_i[:, t, k:k + 1], x.exp[:, k:k + 1]
                    if k == 0:
                        step(nc.vector.tensor_scalar(x.gates[:, t, :], iota, at, gate, ALU.is_equal, ALU.mult))
                        step(nc.vector.tensor_scalar(x.chosen[:, t, :], iota, at, None, ALU.is_equal))
                    else:
                        step(nc.vector.tensor_scalar(x.onehot, iota, at, gate, ALU.is_equal, ALU.mult))
                        step(nc.vector.tensor_tensor(x.gates[:, t, :], x.gates[:, t, :], x.onehot, ALU.add))
                        step(nc.vector.scalar_tensor_tensor(out=x.chosen[:, t, :], in0=iota, scalar=at, in1=x.chosen[:, t, :],
                                                            op0=ALU.is_equal, op1=ALU.add))
                dve.sem_inc(M("gates_known"), 1)
            step(nc.vector.memset(x.place, -1.0))
            for t in range(TT):
                where = small["place", t]
                banks.wait_full(dve, where)
                ins = nc.vector.tensor_tensor(x.place[:, t, 0:NE], m.ps[:, where[0], 0:NE], x.chosen[:, t, :], ALU.mult)
                banks.free_chained(dve, ins, where)
                step(nc.vector.tensor_scalar(x.place[:, t, 0:NE], x.place[:, t, 0:NE], -1.0, None, ALU.add))
            where = small["total"]
            banks.wait_full(dve, where)
            ins = nc.vector.tensor_reduce(x.total[0:1, NE:NE + 1], m.ps[0:1, where[0], 0:NE], axis=AX.X, op=ALU.max)
            banks.free_chained(dve, ins, where)
            step(nc.vector.tensor_copy(m.count[0:1, 0:1], x.total[0:1, NE:NE + 1]))
            where = small["gT"]
            banks.wait_full(dve, where)
            banks.free_chained(dve, nc.vector.tensor_copy(x.gatesT[0:NE, :], m.ps[0:NE, where[0], 0:T]), where)


def moe(nc, d, m, M, banks, ring):
    x = Experts(m)
    ch0 = ring.at["moe"]
    slot = [(ch0 + c) % NSLOT for c in range(PER_EXPERT)]
    nth = [(ch0 + c) // NSLOT for c in range(PER_EXPERT)]
    w = [m.ring[:, s, :].rearrange("p (k j) -> p k j", k=KT) for s in slot]
    n0 = m.norms
    m.norms += TT
    load_base = [f"chunk_in{s}" for s in slot]
    used_base = [f"chunk_used{s}" for s in slot]
    more = range(1, PASSES)

    def name(base, p):
        return base if p == 0 else base + "_more"

    def at(p, e, base=0):
        return e + base if p == 0 else (p - 1) * NE + e + base

    def primed(eng, p, *names):
        if p < 2:
            for n in names:
                eng.sem_inc(M(name(n, p)), 1)

    def picked(p, e, base=0):
        return e + base if p == 0 else (p - 1) * (NE + 1) + e + base

    def overflow(eng, body):
        count = eng.value_load(m.count[0:1, 0:1], min_val=0, max_val=T)
        with eng.If(count > SLOTS):
            for p in more:
                body(p)

    with nc.Block() as block:

        @block.sync
        def _(sp):
            with sp.Fori(1, NE) as e:
                for c in range(PER_EXPERT):
                    sp.wait_ge(M(used_base[c]), e + nth[c])
                    sp.dma_start(m.ring[:, slot[c], :], d["moe"][bass.ds(e, 1), c, :, :].rearrange("e p j -> (e p) j"))\
                        .then_inc(M(load_base[c]), 16)
            ring.sent = ch0 + PER_EXPERT * NE

            def body(p):
                if p == 1:
                    for c in range(PER_EXPERT):
                        sp.wait_ge(M(used_base[c]), NE + nth[c])
                with sp.Fori(0, NE) as e:
                    for c in range(PER_EXPERT):
                        sp.wait_ge(M(f"more_used{c}"), e + ((p - 1) * NE + 1))
                        sp.dma_start(m.ring[:, slot[c], :], d["moe"][bass.ds(e, 1), c, :, :].rearrange("e p j -> (e p) j"))\
                            .then_inc(M(f"more_in{c}"), 16)
                if p == PASSES - 1:
                    for c in range(PER_EXPERT):
                        sp.wait_ge(M(f"more_used{c}"), (PASSES - 1) * NE + 1)

            overflow(sp, body)
            ring.load(sp, ch0 + PER_EXPERT * NE + NSLOT)

        @block.tensor
        def _(pe):
            acc = [m.ps[:, 2 * t + n, :] for t in range(TT) for n in range(2)]
            for i in range(4):
                t, n = i // 2, i % 2
                nc.tensor.matmul(acc[i], x.gatesT[0:NE, t * P:(t + 1) * P], x.b_down[0:NE, n * 512:(n + 1) * 512],
                                 start=True, stop=False, skip_group_check=True)

            def gather(p, count):
                pe.wait_ge(M(name("pick_ready", p)), count)
                for k in range(KT):
                    for t in range(TT):
                        last = nc.tensor.matmul(m.ps[:, 4, k * SLOTS:(k + 1) * SLOTS], m.X[:, t, k * P:(k + 1) * P],
                                                x.pick[:, t, :], start=t == 0, stop=t == TT - 1)
                last.then_inc(M(name("gather_done", p)), 1)

            def one_pass(p):
                arrived = lambda c, e: pe.wait_ge(M(load_base[c] if p == 0 else f"more_in{c}"),
                                                  16 * (e + nth[c] + 1) if p == 0 else 16 * (at(p, e) + 1))
                used = lambda ins, c: ins.then_inc(M(used_base[c] if p == 0 else f"more_used{c}"), 1)
                primed(pe, p, "weigh_turned", "added")
                if p == 1:
                    for c in range(PER_EXPERT):
                        pe.sem_inc(M(f"more_used{c}"), 1)
                gather(p, picked(p, 0, 1))
                with pe.Fori(0, NE) as e:
                    pe.wait_ge(M(name("xe_ready", p)), picked(p, e, 1))
                    for c in range(4):
                        arrived(c, e)
                        bank, half = 5 + c // 2, c % 2
                        if half == 0:
                            pe.wait_ge(M(name(("gate_read", "up_read")[c // 2], p)), at(p, e, 1))
                        for j in range(4):
                            f = 4 * half + j
                            last = products(nc, m.ps[:, bank, f * SLOTS:(f + 1) * SLOTS],
                                            [(w[c][:, k, j * P:(j + 1) * P], x.xe[:, k, :]) for k in range(KT)])
                        used(last, c)
                    pe.wait_ge(M(name("weigh_ready", p)), at(p, e, 1))
                    pe.wait_ge(M(name("ye_ready", p)), 2 * at(p, e) + 1)
                    for t in range(TT):
                        last = nc.tensor.matmul(m.ps[0:SLOTS, 7, t * P:(t + 1) * P], x.weigh[:, t, :], m.const("ident"),
                                                start=True, stop=True)
                    last.then_inc(M(name("weigh_turned", p)), 1)
                    gather(p, picked(p, e, 2))
                    pe.wait_ge(M(name("h_ready", p)), at(p, e, 2))
                    for n in range(2):
                        arrived(4 + n, e)
                        if n == 0:
                            pe.wait_ge(M(name("weighT_ready", p)), at(p, e, 1))
                        else:
                            pe.wait_ge(M(name("xe_ready", p)), picked(p, e, 2))
                        last = products(nc, m.ps[0:SLOTS, (7, 4)[n], :], [(x.h[:, k, :], w[4 + n][:, k, :]) for k in range(KT)])
                        used(last, 4 + n)
                    for n in range(2):
                        pe.wait_ge(M(name("ye_ready", p)), 2 * at(p, e) + n + 2)
                        for t in range(TT):
                            last = nc.tensor.matmul(acc[2 * t + n], x.weighT[0:SLOTS, t * P:(t + 1) * P],
                                                    x.ye[0:SLOTS, n * 512:(n + 1) * 512], start=False, stop=False, skip_group_check=True)
                    last.then_inc(M(name("added", p)), 1)

            one_pass(0)
            overflow(pe, one_pass)
            for i in range(4):
                last = nc.tensor.matmul(acc[i], m.const("zero"), x.xe.rearrange("p a b -> p (a b)"), start=False, stop=True, skip_group_check=True)
            last.then_inc(M("sums_done"), 1)

        @block.scalar
        def _(act):
            def xe_out(p, count):
                act.wait_ge(M(name("gather_done", p)), count)
                nc.scalar.activation(x.xe.rearrange("p a b -> p (a b)"), m.ps[:, 4, :], ACT.Copy).then_inc(M(name("xe_ready", p)), 1)

            def one_pass(p):
                primed(act, p, "ye_ready")
                xe_out(p, picked(p, 0, 1))
                with act.Fori(0, NE) as e:
                    act.wait_ge(M(name("g_ready", p)), at(p, e, 1))
                    nc.scalar.activation(x.sig, x.g, ACT.Sigmoid, scale=SW_ALPHA).then_inc(M(name("sig_ready", p)), 1)
                    act.wait_ge(M(name("weigh_turned", p)), at(p, e, 2))
                    nc.scalar.activation(x.weighT[0:SLOTS, :], m.ps[0:SLOTS, 7, 0:T], ACT.Copy).then_inc(M(name("weighT_ready", p)), 1)
                    xe_out(p, picked(p, e, 2))
                    for n in range(2):
                        act.wait_ge(M(used_base[4 + n] if p == 0 else f"more_used{4 + n}"),
                                    e + nth[4 + n] + 1 if p == 0 else at(p, e, 2))
                        if n == 0:
                            act.wait_ge(M(name("added", p)), at(p, e, 1))
                        nc.scalar.activation(x.ye[0:SLOTS, n * 512:(n + 1) * 512], m.ps[0:SLOTS, (7, 4)[n], :], ACT.Copy)\
                            .then_inc(M(name("ye_ready", p)), 1)

            one_pass(0)
            overflow(act, one_pass)
            for t in range(TT):
                norm_act(nc, act, m, M, n0 + t + 1)

        @block.vector
        def _(dve):
            step = Chain(M, dve, "dve_step")
            iota = m.const("iota")

            def pick(p, e):
                for t in range(TT):
                    last = nc.vector.tensor_scalar(x.pick[:, t, :], iota, x.place[:, t, bass.ds(e, 1)], None, ALU.is_equal)
                last.then_inc(M(name("pick_ready", p)), 1)

            def weigh(p, e):
                for t in range(TT):
                    last = nc.vector.tensor_scalar(x.weigh[:, t, :], iota, x.place[:, t, bass.ds(e, 1)], x.gates[:, t, bass.ds(e, 1)],
                                                   ALU.is_equal, ALU.mult)
                last.then_inc(M(name("weigh_ready", p)), 1)

            def one_pass(p):
                if p:
                    before = p - 1
                    dve.wait_ge(M(name("weigh_ready", before)), at(before, NE))
                    dve.wait_ge(M(name("weigh_turned", before)), at(before, NE, 1))
                    dve.wait_ge(M(name("pick_ready", before)), picked(before, NE, 1))
                    dve.wait_ge(M(name("gather_done", before)), picked(before, NE, 1))
                    nc.vector.tensor_scalar(x.place, x.place, -float(SLOTS), None, ALU.add).then_inc(M("shifted_more"), 1)
                    dve.wait_ge(M("shifted_more"), p)
                primed(dve, p, "gate_read", "up_read", "h_ready")
                pick(p, 0)
                with dve.Fori(0, NE) as e:
                    dve.wait_ge(M(name("weigh_turned", p)), at(p, e, 1))
                    weigh(p, e)
                    dve.wait_ge(M(name("gather_done", p)), picked(p, e, 1))
                    pick(p, e + 1)
                    dve.wait_ge(M(used_base[1] if p == 0 else "more_used1"), e + nth[1] + 1 if p == 0 else at(p, e, 2))
                    bias = lambda b: b[:, bass.ds(e * KT, KT), :].to_broadcast([P, KT, SLOTS])
                    shaped = lambda bank: m.ps[:, bank, :].rearrange("p (k s) -> p k s", k=KT)
                    nc.vector.tensor_tensor(x.g, shaped(5), bias(x.b_gate), ALU.add).then_inc(M(name("gate_read", p)), 1)
                    dve.wait_ge(M(name("gate_read", p)), at(p, e, 2))
                    nc.vector.tensor_scalar(x.g, x.g, LIMIT, None, ALU.min).then_inc(M(name("g_ready", p)), 1)
                    dve.wait_ge(M(used_base[3] if p == 0 else "more_used3"), e + nth[3] + 1 if p == 0 else at(p, e, 2))
                    dve.wait_ge(M(name("h_ready", p)), at(p, e, 1))
                    nc.vector.tensor_tensor(x.u, shaped(6), bias(x.b_up), ALU.add).then_inc(M(name("up_read", p)), 1)
                    dve.wait_ge(M(name("up_read", p)), at(p, e, 2))
                    nc.vector.tensor_scalar(x.u, x.u, LIMIT, -LIMIT, ALU.min, ALU.max).then_inc(M(name("u_ready", p)), 1)
                    dve.wait_ge(M(name("u_ready", p)), at(p, e, 1))
                    dve.wait_ge(M(name("g_ready", p)), at(p, e, 1))
                    nc.vector.scalar_tensor_tensor(out=x.u, in0=x.u, scalar=1.0, in1=x.g, op0=ALU.add, op1=ALU.mult)\
                        .then_inc(M(name("ug_ready", p)), 1)
                    dve.wait_ge(M(name("ug_ready", p)), at(p, e, 1))
                    dve.wait_ge(M(name("sig_ready", p)), at(p, e, 1))
                    nc.vector.tensor_tensor(x.h, x.u, x.sig, ALU.mult).then_inc(M(name("h_ready", p)), 1)

            one_pass(0)
            overflow(dve, one_pass)
            dve.wait_ge(M("sums_done"), 1)
            for t in range(TT):
                X = m.X[:, t, :]
                step(nc.vector.scalar_tensor_tensor(out=X, in0=X, scalar=ALPHA1,
                                                    in1=m.ps[:, 2 * t:2 * t + 2, :].rearrange("p a b -> p (a b)"), op0=ALU.mult, op1=ALU.add))
                norm_dve(nc, dve, step, m, M, X, n0 + t + 1)
                step(nc.vector.tensor_tensor(X, X, row(m, 2), ALU.mult))
                step(nc.vector.tensor_tensor(X, X, row(m, 3), ALU.add))



SHIFT1, SCALE1, GATE1, SHIFT2, SCALE2, GATE2 = range(6)


def modulations(nc, d, m, M, banks, ring):
    bias = m.part(0, 2, 6 * D)
    c = m.H[:, 0, 0:KT * 2].rearrange("p (k s) -> p k s", k=KT)
    sc = m.H[:, 0, 16:16 + KT * 2].rearrange("p (k s) -> p k s", k=KT)
    stage = m.H[0:2, 1:4, :].rearrange("p a (b c) -> p (a b) c", b=2)
    n_stage = 6
    groups = [(layer, n) for layer in range(2) for n in range(12)]
    plan = banks.plan(groups, [0, 1, 2, 3])
    with nc.Block() as block:

        @block.sync
        def _(sp):
            sp.dma_start(c, d["c"]).then_inc(M("c_in"), 16)
            sp.dma_start(bias[0:1, :, :], d["b_mod"].rearrange("(o l) n -> o l n", o=1)).then_inc(M("c_in"), 16)
            sp.dma_start(m.X[:, 2:4, :], d["ctx"].rearrange("(t p) c -> p t c", p=P)).then_inc(M("ctx_in"), 16)
            for layer in range(2):
                for n in range(12):
                    i = 12 * layer + n
                    ring.load(sp, ring.at["w_mod0"] + i + NSLOT)
                    sp.wait_ge(M("mod_staged"), i + 1)
                    sp.dma_start(d["mod"][layer, :, n * 512:(n + 1) * 512], stage[:, i % n_stage, :]).then_inc(M(f"mod_out{i % n_stage}"), 16)
            for i in range(n_stage):
                sp.wait_ge(M(f"mod_out{i}"), 16 * (len(groups) // n_stage))
            sp.wait_ge(M("ctx_in"), 16)

        @block.tensor
        def _(pe):
            pe.wait_ge(M("c_in"), 32)
            pe.wait_ge(M("silu_c"), 1)
            for layer, n in groups:
                w = ring.wait(pe, "w_mod0", 12 * layer + n)
                where = plan[layer, n]
                banks.wait_free(pe, where)
                pairs = [(m.const("ones")[0:1, 0:2], bias[0:1, layer, n * 512:(n + 1) * 512])]
                pairs += [(sc[:, k, :], w[:, k, :]) for k in range(KT)]
                banks.fill(products(nc, m.ps[0:2, where[0], :], pairs), where)
                pe.wait_ge(M(f"bank_full{where[0]}"), where[1] + 1)
                pe.sem_inc(M(f"chunk_used{(ring.at['w_mod0'] + 12 * layer + n) % NSLOT}"), 1)

        @block.vector
        def _(dve):
            nc.vector.memset(m.idx[:, :], 0).then_inc(M("idx_clear"), 1)
            dve.wait_ge(M("idx_clear"), 1)

        @block.scalar
        def _(act):
            act.wait_ge(M("c_in"), 32)
            nc.scalar.activation(sc, c, ACT.Silu).then_inc(M("silu_c"), 1)
            for i, (layer, n) in enumerate(groups):
                where = plan[layer, n]
                banks.wait_full(act, where)
                if i >= n_stage:
                    act.wait_ge(M(f"mod_out{i % n_stage}"), 16 * (i // n_stage))
                ins = nc.scalar.activation(stage[:, i % n_stage, :], m.ps[0:2, where[0], :], ACT.Copy,
                                           bias=1.0 if n // 2 in (SCALE1, SCALE2) else 0.0)
                banks.free_chained(act, ins, where)
                act.sem_inc(M("mod_staged"), 1)


def mod_row(d, layer, stream, which):
    return d["mod"][layer, stream:stream + 1, which * D:(which + 1) * D]


def modulate(nc, d, m, M, banks, ring, layer, scale, shift, tiles):
    hT = m.part(0, KT, tiles * P)
    plan = banks.plan([(t, n) for t in range(tiles) for n in range(2)], list(range(8)))
    base = M.n.get("h_ready_now", 0)
    with nc.Block() as block:

        @block.sync
        def _(sp):
            load_rows(sp, M, m, [mod_row(d, layer, s, w) for s in range(tiles // 2) for w in (scale, shift)])

        @block.vector
        def _(dve):
            step = Chain(M, dve, "dve_step")
            dve.wait_ge(M("rows_in"), m.rows_sent)
            for t in range(tiles):
                step(nc.vector.tensor_tensor(m.H[:, t, :], m.X[:, t, :], row(m, 2 * (t // 2)), ALU.mult))
                step(nc.vector.tensor_tensor(m.H[:, t, :], m.H[:, t, :], row(m, 2 * (t // 2) + 1), ALU.add), "h_ready_now")

        @block.tensor
        def _(pe):
            for t in range(tiles):
                pe.wait_ge(M("h_ready_now"), base + t + 1)
                for n in range(2):
                    where = plan[t, n]
                    banks.wait_free(pe, where)
                    for k in range(4):
                        last = nc.tensor.transpose(m.ps[:, where[0], k * P:(k + 1) * P],
                                                   m.H[:, t, (4 * n + k) * P:(4 * n + k + 1) * P], m.const("ident"))
                    banks.fill(last, where)

        @block.scalar
        def _(act):
            for t in range(tiles):
                for n in range(2):
                    where = plan[t, n]
                    banks.wait_full(act, where)
                    ins = nc.scalar.activation(hT[:, 4 * n:4 * n + 4, t * P:(t + 1) * P],
                                               m.ps[:, where[0], :].rearrange("p (k c) -> p k c", k=4), ACT.Copy)
                    banks.free(ins, where)


def residual(nc, d, m, M, banks, sums, layer, gate, which, tiles, out=None):
    n0 = m.norms
    m.norms += tiles
    tmp = m.part(4096, D)
    base = M.n.get("x_done", 0)
    with nc.Block() as block:

        @block.sync
        def _(sp):
            load_rows(sp, M, m, [mod_row(d, layer, 0, gate), mod_row(d, layer, tiles // 2 - 1, gate),
                                 d["ln_g"][2 * layer + which:2 * layer + which + 1, :], d["ln_b"][2 * layer + which:2 * layer + which + 1, :]])
            if out is not None:
                view = out.rearrange("a (t p) c -> p (a t) c", p=P)
                for t in range(tiles):
                    sp.wait_ge(M("x_done"), base + t + 1)
                    sp.dma_start(view[:, t, :], m.X[:, t, :]).then_inc(M("stored"), 16)
                sp.wait_ge(M("stored"), 16 * tiles)

        @block.scalar
        def _(act):
            for t in range(tiles):
                norm_act(nc, act, m, M, n0 + t + 1)

        @block.vector
        def _(dve):
            step = Chain(M, dve, "dve_step")
            dve.wait_ge(M("rows_in"), m.rows_sent)
            for t in range(tiles):
                X = m.X[:, t, :]
                for n in range(2):
                    where = sums[t, n]
                    banks.wait_full(dve, where)
                    half = slice(n * 512, (n + 1) * 512)
                    ins = nc.vector.tensor_tensor(tmp[:, half], m.ps[:, where[0], :], row(m, t // 2)[:, half], ALU.mult)
                    banks.free_chained(dve, ins, where)
                step(nc.vector.scalar_tensor_tensor(out=X, in0=X, scalar=ALPHA2, in1=tmp, op0=ALU.mult, op1=ALU.add))
                norm_dve(nc, dve, step, m, M, X, n0 + t + 1)
                step(nc.vector.tensor_tensor(X, X, row(m, 2), ALU.mult))
                step(nc.vector.tensor_tensor(X, X, row(m, 3), ALU.add), "x_done")



def chunk_mlp(nc, d, m, M, banks, ring):
    tiles = 4
    hT = m.part(0, KT, tiles * P)
    u = m.part(4096, tiles, D)
    v = m.part(8192, tiles, D)
    w_s = m.H[:, 0, :].rearrange("p (h c) -> p h c", h=8)
    b_s = m.H[:, 1, 0:8]
    tmp = m.H[:, 2, :]
    n0 = m.norms
    m.norms += tiles
    z = banks.plan([(n, t) for n in range(4) for t in range(tiles)], list(range(8)))
    mixed = banks.plan([(t, n) for t in range(tiles) for n in range(2)], list(range(8)))
    turned = banks.plan([(t, n) for t in range(tiles) for n in range(2)], list(range(8)))
    sums = banks.plan([(t, n) for t in range(tiles) for n in range(2)], list(range(8)))
    with nc.Block() as block:

        @block.sync
        def _(sp):
            sp.dma_start(w_s, d["a_w_s"]).then_inc(M("mlp_in"), 16)
            sp.dma_start(b_s, d["a_b_s"]).then_inc(M("mlp_in"), 16)
            load_rows(sp, M, m, [d["a_norm"][i:i + 1, :] for i in range(2)])
            ring.load(sp, ring.at["a_w_out"] + 2 + NSLOT)

        @block.tensor
        def _(pe):
            for n in range(4):
                w = ring.wait(pe, "a_w_in", n)
                for t in range(tiles):
                    where = z[n, t]
                    banks.wait_free(pe, where)
                    last = products(nc, m.ps[:, where[0], :], [(hT[:, k, t * P:(t + 1) * P], w[:, k, :]) for k in range(KT)])
                    banks.fill(last, where)
                pe.wait_ge(M(f"bank_full{where[0]}"), where[1] + 1)
                pe.sem_inc(M(f"chunk_used{(ring.at['a_w_in'] + n) % NSLOT}"), 1)
            pe.wait_ge(M("mlp_in"), 32)
            for t in range(tiles):
                pe.wait_ge(M("v_normed"), t + 1)
                for n in range(2):
                    where = mixed[t, n]
                    banks.wait_free(pe, where)
                    for k in range(4):
                        head = 4 * n + k
                        last = nc.tensor.matmul(m.ps[:, where[0], k * P:(k + 1) * P], w_s[:, head, :],
                                                v[:, t, head * P:(head + 1) * P], start=True, stop=True)
                    banks.fill(last, where)
            for t in range(tiles):
                pe.wait_ge(M("gated_ready"), t + 1)
                for n in range(2):
                    where = turned[t, n]
                    banks.wait_free(pe, where)
                    for k in range(4):
                        c = (4 * n + k) * P
                        last = nc.tensor.transpose(m.ps[:, where[0], k * P:(k + 1) * P], u[:, t, c:c + P], m.const("ident"))
                    banks.fill(last, where)
            pe.wait_ge(M("gatedT_ready"), 2 * tiles)
            for n in range(2):
                w = ring.wait(pe, "a_w_out", n)
                for t in range(tiles):
                    where = sums[t, n]
                    banks.wait_free(pe, where)
                    last = products(nc, m.ps[:, where[0], :], [(hT[:, k, t * P:(t + 1) * P], w[:, k, :]) for k in range(KT)])
                    banks.fill(last, where)
                pe.wait_ge(M(f"bank_full{where[0]}"), where[1] + 1)
                pe.sem_inc(M(f"chunk_used{(ring.at['a_w_out'] + n) % NSLOT}"), 1)

        @block.scalar
        def _(act):
            def gelu(n, t):
                where = z[n, t]
                banks.wait_full(act, where)
                dst = (v if n < 2 else u)[:, t, (n % 2) * 512:(n % 2) * 512 + 512]
                banks.free_chained(act, nc.scalar.activation(dst, m.ps[:, where[0], :], ACT.Gelu_apprx_tanh), where)
                act.sem_inc(M("z_ready"), 1)

            for n in range(2):
                for t in range(tiles):
                    gelu(n, t)
            for t in range(tiles):
                norm_act(nc, act, m, M, n0 + t + 1)
            for n in range(2, 4):
                for t in range(tiles):
                    gelu(n, t)
            for t in range(tiles):
                for n in range(2):
                    where = turned[t, n]
                    banks.wait_full(act, where)
                    ins = nc.scalar.activation(hT[:, 4 * n:4 * n + 4, t * P:(t + 1) * P],
                                               m.ps[:, where[0], :].rearrange("p (k c) -> p k c", k=4), ACT.Copy)
                    banks.free_chained(act, ins, where)
                    act.sem_inc(M("gatedT_ready"), 1)

        @block.vector
        def _(dve):
            step = Chain(M, dve, "dve_step")
            dve.wait_ge(M("rows_in"), m.rows_sent)
            dve.wait_ge(M("mlp_in"), 32)
            for t in range(tiles):
                dve.wait_ge(M("z_ready"), tiles + t + 1)
                V = v[:, t, :]
                norm_dve(nc, dve, step, m, M, V, n0 + t + 1)
                step(nc.vector.tensor_tensor(V, V, row(m, 0), ALU.mult))
                step(nc.vector.tensor_tensor(V, V, row(m, 1), ALU.add), "v_normed")
            for t in range(tiles):
                dve.wait_ge(M("z_ready"), 3 * tiles + t + 1)
                for n in range(2):
                    where = mixed[t, n]
                    banks.wait_full(dve, where)
                    half = slice(n * 512, (n + 1) * 512)
                    bias = b_s[:, 4 * n:4 * n + 4].rearrange("p (h c) -> p h c", c=1).to_broadcast([P, 4, P])
                    ins = nc.vector.tensor_tensor(tmp[:, half].rearrange("p (h c) -> p h c", h=4),
                                                  m.ps[:, where[0], :].rearrange("p (h c) -> p h c", h=4), bias, ALU.add)
                    banks.free_chained(dve, ins, where)
                step(nc.vector.tensor_tensor(u[:, t, :], u[:, t, :], tmp, ALU.mult), "gated_ready")
    return sums



def select(nc, d, m, M, banks, ring, layer, tiles):
    tok = tiles * P
    hT = m.part(0, KT, tok)
    qT = m.part(4096, PH, tok)
    s = m.part(8192, 16, NKEY)
    rest = m.part(10240, 16, NKEY)
    keys = m.part(12288, NKEY)
    best = m.part(12416, 2, PH, PK)
    best_at = m.arena[:, 12672:12928].bitcast(U32).rearrange("p (r k) -> p r k", r=16)
    best_i = m.part(12928, 2, PH, PK)
    sums = m.part(0, PH, PK, PK)
    sums_rest = m.part(2048, PH, PK * PK)
    top = m.part(13184, PH, PK)
    top_at = m.arena[:, 13312:13440].bitcast(U32).rearrange("p (h k) -> p h k", h=PH)
    part_at = m.arena[:, 13440:13568].bitcast(U32)
    parts = m.part(13568, 2, P)
    found = m.part(13824, 2, P)
    hit = m.part(10240, P, PK)
    z = m.part(14080, 2 * PH)
    q = banks.plan([("q", h) for h in range(PH)], [0, 1, 2, 3])
    sc = banks.plan([(t, p, i) for t in range(tiles) for p in range(2) for i in range(2)], [4, 5, 6, 7])
    L = f"_{layer}"
    with nc.Block() as block:

        @block.sync
        def _(sp):
            sp.dma_start(keys, d["keys"][layer]).then_inc(M("keys_in"), 16)
            ring.load(sp, ring.at[f"w_q{layer}"] + 2 + NSLOT)

        @block.tensor
        def _(pe):
            for h in range(PH):
                if h % 4 == 0:
                    w = ring.wait(pe, f"w_q{layer}", h // 4)
                where = q["q", h]
                banks.wait_free(pe, where)
                j = h % 4
                last = products(nc, m.ps[:, where[0], 0:tok], [(w[:, k, j * P:(j + 1) * P], hT[:, k, :]) for k in range(KT)])
                banks.fill(last, where)
                if j == 3:
                    pe.wait_ge(M(f"bank_full{where[0]}"), where[1] + 1)
                    pe.sem_inc(M(f"chunk_used{(ring.at[f'w_q{layer}'] + h // 4) % NSLOT}"), 1)
            pe.wait_ge(M("qT_ready" + L), PH)
            pe.wait_ge(M("keys_in"), 16 * (layer + 1))
            for t in range(tiles):
                for p in range(2):
                    for i in range(2):
                        where = sc[t, p, i]
                        banks.wait_free(pe, where)
                        rows_ = slice(p * HD, (p + 1) * HD)
                        for k in range(4):
                            last = nc.tensor.matmul(m.ps[:, where[0], k * P:(k + 1) * P], qT[rows_, 4 * i + k, t * P:(t + 1) * P],
                                                    keys[rows_, :], start=True, stop=True)
                        banks.fill(last, where)

        @block.scalar
        def _(act):
            for h in range(PH):
                where = q["q", h]
                banks.wait_full(act, where)
                banks.free_chained(act, nc.scalar.activation(qT[:, h, :], m.ps[:, where[0], 0:tok], ACT.Copy), where)
                act.sem_inc(M("qT_ready" + L), 1)
            for t in range(tiles):
                if t:
                    act.wait_ge(M("scores_sorted" + L), t)
                for p in range(2):
                    for i in range(2):
                        where = sc[t, p, i]
                        banks.wait_full(act, where)
                        r = 8 * p + 4 * i
                        ins = nc.scalar.activation(s[:, r:r + 4, :].rearrange("p a b -> p (a b)"), m.ps[:, where[0], :], ACT.Copy)
                        banks.free_chained(act, ins, where)
                        act.sem_inc(M("scores_out" + L), 1)
                act.wait_ge(M("peer_top" + L), t + 1)
                nc.scalar.activation(top, top, ACT.Exp).then_inc(M("peer_exp" + L), 1)

        @block.vector
        def _(dve):
            step = Chain(M, dve, "dve_step")

            def each(make, rows_):
                for r in range(rows_):
                    value = M.up(make(r), "dve_step")
                dve.wait_ge(M("dve_step"), value)

            def top16(src, spare, values, places, rows_):
                each(lambda r: nc.vector.max(values[:, r, 0:8], src[:, r, :]), rows_)
                each(lambda r: nc.vector.max_index(places[:, r, 0:8], values[:, r, 0:8], src[:, r, :]), rows_)
                each(lambda r: nc.vector.match_replace(out=spare[:, r, :], in_to_replace=values[:, r, 0:8], in_values=src[:, r, :],
                                                       imm_value=LOWEST), rows_)
                each(lambda r: nc.vector.max(values[:, r, 8:16], spare[:, r, :]), rows_)
                each(lambda r: nc.vector.max_index(places[:, r, 8:16], values[:, r, 8:16], spare[:, r, :]), rows_)

            iota = m.const("iota")[:, 0:PK].rearrange("p (o j) -> p o j", o=1)
            best16 = best.rearrange("p a h k -> p (a h) k")
            for t in range(tiles):
                dve.wait_ge(M("scores_out" + L), 4 * (t + 1))
                top16(s, rest, best16, best_at, 16)
                dve.sem_inc(M("scores_sorted" + L), 1)
                step(nc.vector.tensor_copy(best_i.rearrange("p a h k -> p (a h) k"), best_at))
                first = best[:, 0, :, :].rearrange("p h (k o) -> p h k o", o=1).to_broadcast([P, PH, PK, PK])
                second = best[:, 1, :, :].rearrange("p h (o k) -> p h o k", o=1).to_broadcast([P, PH, PK, PK])
                step(nc.vector.tensor_tensor(sums, first, second, ALU.add))
                top16(sums.rearrange("p h a b -> p h (a b)"), sums_rest, top, top_at, PH)
                flat = top_at.rearrange("p h k -> p (h k)")
                for n, (op, by) in enumerate(((ALU.logical_shift_right, 4), (ALU.bitwise_and, 15))):
                    step(nc.vector.tensor_scalar(part_at, flat, by, None, op))
                    step(nc.vector.tensor_copy(parts[:, n, :], part_at))
                for n in range(2):
                    at = parts[:, n, :].rearrange("p (r o) -> p r o", o=1).to_broadcast([P, P, PK])
                    step(nc.vector.tensor_tensor(hit, at, iota.to_broadcast([P, P, PK]), ALU.is_equal))
                    keys_i = best_i[:, n, :, :].rearrange("p h (o k) -> p h o k", o=1).to_broadcast([P, PH, PK, PK])
                    hit4 = hit.rearrange("p (h k) j -> p h k j", h=PH)
                    step(nc.vector.tensor_tensor(hit4, hit4, keys_i, ALU.mult))
                    step(nc.vector.tensor_reduce(found[:, n, :], hit, axis=AX.X, op=ALU.add))
                step(nc.vector.scalar_tensor_tensor(out=m.idx[:, t * P:(t + 1) * P], in0=found[:, 0, :], scalar=float(NKEY),
                                                    in1=found[:, 1, :], op0=ALU.mult, op1=ALU.add))
                step(nc.vector.tensor_copy(z[:, 0:PH], top[:, :, 0]))
                z3 = z.rearrange("p (a h o) -> p a h o", a=2, o=1)
                step(nc.vector.tensor_tensor(top, top, z3[:, 0, :, :].to_broadcast([P, PH, PK]), ALU.subtract), "peer_top" + L)
                dve.wait_ge(M("peer_exp" + L), t + 1)
                step(nc.vector.tensor_reduce(z[:, 0:PH], top, axis=AX.X, op=ALU.add))
                step(nc.vector.reciprocal(z[:, PH:2 * PH], z[:, 0:PH]))
                step(nc.vector.tensor_tensor(m.wts[:, t * P:(t + 1) * P].rearrange("p (h k) -> p h k", h=PH), top,
                                             z3[:, 1, :, :].to_broadcast([P, PH, PK]), ALU.mult))


BUFS, LOT = 8, 4


def peer(nc, d, m, M, banks, layer, tiles, first):
    u_buf = [m.part(b * D, D) for b in range(BUFS)]
    v_buf = [m.part((BUFS + b) * D, D) for b in range(BUFS)]
    cur = [m.cur_idx[:, 0:PK], m.cur_idx[:, PK:2 * PK]]
    sums = banks.plan([(t, n) for t in range(tiles) for n in range(2)], list(range(2 * tiles)))
    pairs = PH // 2
    slots = PH * PK

    with nc.Block() as block:

        @block.gpsimd
        def _(pool):
            for t in range(tiles):
                with pool.Fori(0, pairs) as i:
                    for hh in range(2):
                        done = i * 2 * PK + ((first + t) * slots + hh * PK)
                        pool.wait_ge(M("idx_ready"), i * 2 + ((first + t) * PH + layer + hh + 1))
                        for lot in range(PK // LOT):
                            for table, bufs, free, arrived in ((d[f"u{layer}"], u_buf, "u_free", "u_in"),
                                                               (d[f"v{layer}"], v_buf, "v_free", "v_in")):
                                for j in range(LOT):
                                    k = lot * LOT + j
                                    b = k % BUFS
                                    pool.wait_ge(M(free), done + k + 1)
                                    pool.sem_inc(M("gather_ticket"), 1)
                                    pool.indirect_dma_start(bufs[b], None, table, bass.IndirectOffsetOnAxis(cur[hh][:, k:k + 1], 0))\
                                        .then_inc(M(f"{arrived}{b}"), 16)

        @block.vector
        def _(dve):
            def arrivals(t, i, hh, k):
                return 16 * (((first + t) * slots + hh * PK + k) // BUFS + 1) + i * (16 * 2 * PK // BUFS)

            if first == 0:
                dve.sem_inc(M("u_free"), BUFS)
            for t in range(tiles):
                if t == 0:
                    nc.vector.tensor_copy(cur[0], m.idx[:, t * P:t * P + PK]).then_inc(M("idx_ready"), 1)
                with dve.Fori(0, pairs) as i:
                    for hh in range(2):
                        for k in range(PK):
                            b = k % BUFS
                            dve.wait_ge(M(f"u_in{b}"), arrivals(t, i, hh, k))
                            nc.vector.scalar_tensor_tensor(out=u_buf[b], in0=u_buf[b], scalar=1.0, in1=m.H[:, t, :], op0=ALU.mult,
                                                           op1=ALU.mult, accum_out=m.dots[:, k:k + 1]).then_inc(M("u_free"), 1)
                            if k % LOT == LOT - 1:
                                lots = ((first + t) * slots + hh * PK + k) // LOT + i * (2 * PK // LOT)
                                dve.wait_ge(M("gelu_done"), lots + 1)
                                a = m.act[:, k + 1 - LOT:k + 1]
                                nc.vector.tensor_tensor(a, a, m.wts[:, bass.ds(i * 2 * PK + (t * P + hh * PK + k + 1 - LOT), LOT)], ALU.mult)\
                                    .then_inc(M("act_ready"), 1)
                            if k == LOT - 1:
                                dve.wait_ge(M("v_free"), i * 2 * PK + ((first + t) * slots + hh * PK + BUFS))
                                nc.vector.tensor_copy(cur[1 - hh], m.idx[:, bass.ds(i * 2 * PK + (t * P + (hh + 1) * PK), PK)])\
                                    .then_inc(M("idx_ready"), 1)

        @block.scalar
        def _(act):
            for t in range(tiles):
                with act.Fori(0, pairs) as i:
                    for hh in range(2):
                        for k in range(PK):
                            n = (first + t) * slots + hh * PK + k
                            if k % LOT == 0:
                                act.wait_ge(M("u_free"), i * 2 * PK + (n + LOT + BUFS))
                                a = slice(k, k + LOT)
                                nc.scalar.activation(m.act[:, a], m.dots[:, a], ACT.Gelu_apprx_tanh).then_inc(M("gelu_done"), 1)
                                act.wait_ge(M("act_ready"), i * (2 * PK // LOT) + (n // LOT + 1))
                            act.wait_ge(M("v_free"), i * 2 * PK + (n - 3 + BUFS))
                            nc.scalar.activation(m.diag[k % 4], m.const("ident"), ACT.Copy, scale=m.act[:, k:k + 1]).then_inc(M("diag_ready"), 1)

        @block.tensor
        def _(pe):
            if first == 0:
                pe.sem_inc(M("v_free"), BUFS)
            for t in range(tiles):
                out = [m.ps[:, sums[t, n][0], :] for n in range(2)]
                for n in range(2):
                    banks.wait_free(pe, sums[t, n])
                    nc.tensor.matmul(out[n], m.const("zero"), m.H[:, t, 0:512], start=True, stop=False, skip_group_check=True)
                with pe.Fori(0, pairs) as i:
                    for hh in range(2):
                        for k in range(PK):
                            n_ = (first + t) * slots + hh * PK + k
                            b = k % BUFS
                            pe.wait_ge(M("diag_ready"), i * 2 * PK + (n_ + 1))
                            pe.wait_ge(M(f"v_in{b}"), i * (16 * 2 * PK // BUFS) + 16 * (n_ // BUFS + 1))
                            for n in range(2):
                                last = nc.tensor.matmul(out[n], m.diag[k % 4], v_buf[b][:, n * 512:(n + 1) * 512],
                                                        start=False, stop=False, skip_group_check=True)
                            last.then_inc(M("v_free"), 1)
                for n in range(2):
                    last = nc.tensor.matmul(out[n], m.const("zero"), m.H[:, t, 0:512], start=False, stop=True, skip_group_check=True)
                    banks.fill(last, sums[t, n])
    return sums



def gla(nc, d, m, M, banks, ring):
    tiles = 4
    hT = m.part(0, KT, tiles * P)
    k_end = m.part(0, tiles, 2, GH * DK)
    v = m.part(4096, tiles, D)
    g = m.part(8192, tiles, 2, GH * DK)
    k = m.part(12288, tiles, GH * DK)
    o = m.part(12288, TT, D)
    r = m.part(14336, TT, D)
    yT = m.part(0, KT, T)
    H = m.H[:, :, :].rearrange("p a b -> p (a b)")
    qT = H[:, 0:1024].rearrange("p (h t) -> p h t", h=GH)
    kT = H[:, 1024:2048].rearrange("p (h t) -> p h t", h=GH)
    glT = H[:, 2048:3072].rearrange("p (j t) -> p j t", j=2)
    gn = H[:, 3072:4096]
    X2 = m.X[:, 2:4, :].rearrange("p a b -> p (a b)")
    w_gl = X2[:, 0:256].rearrange("p (k j) -> p k j", k=KT)
    w_gate = X2[:, 256:1280].rearrange("p (j n) -> p j n", j=2)
    E = m.ring[:, 4:6, :].rearrange("p a b -> p (a b)")
    q_in = E[:, 0:2048].rearrange("p (j h t) -> p j h t", j=2, h=GH)
    k_in = E[:, 2048:4096].rearrange("p (j h t) -> p j h t", j=2, h=GH)
    S = E[:, 4096:5120].rearrange("p (j b e) -> p j b e", j=2, b=2)
    att = E[:, 5120:6144].rearrange("p (b c) -> p b c", b=2)
    decay = E[:, 6144:6208]
    ab = E[:, 6208:7232].rearrange("p (b c) -> p b c", b=2)
    low = X2[:, 1280:1792]
    assert [(ring.at["b_w_in"] + n) % NSLOT for n in (4, 5)] == [4, 5]

    n0 = m.norms
    m.norms += TT * GH
    jobs = [("k", 0, t) for t in range(tiles)] + [("kT", 0, i) for i in range(2)]
    jobs += [("v", 1 + n, t) for n in range(2) for t in range(tiles)] + [("qT", 3, i) for i in range(2)]
    jobs += [("r", 4 + n, t) for n in range(2) for t in range(TT)]
    proj = banks.plan([("gl", j) for j in range(2)] + jobs, [0, 1, 2, 3])
    zs = banks.plan([("z", t, j) for t in range(tiles) for j in range(2)], [4, 5])
    cums = banks.plan([("b", j, i) for j in range(2) for i in range(2)], [6, 7])
    sufs = banks.plan([("e", t, j) for t in range(tiles) for j in range(2)] + ["decay"], [6, 7])
    atts = banks.plan([("att", h) for h in range(GH)], [2, 3])
    outs = banks.plan([("o", h) for h in range(GH)], [0, 1])
    steps = [[(2 + c // 2, c % 2) for c in order] + [(c // 2, c % 2) for c in order]
             for order in (range(4), range(3, -1, -1))]
    kv = {}
    for h in range(GH):
        for s in range(7):
            for j in range(2):
                kv[h, s, j] = banks.plan(["x"], [4 + 2 * j + steps[j][s][1]])["x"]
    turned = banks.plan([(t, n) for t in range(TT) for n in range(2)], [4, 5, 6, 7])
    sums = banks.plan([(t, n) for t in range(TT) for n in range(2)], [0, 1, 2, 3])

    with nc.Block() as block:

        @block.sync
        def _(sp):
            sp.dma_start(w_gl, d["b_w_gl"]).then_inc(M("gla_in"), 16)
            sp.dma_start(w_gate[0:RANK + 1, :, :], d["b_w_gate"]).then_inc(M("gla_in"), 16)
            sp.dma_start(gn, d["b_gn_g"].to_broadcast([P, D])).then_inc(M("gla_in"), 16)
            ring.load(sp, ring.at["b_w_out"] + 2 + NSLOT)

        @block.tensor
        def _(pe):
            pe.wait_ge(M("gla_in"), 48)
            for j in range(2):
                where = proj["gl", j]
                banks.wait_free(pe, where)
                banks.fill(products(nc, m.ps[0:RANK, where[0], :], [(w_gl[:, c, j * RANK:(j + 1) * RANK], hT[:, c, :]) for c in range(KT)]), where)
            for n, job in enumerate(jobs):
                kind, chunk, i = job
                w = ring.wait(pe, "b_w_in", chunk)
                where = proj[job]
                banks.wait_free(pe, where)
                if kind in ("kT", "qT"):
                    for half in range(2):
                        col = (2 * i + half) * P
                        last = products(nc, m.ps[:, where[0], half * T:(half + 1) * T],
                                        [(w[:, c, col:col + P], hT[:, c, 0:T]) for c in range(KT)])
                else:
                    last = products(nc, m.ps[:, where[0], :], [(hT[:, c, i * P:(i + 1) * P], w[:, c, :]) for c in range(KT)])
                banks.fill(last, where)
                if n + 1 == len(jobs) or jobs[n + 1][1] != chunk:
                    pe.wait_ge(M(f"bank_full{where[0]}"), where[1] + 1)
                    pe.sem_inc(M(f"chunk_used{(ring.at['b_w_in'] + chunk) % NSLOT}"), 1)
                    if n + 1 == len(jobs):
                        pe.sem_inc(M("projected"), 1)
            pe.wait_ge(M("glT_ready"), 2)
            for t in range(tiles):
                for j in range(2):
                    where = zs["z", t, j]
                    banks.wait_free(pe, where)
                    banks.fill(nc.tensor.matmul(m.ps[:, where[0], :], glT[0:RANK + 1, j, t * P:(t + 1) * P], w_gate[0:RANK + 1, j, :],
                                                start=True, stop=True), where)
            pe.wait_ge(M("g_ready_gla"), tiles * 2)
            for j in range(2):
                for i in range(2):
                    where = cums["b", j, i]
                    banks.wait_free(pe, where)
                    for half in range(2):
                        for t in range(TT):
                            c = (2 * i + half) * DK
                            last = nc.tensor.matmul(m.ps[:, where[0], half * T + t * P:half * T + (t + 1) * P], g[:, t, j, c:c + DK],
                                                    m.const(("fwd", "bwd")[j]), start=True, stop=True)
                    banks.fill(last, where)
            for t in range(tiles):
                for j in range(2):
                    where = sufs["e", t, j]
                    banks.wait_free(pe, where)
                    banks.fill(nc.tensor.matmul(m.ps[:, where[0], :], m.const(("after", "before")[j]), g[:, t, j, :], start=True, stop=True), where)
            where = sufs["decay"]
            banks.wait_free(pe, where)
            for t in range(tiles):
                for j in range(2):
                    for h in range(GH):
                        col = (j * GH + h) * 8 + 2 * t
                        last = nc.tensor.matmul(m.ps[:, where[0], col:col + 2], g[:, t, j, h * DK:(h + 1) * DK], m.const("chunk"),
                                                start=True, stop=True)
            banks.fill(last, where)

            def scores(h):
                where = atts["att", h]
                banks.wait_free(pe, where)
                for j in range(2):
                    for t in range(TT):
                        cols = slice(t * P, (t + 1) * P)
                        last = nc.tensor.matmul(m.ps[:, where[0], (j * TT + t) * P:(j * TT + t + 1) * P], k_in[:, j, h, cols],
                                                q_in[:, j, h, cols], start=True, stop=True)
                banks.fill(last, where)

            pe.wait_ge(M("in_ready"), 8)
            pe.wait_ge(M("k_end_ready"), tiles * 2)
            scores(0)
            for h in range(GH):
                if h + 1 < GH:
                    scores(h + 1)
                e = slice(h * DV, (h + 1) * DV)
                where = outs["o", h]
                banks.wait_free(pe, where)
                pe.wait_ge(M("att_masked"), h + 1)
                for t in range(TT):
                    for j in range(2):
                        nc.tensor.matmul(m.ps[:, where[0], t * DV:(t + 1) * DV], att[:, h % 2, (j * TT + t) * P:(j * TT + t + 1) * P],
                                         v[:, t, e], start=t == 0 and j == 0, stop=False, skip_group_check=True)
                for s in range(8):
                    for j in range(2):
                        t, c = steps[j][s]
                        rows_ = slice(c * CH, (c + 1) * CH)
                        if s >= 4:
                            pe.wait_ge(M(f"state_ready{j}"), 7 * h + s)
                            last = nc.tensor.matmul(m.ps[rows_, where[0], t * DV:(t + 1) * DV],
                                                    q_in[:, j, h, t * P + c * CH:t * P + (c + 1) * CH], S[:, j, (s - 1) % 2, :],
                                                    start=False, stop=s == 7, skip_group_check=True)
                            if s == 7 and j == 1:
                                banks.fill(last, where)
                            else:
                                last.then_inc(M(f"state_read{j}"), 1)
                        if s < 7:
                            there = kv[h, s, j]
                            banks.wait_free(pe, there)
                            banks.fill(nc.tensor.matmul(m.ps[:, there[0], 0:DV], k_end[rows_, t, j, h * DK:(h + 1) * DK], v[rows_, t, e],
                                                        start=True, stop=True), there)
            for t in range(TT):
                pe.wait_ge(M("y_gla"), t + 1)
                for n in range(2):
                    where = turned[t, n]
                    banks.wait_free(pe, where)
                    for c in range(4):
                        at = (4 * n + c) * P
                        last = nc.tensor.transpose(m.ps[:, where[0], c * P:(c + 1) * P], o[:, t, at:at + P], m.const("ident"))
                    banks.fill(last, where)
            pe.wait_ge(M("yT_gla"), 2 * TT)
            for n in range(2):
                w = ring.wait(pe, "b_w_out", n)
                for t in range(TT):
                    where = sums[t, n]
                    banks.wait_free(pe, where)
                    last = products(nc, m.ps[:, where[0], :], [(yT[:, c, t * P:(t + 1) * P], w[:, c, :]) for c in range(KT)])
                    banks.fill(last, where)
                pe.wait_ge(M(f"bank_full{where[0]}"), where[1] + 1)
                pe.sem_inc(M(f"chunk_used{(ring.at['b_w_out'] + n) % NSLOT}"), 1)

        @block.scalar
        def _(act):
            act.wait_ge(M("glT_ones"), 1)
            for j in range(2):
                where = proj["gl", j]
                banks.wait_full(act, where)
                banks.free_chained(act, nc.scalar.activation(glT[0:RANK, j, :], m.ps[0:RANK, where[0], :], ACT.Copy), where)
                act.sem_inc(M("glT_ready"), 1)
            for job in jobs:
                kind, chunk, i = job
                where = proj[job]
                banks.wait_full(act, where)
                src = m.ps[:, where[0], :]
                func, scale = ACT.Copy, 1.0
                if kind == "k":
                    dst = k[:, i, :]
                elif kind == "v":
                    dst = v[:, i, (chunk - 1) * 512:chunk * 512]
                elif kind == "r":
                    dst, func = r[:, i, (chunk - 4) * 512:(chunk - 3) * 512], ACT.Silu
                else:
                    dst = (kT if kind == "kT" else qT)[:, 2 * i:2 * i + 2, :].rearrange("p a b -> p (a b)")
                    scale = 1.0 if kind == "kT" else DK ** -0.5
                banks.free_chained(act, nc.scalar.activation(dst, src, func, scale=scale), where)
                act.sem_inc(M("gla_proj"), 1)
            for n in range(tiles * 2):
                act.wait_ge(M("abs_ready"), n + 1)
                a = ab[:, n % 2, :]
                nc.scalar.activation(a, a, ACT.Exp, scale=-1.0).then_inc(M("act_step"), 1)
                act.wait_ge(M("act_step"), n + 1)
                nc.scalar.activation(a, a, ACT.Ln, bias=1.0).then_inc(M("log_ready"), 1)
            for n, (j, i) in enumerate([(j, i) for j in range(2) for i in range(2)]):
                where = cums["b", j, i]
                banks.wait_full(act, where)
                for sign in range(2):
                    if n or sign:
                        pass
                    if 2 * n + sign >= 2:
                        act.wait_ge(M("in_ready"), 2 * n + sign - 1)
                    ins = nc.scalar.activation(ab[:, sign, :], m.ps[:, where[0], :], ACT.Exp, scale=(1 - 2 * sign) / TAU)
                    if sign:
                        banks.free_chained(act, ins, where)
                        act.sem_inc(M("exp_ready_gla"), 1)
                    else:
                        ins.then_inc(M("exp_ready_gla"), 1)
                        act.wait_ge(M("exp_ready_gla"), 2 * n + 1)
            for n, (t, j) in enumerate([(t, j) for t in range(tiles) for j in range(2)]):
                where = sufs["e", t, j]
                banks.wait_full(act, where)
                if n < 2:
                    act.wait_ge(M("in_ready"), 8)
                else:
                    act.wait_ge(M("k_end_ready"), n - 1)
                banks.free_chained(act, nc.scalar.activation(ab[:, n % 2, :], m.ps[:, where[0], :], ACT.Exp, scale=1.0 / TAU), where)
                act.sem_inc(M("suffix_ready"), 1)
            where = sufs["decay"]
            banks.wait_full(act, where)
            banks.free_chained(act, nc.scalar.activation(decay, m.ps[:, where[0], 0:64], ACT.Exp, scale=1.0 / TAU), where)
            act.sem_inc(M("decay_ready"), 1)
            for n in range(TT * GH):
                norm_act(nc, act, m, M, n0 + n + 1)
            for t in range(TT):
                for n in range(2):
                    where = turned[t, n]
                    banks.wait_full(act, where)
                    ins = nc.scalar.activation(yT[:, 4 * n:4 * n + 4, t * P:(t + 1) * P],
                                               m.ps[:, where[0], :].rearrange("p (c q) -> p c q", c=4), ACT.Copy)
                    banks.free_chained(act, ins, where)
                    act.sem_inc(M("yT_gla"), 1)

        @block.vector
        def _(dve):
            step = Chain(M, dve, "dve_step")
            step(nc.vector.memset(glT[0:RANK + 1, :, :], 1.0), "glT_ones")
            dve.wait_ge(M("projected"), 1)
            for n, (t, j) in enumerate([(t, j) for t in range(tiles) for j in range(2)]):
                where = zs["z", t, j]
                banks.wait_full(dve, where)
                z = m.ps[:, where[0], :]
                step(nc.vector.tensor_copy(low, z))
                a = ab[:, n % 2, :]
                ins = nc.vector.scalar_tensor_tensor(out=a, in0=z, scalar=-1.0, in1=low, op0=ALU.mult, op1=ALU.max)
                banks.free_chained(dve, ins, where)
                dve.sem_inc(M("abs_ready"), 1)
                dve.wait_ge(M("log_ready"), n + 1)
                step(nc.vector.scalar_tensor_tensor(out=g[:, t, j, :], in0=low, scalar=0.0, in1=a, op0=ALU.min, op1=ALU.subtract), "g_ready_gla")
            dve.wait_ge(M("gla_proj"), len(jobs))
            for n, (j, i) in enumerate([(j, i) for j in range(2) for i in range(2)]):
                for sign, (dst, src) in enumerate(((q_in, qT), (k_in, kT))):
                    dve.wait_ge(M("exp_ready_gla"), 2 * n + sign + 1)
                    step(nc.vector.tensor_tensor(dst[:, j, 2 * i:2 * i + 2, :].rearrange("p a b -> p (a b)"),
                                                 src[:, 2 * i:2 * i + 2, :].rearrange("p a b -> p (a b)"), ab[:, sign, :], ALU.mult), "in_ready")
            for n, (t, j) in enumerate([(t, j) for t in range(tiles) for j in range(2)]):
                dve.wait_ge(M("suffix_ready"), n + 1)
                step(nc.vector.tensor_tensor(k_end[:, t, j, :], k[:, t, :], ab[:, n % 2, :], ALU.mult), "k_end_ready")
            dve.wait_ge(M("decay_ready"), 1)

            def masked(h):
                where = atts["att", h]
                banks.wait_full(dve, where)
                if h >= 2:
                    banks.wait_full(dve, outs["o", h - 2])
                a = att[:, h % 2, :]
                banks.free_chained(dve, nc.vector.tensor_scalar(a, m.ps[:, where[0], :], -LOWEST, LOWEST, ALU.min, ALU.max), where)
                for j in range(2):
                    part = a[:, j * T:(j + 1) * T].rearrange("p (t i) -> p t i", t=TT)
                    mask = m.const(("fwd", "bwd")[j]).rearrange("p (o i) -> p o i", o=1).to_broadcast([P, TT, P])
                    ins = nc.vector.tensor_tensor(part, part, mask, ALU.mult)
                    if j == 0:
                        step(ins)
                    else:
                        step(ins, "att_masked")

            masked(0)
            for h in range(GH):
                if h + 1 < GH:
                    masked(h + 1)
                for s in range(7):
                    for j in range(2):
                        t, c = steps[j][s]
                        there = kv[h, s, j]
                        banks.wait_full(dve, there)
                        if s >= 5:
                            dve.wait_ge(M(f"state_read{j}"), (4 - j) * h + s - 4)
                        elif s <= 1 and h:
                            banks.wait_full(dve, outs["o", h - 1])
                        new, kv_ = S[:, j, s % 2, :], m.ps[:, there[0], 0:DV]
                        if s == 0:
                            ins = nc.vector.tensor_copy(new, kv_)
                        else:
                            col = (j * GH + h) * 8 + 2 * t + c
                            ins = nc.vector.scalar_tensor_tensor(out=new, in0=S[:, j, (s - 1) % 2, :], scalar=decay[:, col:col + 1], in1=kv_,
                                                                 op0=ALU.mult, op1=ALU.add)
                        banks.free_chained(dve, ins, there)
                        dve.sem_inc(M(f"state_ready{j}"), 1)
                where = outs["o", h]
                banks.wait_full(dve, where)
                for t in range(TT):
                    norm_dve(nc, dve, step, m, M, m.ps[:, where[0], t * DV:(t + 1) * DV], n0 + TT * h + t + 1,
                             out=o[:, t, h * DV:(h + 1) * DV])
                banks.free_chained(dve, nc.vector.memset(m.stats[:, 40:41], 0.0), where)
            dve.wait_ge(M("gla_in"), 48)
            for t in range(TT):
                step(nc.vector.tensor_tensor(o[:, t, :], o[:, t, :], gn, ALU.mult))
                step(nc.vector.tensor_tensor(o[:, t, :], o[:, t, :], r[:, t, :], ALU.mult), "y_gla")
    return sums


LASTING = ("bank_", "chunk_", "dve_step", "rows_in", "variance_ready", "std_ready", "consts_in")



def program(nc, d, out):
    with ExitStack() as ctx:
        m = Memory(nc, ctx)
        d = dict(d, mod=nc.dram_tensor("mod_rows", [2, 2, 6 * D], F32, kind="Internal").ap())
        M = Marks(nc, ctx)
        banks = Banks(M)
        chunks = [("w_in", d["w_in"][n], SLOT) for n in range(N_IN)]
        chunks += [("w_proj_a", d["w_proj_a"], 2 * D)]
        chunks += [("w_proj_b", d["w_proj_b"][n], SLOT) for n in range(2)]
        chunks += [("w_out", d["w_out"][n], SLOT) for n in range(2)]
        chunks += [("moe", d["moe"][n // PER_EXPERT, n % PER_EXPERT], SLOT) for n in range(PER_EXPERT * NE)]
        for layer in range(2):
            chunks += [(f"w_mod{layer}", d["w_mod"][layer, n], SLOT) for n in range(12)]
        chunks += [("a_w_in", d["a_w_in"][n], SLOT) for n in range(4)]
        chunks += [("a_w_out", d["a_w_out"][n], SLOT) for n in range(2)]
        chunks += [("w_q0", d["w_q"][0, n], SLOT) for n in range(2)]
        chunks += [("b_w_in", d["b_w_in"][n], SLOT) for n in range(6)]
        chunks += [("b_w_out", d["b_w_out"][n], SLOT) for n in range(2)]
        chunks += [("w_q1", d["w_q"][1, n], SLOT) for n in range(2)]
        ring = Ring(M, m.ring, chunks)
        attention(nc, d, m, M, banks, ring)
        route(nc,d,m,M,banks,ring)
        moe(nc,d,m,M,banks,ring)
        M.retire(LASTING)
        modulations(nc, d, m, M, banks, ring)
        modulate(nc, d, m, M, banks, ring, 0, SCALE1, SHIFT1, 4)
        sums = chunk_mlp(nc, d, m, M, banks, ring)
        residual(nc, d, m, M, banks, sums, 0, GATE1, 0, 4)
        modulate(nc, d, m, M, banks, ring, 0, SCALE2, SHIFT2, 4)
        select(nc, d, m, M, banks, ring, 0, 4)
        sums = peer(nc, d, m, M, banks, 0, 4, 0)
        residual(nc, d, m, M, banks, sums, 0, GATE2, 1, 4)
        modulate(nc, d, m, M, banks, ring, 1, SCALE1, SHIFT1, 4)
        sums = gla(nc, d, m, M, banks, ring)
        residual(nc, d, m, M, banks, sums, 1, GATE1, 0, 2)
        modulate(nc, d, m, M, banks, ring, 1, SCALE2, SHIFT2, 2)
        select(nc, d, m, M, banks, ring, 1, 2)
        sums = peer(nc, d, m, M, banks, 1, 2, 4)
        residual(nc, d, m, M, banks, sums, 1, GATE2, 1, 2, out)


def chunked(w):
    lead = w.shape[:-2]
    n = w.shape[-1] // 512
    w = w.reshape(*lead, KT, P, n, 512)
    k = len(lead)
    return np.ascontiguousarray(w.transpose(*range(k), k + 2, k + 1, k, k + 3)).reshape(*lead, n, P, KT * 512)


def pair_heads(w, axis):
    w = np.moveaxis(w, axis, -1)
    w = w.reshape(*w.shape[:-1], 2, SWA_PAIRS, HD).swapaxes(-3, -2).reshape(*w.shape[:-1], -1)
    return np.moveaxis(w, -1, axis)


def columns(a):
    a = a.reshape(*a.shape[:-1], -1, P)
    return np.moveaxis(a, -1, 0)


def layout(i):
    w = i["w_in"][0]
    qa, ka, va, qb, kb, vb, ga, gb = np.split(w, np.cumsum([768, 768, 768, 1024, 128, 128, 1024]), axis=1)
    w_in = np.concatenate([qa, ka, pair_heads(qb, 1), kb, va, vb, ga, gb], axis=1)
    moe = np.stack([chunked(i[n][0]) for n in ("w_gate", "w_up", "w_down")], 1).reshape(NE, PER_EXPERT, P, SLOT)
    out = {
        "x": i["x"][0],
        "xT": i["x"][0].T.reshape(KT, P, T).transpose(1, 0, 2),
        "w_in": chunked(w_in),
        "w_proj_a": i["w_proj_a"][0].reshape(2, P, D).transpose(1, 0, 2).reshape(P, 2 * D),
        "w_proj_b": chunked(pair_heads(i["w_proj_b"][0], 0)),
        "w_out": chunked(i["w_out"][0]),
        "sinks": i["sinks"],
        "moe": moe,
        "lns": np.stack([i["ln1_g"][0], i["ln1_b"][0], i["ln2_g"][0], i["ln2_b"][0]]),
        "router_w": i["router_w"][0].reshape(KT, P, NE).transpose(1, 0, 2),
        "router_b": i["router_b"],
        "b_gate": columns(i["b_gate"][0]).reshape(P, NE * KT),
        "b_up": columns(i["b_up"][0]).reshape(P, NE * KT),
        "b_down": i["b_down"][0],
        "c": np.stack([i["c_2"][0], i["c_ctx_2"]]).reshape(2, KT, P).transpose(2, 1, 0),
        "ctx": i["ctx_2"][0],
        "w_mod": chunked(i["w_mod_2"]),
        "b_mod": i["b_mod_2"],
        "ln_g": i["ln_g_2"].reshape(4, D),
        "ln_b": i["ln_b_2"].reshape(4, D),
        "a_w_in": chunked(np.concatenate([i["a_w_in_2"][0][:, D:], i["a_w_in_2"][0][:, :D]], 1)),
        "a_norm": np.stack([i["a_norm_g_2"][0], i["a_norm_b_2"][0]]),
        "a_w_s": i["a_w_s_2"][0].transpose(2, 0, 1),
        "a_b_s": i["a_b_s_2"][0].T,
        "a_w_out": chunked(i["a_w_out_2"][0]),
        "b_w_in": chunked(np.concatenate([i["b_w_in_2"][0][:, a:b] for a, b in ((512, 1024), (1024, 2048), (0, 512), (2048, 3072))], 1)),
        "b_w_gl": i["b_w_in_2"][0][:, 3072:].reshape(KT, P, 2 * RANK).transpose(1, 0, 2),
        "b_w_gate": np.concatenate([i["b_w_gate_2"][0], i["b_gate_bias_2"][0][:, None, :]], 1).transpose(1, 0, 2),
        "b_gn_g": i["b_gn_g_2"],
        "b_w_out": chunked(i["b_w_out_2"][0]),
        "w_q": chunked(i["p_w_q_2"]),
        "keys": i["p_keys_2"].transpose(0, 1, 3, 2).reshape(2, P, NKEY),
        "u0": i["p_u_2"][0], "u1": i["p_u_2"][1], "v0": i["p_v_2"][0], "v1": i["p_v_2"][1],
    }
    out["consts"] = np.concatenate([np.asarray(a, np.float32) for a in constants().values()], 1)
    out["dist"] = distances()
    return out


def kernel(**inputs):
    import numpy as _np
    import concourse.bacc as _bacc
    from concourse import mybir as _mybir
    from concourse.bass_utils import run_bass_kernel_spmd as _run

    nc = _bacc.Bacc("TRN2", target_bir_lowering=False, num_devices=1)
    arrays, aps = {}, {}
    for name, a in layout({k: _np.asarray(v) for k, v in inputs.items()}).items():
        a = _np.ascontiguousarray(a)
        arrays[f"in_{name}"] = a
        aps[name] = nc.dram_tensor(f"in_{name}", a.shape, _mybir.dt.from_np(a.dtype), kind="ExternalInput").ap()
    out = nc.dram_tensor("out_0", (1, T, D), _mybir.dt.float32, kind="ExternalOutput").ap()
    program(nc, aps, out)
    r = _run(nc, [arrays], core_ids=[0])
    return r.results[0]["out_0"]
```

```python
from contextlib import ExitStack

import numpy as np
import concourse.bass as bass
from concourse import mybir

F32 = mybir.dt.float32
U32 = mybir.dt.uint32
I32 = mybir.dt.int32
ALU = mybir.AluOpType
ACT = mybir.ActivationFunctionType
AX = mybir.AxisListType

P = 128
D = 1024
KT = D // P
T = 256
TT = T // P
HD = 64
EPS = 1e-5
DIL_HEADS, DIL_GROUPS, SWA_PAIRS = 4, 3, 8
N_SLOPES = 28
SLOPES = [float(np.float32(2.0 ** (-8.0 * (h + 1) / N_SLOPES))) for h in range(N_SLOPES)]
Q_A, K_A, Q_B, K_B, V_T, GATE = 0, 6, 12, 20, 21, 28
V_COLS = 896
N_IN = 11
ALPHA1 = 2.0 ** 0.25
FAR = -1e34
NE, TOPK, SLOTS = 32, 4, 64
PASSES = T // SLOTS
PER_EXPERT = 6
LIMIT, SW_ALPHA = 7.0, 1.702
ALPHA2 = 4.0 ** 0.25
PH, PK, NKEY = 8, 16, 128
GH, DK, DV, RANK, TAU = 4, 128, 256, 16, 16.0
CH = 64
LOWEST = -3.0e38
SLOT = KT * 512
NSLOT = 6


class Marks:

    def __init__(self, nc, ctx):
        self.nc, self.ctx, self.sems, self.n, self.spare = nc, ctx, {}, {}, []

    def __call__(self, name):
        if name not in self.sems:
            self.sems[name] = self.spare.pop() if self.spare else self.ctx.enter_context(self.nc.semaphore(name))
        return self.sems[name]

    def retire(self, kept):
        names = [n for n in self.sems if not n.startswith(kept)]
        with self.nc.Block() as block:

            @block.sync
            def _(sp):
                for name in names:
                    sp.sem_clear(self.sems[name])

        for name in names:
            self.spare.append(self.sems.pop(name))
            self.n.pop(name, None)

    def up(self, ins, name, by=1):
        ins.then_inc(self(name), by)
        self.n[name] = self.n.get(name, 0) + by
        return self.n[name]


class Chain:

    def __init__(self, marks, eng, name):
        self.marks, self.eng, self.name = marks, eng, name

    def __call__(self, ins, name=None):
        name = name or self.name
        value = self.marks.up(ins, name)
        self.eng.wait_ge(self.marks(name), value)


class Banks:

    def __init__(self, marks):
        self.marks, self.used = marks, [0] * 8

    def plan(self, names, banks):
        table = {}
        for i, name in enumerate(names):
            bank = banks[i % len(banks)]
            table[name] = (bank, self.used[bank])
            self.used[bank] += 1
        return table

    def wait_free(self, pe, where):
        bank, nth = where
        if nth:
            pe.wait_ge(self.marks(f"bank_free{bank}"), nth)

    def fill(self, ins, where):
        ins.then_inc(self.marks(f"bank_full{where[0]}"), 1)

    def wait_full(self, eng, where):
        eng.wait_ge(self.marks(f"bank_full{where[0]}"), where[1] + 1)

    def free(self, ins, where):
        ins.then_inc(self.marks(f"bank_free{where[0]}"), 1)

    def free_chained(self, eng, ins, where):
        ins.then_inc(self.marks(f"bank_free{where[0]}"), 1)
        eng.wait_ge(self.marks(f"bank_free{where[0]}"), where[1] + 1)


class Ring:

    def __init__(self, marks, mem, chunks):
        self.marks, self.mem, self.chunks, self.sent = marks, mem, chunks, 0
        self.at = {}
        for n, (name, _, _) in enumerate(chunks):
            self.at.setdefault(name, n)

    def load(self, sp, end):
        for n in range(self.sent, min(end, len(self.chunks))):
            slot, nth = n % NSLOT, n // NSLOT
            _, src, size = self.chunks[n]
            if nth:
                sp.wait_ge(self.marks(f"chunk_used{slot}"), nth)
            sp.dma_start(self.mem[:, slot, 0:size], src).then_inc(self.marks(f"chunk_in{slot}"), 16)
        self.sent = max(self.sent, min(end, len(self.chunks)))

    def upto(self, name, count):
        return self.at[name] + count + NSLOT

    def wait(self, pe, name, i=0):
        n = self.at[name] + i
        pe.wait_ge(self.marks(f"chunk_in{n % NSLOT}"), 16 * (n // NSLOT + 1))
        return self.mem[:, n % NSLOT, :].rearrange("p (k j) -> p k j", k=KT)

    def used(self, ins, name, i=0):
        ins.then_inc(self.marks(f"chunk_used{(self.at[name] + i) % NSLOT}"), 1)


def products(nc, out, pairs):
    for i, (lhs, rhs) in enumerate(pairs):
        last = nc.tensor.matmul(out, lhs, rhs, start=i == 0, stop=i == len(pairs) - 1)
    return last


class Memory:

    def __init__(self, nc, ctx):
        def sb(name, shape, dtype=F32):
            return ctx.enter_context(nc.sbuf_tensor("sb_" + name, shape, dtype))

        self.ring = sb("ring", [P, NSLOT, SLOT])
        self.arena = sb("arena", [P, 16384])
        self.H = sb("H", [P, 4, D])
        self.X = sb("X", [P, 4, D])
        self.consts = sb("consts", [P, CONST_COLS])
        self.idx = sb("idx", [P, 2 * PK], U32)[:, :]
        self.wts = sb("wts", [P, 4 * PK])
        self.diag = [sb(f"diag{i}", [P, P])[:, :] for i in range(4)]
        self.cur_idx = sb("cur_idx", [P, 2 * PK], U32)
        self.dots = sb("dots", [P, PK])
        self.act = sb("act", [P, PK])
        self.stats = sb("stats", [P, 64])
        self.count = sb("count", [1, 2], I32)
        self.norms, self.rows_sent = 0, 0
        self.ps = ctx.enter_context(nc.psum_tensor("ps", [P, 8, 512], F32))

    def const(self, name):
        a, n = CONST_AT[name]
        return self.consts[:, a:a + n]

    def part(self, start, *dims):
        size = int(np.prod(dims))
        flat = self.arena[:, start:start + size]
        names = "abcd"[:len(dims)]
        if len(dims) == 1:
            return flat
        return flat.rearrange(f"p ({' '.join(names)}) -> p {' '.join(names)}",
                              **{n: d for n, d in zip(names, dims)})


def constants():
    j, i = np.arange(P)[:, None], np.arange(P)[None, :]
    same = (j // CH) == (i // CH)
    parts = {
        "ident": (j == i),
        "upto": (j <= i),
        "ones": np.ones((P, P)),
        "fwd": (j <= i) & same,
        "bwd": (j >= i) & same,
        "after": (j > i) & same,
        "before": (j < i) & same,
        "chunk": j // CH == np.arange(2)[None, :],
        "iota": np.broadcast_to(np.arange(P) % CH, (P, P)),
        "zero": np.zeros((P, P)),
    }
    return parts


CONST_AT, CONST_COLS = {}, 0
for _name, _a in constants().items():
    CONST_AT[_name] = (CONST_COLS, _a.shape[1])
    CONST_COLS += _a.shape[1]


def distances():
    out = np.full((P, 4, 384), FAR, np.float32)
    for block, (at, nk) in enumerate(((0, 128), (128, 256))):
        i, j = block * P + np.arange(P)[:, None], np.arange(nk)[None, :]
        d = i - j
        seen = [(d >= 0) & (d <= 127), (d >= 0) & (d <= 128), (d >= 0) & (d % 4 == 0), (d >= 0) & (d % 16 == 0)]
        for kind, s in enumerate(seen):
            out[:, kind, at:at + nk] = np.where(s, -d, FAR)
    return out



def attention(nc, d, m, M, banks, ring):
    qk = m.part(0, 21, T)
    v = m.part(5376, TT, V_COLS)
    gates = m.part(7168, 16, T)
    oT = m.part(11264, 10, T)
    pT = m.part(13824, 2, 6, P)
    tmp = m.part(15360, 2, T)
    rows = m.H[:, :, :].rearrange("p a b -> p (a b)")
    xT = rows[:, 0:2048].rearrange("p (k t) -> p k t", k=KT)
    sc = rows[:, 2048:2048 + 2 * 772].rearrange("p (u c) -> p u c", u=2)
    spare = m.X[:, 2:4, :].rearrange("p a b -> p (a b)")
    dist = spare[:, 0:1536].rearrange("p (k c) -> p k c", k=4)
    sinks = spare[:, 1536:1552]
    X = m.X
    ident = m.const("ident")

    units = [("dil", h, b) for b in range(TT) for h in range(DIL_HEADS)]
    units += [("swa", t, b) for b in range(TT) for t in range(SWA_PAIRS)]

    def blocks(unit):
        return (DIL_GROUPS if unit[0] == "dil" else 2), unit[2] + 1

    proj = [("qk", n) for n in range(10)] + [("kb", 0)] + [("v", i) for i in range(4)]
    proj += [("gate", n) for n in range(8)]
    gp = banks.plan(proj, [0, 1, 2, 3])
    go = banks.plan([("o", u) for u in range(len(units))], [6, 7])
    gm = banks.plan([("m", i) for i in range(KT)], [0, 1, 2, 3])
    gx = banks.plan([("x", i) for i in range(4)], [4, 5, 6, 7])

    with nc.Block() as block:

        @block.sync
        def _(sp):
            sp.dma_start(xT, d["xT"]).then_inc(M("xT_in"), 16)
            ring.load(sp, 2)
            sp.dma_start(m.consts[:, :], d["consts"]).then_inc(M("consts_in"), 16)
            sp.dma_start(dist, d["dist"]).then_inc(M("dist_in"), 16)
            sp.dma_start(sinks, d["sinks"].to_broadcast([P, 16])).then_inc(M("dist_in"), 16)
            sp.dma_start(X[:, 0:TT, :], d["x"].rearrange("(t p) c -> p t c", p=P)).then_inc(M("x_in"), 16)
            ring.load(sp, ring.upto("w_out", 2))

        @block.tensor
        def _(pe):
            pe.wait_ge(M("xT_in"), 16)

            def channel_tile(chunk, j, out):
                return products(nc, out, [(w[:, k, j * P:(j + 1) * P], xT[:, k, :]) for k in range(KT)])

            w = ring.wait(pe, "w_in", 0)
            for n in range(10):
                if n and n % 2 == 0:
                    w = ring.wait(pe, "w_in", n // 2)
                where = gp["qk", n]
                banks.wait_free(pe, where)
                channel_tile(w, 2 * (n % 2), m.ps[:, where[0], 0:T])
                last = channel_tile(w, 2 * (n % 2) + 1, m.ps[:, where[0], T:2 * T])
                banks.fill(last, where)
                if n % 2:
                    pe.wait_ge(M(f"bank_full{where[0]}"), where[1] + 1)
                    pe.sem_inc(M(f"chunk_used{(ring.at['w_in'] + n // 2) % NSLOT}"), 1)
            w = ring.wait(pe, "w_in", 5)
            where = gp["kb", 0]
            banks.wait_free(pe, where)
            banks.fill(channel_tile(w, 0, m.ps[:, where[0], 0:T]), where)
            for i in range(4):
                t, piece = i % 2, i // 2
                if i == 2:
                    w = ring.wait(pe, "w_in", 6)
                cols = slice(P, 512) if piece == 0 else slice(0, 512)
                where = gp["v", i]
                banks.wait_free(pe, where)
                last = products(nc, m.ps[:, where[0], 0:cols.stop - cols.start],
                                [(xT[:, k, t * P:(t + 1) * P], w[:, k, cols]) for k in range(KT)])
                banks.fill(last, where)
                if t:
                    pe.wait_ge(M(f"bank_full{where[0]}"), where[1] + 1)
                    pe.sem_inc(M(f"chunk_used{(ring.at['w_in'] + 5 + piece) % NSLOT}"), 1)
            for n in range(8):
                if n % 2 == 0:
                    w = ring.wait(pe, "w_in", 7 + n // 2)
                where = gp["gate", n]
                banks.wait_free(pe, where)
                channel_tile(w, 2 * (n % 2), m.ps[:, where[0], 0:T])
                last = channel_tile(w, 2 * (n % 2) + 1, m.ps[:, where[0], T:2 * T])
                banks.fill(last, where)
                if n % 2:
                    pe.wait_ge(M(f"bank_full{where[0]}"), where[1] + 1)
                    pe.sem_inc(M(f"chunk_used{(ring.at['w_in'] + 7 + n // 2) % NSLOT}"), 1)

            def scores(u):
                kind, h, b = units[u]
                nk = P * (b + 1)
                out = m.ps[:, 2 * (u % 2):2 * (u % 2) + 2, :].rearrange("p a b -> p (a b)")
                if u >= 2:
                    pe.wait_ge(M("scores_read"), u - 1)
                for g in range(blocks(units[u])[0]):
                    if kind == "dil":
                        rows_ = slice((h % 2) * HD, (h % 2) * HD + HD)
                        qt, kt = Q_A + 2 * g + h // 2, K_A + 2 * g + h // 2
                    else:
                        rows_ = slice(g * HD, (g + 1) * HD)
                        qt, kt = Q_B + h, K_B
                    at = g * nk if kind == "dil" else g * 512
                    last = nc.tensor.matmul(out[:, at:at + nk], qk[rows_, qt, b * P:(b + 1) * P],
                                            qk[rows_, kt, 0:nk], start=True, stop=True)
                last.then_inc(M("scores_done"), 1)

            pe.wait_ge(M("qkv_ready"), 15)
            pe.wait_ge(M("consts_in"), 16)
            pe.wait_ge(M("gates_ready"), 8)
            scores(0)
            scores(1)
            for u, unit in enumerate(units):
                n_seg, nb = blocks(unit)
                turned = m.ps[:, 4:6, :].rearrange("p a b -> p (a b)")
                pe.wait_ge(M("probs_ready"), u + 1)
                if u:
                    pe.wait_ge(M("probsT_ready"), u)
                stride = nb * P + (1 if unit[0] == "swa" else 0)
                for g in range(n_seg):
                    for kb in range(nb):
                        at = g * stride + kb * P
                        i = g * nb + kb
                        last = nc.tensor.transpose(turned[:, i * P:(i + 1) * P], sc[:, u % 2, at:at + P], ident)
                last.then_inc(M("probsT_done"), 1)
                if u + 2 < len(units):
                    scores(u + 2)
                pe.wait_ge(M("probsT_ready"), u + 1)
                where = go["o", u]
                banks.wait_free(pe, where)
                kind, h, b = unit
                for g in range(n_seg):
                    for kb in range(nb):
                        i = g * nb + kb
                        if kind == "dil":
                            rows_ = slice((h % 2) * HD, (h % 2) * HD + HD)
                            col, start, stop = g * 256 + h * HD, i == 0, i == n_seg * nb - 1
                        else:
                            rows_ = slice(g * HD, (g + 1) * HD)
                            col, start, stop = 768 + g * HD, kb == 0, kb == nb - 1
                        last = nc.tensor.matmul(m.ps[rows_, where[0], 0:P], v[:, kb, col:col + HD],
                                                pT[:, u % 2, i, :], start=start, stop=stop)
                banks.fill(last, where)

            wa = ring.wait(pe, "w_proj_a", 0)
            wa = ring.mem[:, ring.at["w_proj_a"] % NSLOT, 0:2048].rearrange("p (k j) -> p k j", k=2)
            pe.wait_ge(M("o_ready"), len(units))
            for i in range(KT):
                if i % 4 == 0:
                    wb = ring.wait(pe, "w_proj_b", i // 4)
                where = gm["m", i]
                banks.wait_free(pe, where)
                products(nc, m.ps[:, where[0], 0:T], [(wa[:, k, i * P:(i + 1) * P], oT[:, k, :]) for k in range(2)])
                j = i % 4
                last = products(nc, m.ps[:, where[0], T:2 * T],
                                [(wb[:, k, j * P:(j + 1) * P], oT[:, 2 + k, :]) for k in range(KT)])
                banks.fill(last, where)
                if j == 3:
                    pe.wait_ge(M(f"bank_full{where[0]}"), where[1] + 1)
                    pe.sem_inc(M(f"chunk_used{(ring.at['w_proj_b'] + i // 4) % NSLOT}"), 1)
                    if i == KT - 1:
                        pe.sem_inc(M(f"chunk_used{ring.at['w_proj_a'] % NSLOT}"), 1)
            pe.wait_ge(M("merged_ready"), KT)
            for i in range(4):
                half, t = i // 2, i % 2
                w = ring.wait(pe, "w_out", half)
                where = gx["x", i]
                banks.wait_free(pe, where)
                last = products(nc, m.ps[:, where[0], :], [(gates[:, k, t * P:(t + 1) * P], w[:, k, :]) for k in range(KT)])
                banks.fill(last, where)
                if t:
                    pe.wait_ge(M(f"bank_full{where[0]}"), where[1] + 1)
                    pe.sem_inc(M(f"chunk_used{(ring.at['w_out'] + half) % NSLOT}"), 1)

        @block.scalar
        def _(act):
            for n in range(10):
                where = gp["qk", n]
                banks.wait_full(act, where)
                is_q = n < 3 or n >= 6
                ins = nc.scalar.activation(qk[:, 2 * n:2 * n + 2, :].rearrange("p a b -> p (a b)"), m.ps[:, where[0], :],
                                           ACT.Copy, scale=HD ** -0.5 if is_q else 1.0)
                banks.free_chained(act, ins, where)
                act.sem_inc(M("qkv_ready"), 1)
            where = gp["kb", 0]
            banks.wait_full(act, where)
            banks.free_chained(act, nc.scalar.activation(qk[:, K_B, :], m.ps[:, where[0], 0:T], ACT.Copy), where)
            act.sem_inc(M("qkv_ready"), 1)
            for i in range(4):
                t, piece = i % 2, i // 2
                where = gp["v", i]
                banks.wait_full(act, where)
                dst = v[:, t, 0:384] if piece == 0 else v[:, t, 384:V_COLS]
                banks.free_chained(act, nc.scalar.activation(dst, m.ps[:, where[0], 0:384 if piece == 0 else 512], ACT.Copy), where)
                act.sem_inc(M("qkv_ready"), 1)
            for n in range(8):
                where = gp["gate", n]
                banks.wait_full(act, where)
                ins = nc.scalar.activation(gates[:, 2 * n:2 * n + 2, :].rearrange("p a b -> p (a b)"), m.ps[:, where[0], :], ACT.Sigmoid)
                banks.free_chained(act, ins, where)
                act.sem_inc(M("gates_ready"), 1)

            def exps(u):
                kind, h, b = units[u]
                nk = P * (b + 1)
                act.wait_ge(M("max_ready"), u + 1)
                n, width = (1, 3 * nk) if kind == "dil" else (2, nk + 1)
                for s in range(n):
                    part = sc[:, u % 2, s * width:(s + 1) * width]
                    ins = nc.scalar.activation(part, part, ACT.Exp, bias=m.stats[:, 4 + 2 * (u % 2) + s:5 + 2 * (u % 2) + s],
                                               accum_out=m.stats[:, 8 + 2 * (u % 2) + s:9 + 2 * (u % 2) + s])
                ins.then_inc(M("exp_done"), 1)

            def turn(u):
                n_seg, nb = blocks(units[u])
                act.wait_ge(M("probsT_done"), u + 1)
                if u >= 2:
                    banks.wait_full(act, go["o", u - 2])
                n = n_seg * nb * P
                nc.scalar.activation(pT[:, u % 2, :, :].rearrange("p a b -> p (a b)")[:, 0:n],
                                     m.ps[:, 4:6, :].rearrange("p a b -> p (a b)")[:, 0:n], ACT.Copy)\
                    .then_inc(M("probsT_ready"), 1)

            exps(0)
            for u in range(len(units)):
                if u + 1 < len(units):
                    exps(u + 1)
                turn(u)

        @block.vector
        def _(dve):
            step = Chain(M, dve, "dve_step")
            dve.wait_ge(M("dist_in"), 32)

            def biased(u):
                kind, h, b = units[u]
                nk = P * (b + 1)
                dve.wait_ge(M("scores_done"), u + 1)
                if u >= 2:
                    dve.wait_ge(M("probsT_done"), u - 1)
                scores_ = m.ps[:, 2 * (u % 2):2 * (u % 2) + 2, :].rearrange("p a b -> p (a b)")
                at = 0 if b == 0 else P
                n_seg = blocks(units[u])[0]
                for g in range(n_seg):
                    if kind == "dil":
                        kindd, slope, col, src = 1 + g, SLOPES[16 + 4 * g + h], g * nk, g * nk
                    else:
                        kindd, slope, col, src = 0, SLOPES[8 * g + h], g * (nk + 1), g * 512
                        nc.vector.tensor_copy(sc[:, u % 2, col + nk:col + nk + 1], sinks[:, 8 * g + h:8 * g + h + 1]).then_inc(M("sink_set"), 1)
                    last = nc.vector.scalar_tensor_tensor(
                        out=sc[:, u % 2, col:col + nk], in0=dist[:, kindd, at:at + nk], scalar=slope,
                        in1=scores_[:, src:src + nk], op0=ALU.mult, op1=ALU.add)
                last.then_inc(M("scores_read"), 1)
                dve.wait_ge(M("scores_read"), u + 1)
                n, width = (1, 3 * nk) if kind == "dil" else (2, nk + 1)
                step(nc.vector.tensor_reduce(m.stats[:, 0:n], sc[:, u % 2, 0:n * width].rearrange("p (s c) -> p s c", s=n),
                                             axis=AX.X, op=ALU.max))
                nc.vector.tensor_scalar(m.stats[:, 4 + 2 * (u % 2):4 + 2 * (u % 2) + n], m.stats[:, 0:n], -1.0, None, ALU.mult)\
                    .then_inc(M("max_ready"), 1)
                dve.wait_ge(M("max_ready"), u + 1)

            def normal(u):
                kind, h, b = units[u]
                nk = P * (b + 1)
                dve.wait_ge(M("exp_done"), u + 1)
                n, width = (1, 3 * nk) if kind == "dil" else (2, nk + 1)
                den = m.stats[:, 8 + 2 * (u % 2):8 + 2 * (u % 2) + n]
                step(nc.vector.reciprocal(m.stats[:, 12:12 + n], den))
                p3 = sc[:, u % 2, 0:n * width].rearrange("p (s c) -> p s c", s=n)
                nc.vector.tensor_tensor(p3, p3, m.stats[:, 12:12 + n].rearrange("p (s c) -> p s c", c=1).to_broadcast([P, n, width]),
                                        ALU.mult).then_inc(M("probs_ready"), 1)
                dve.wait_ge(M("probs_ready"), u + 1)

            def out_of(u):
                kind, h, b = units[u]
                where = go["o", u]
                banks.wait_full(dve, where)
                if kind == "dil":
                    rows_, tile = slice((h % 2) * HD, (h % 2) * HD + HD), h // 2
                else:
                    rows_, tile = slice(0, P), 2 + h
                ins = nc.vector.tensor_copy(oT[rows_, tile, b * P:(b + 1) * P], m.ps[rows_, where[0], 0:P])
                banks.free_chained(dve, ins, where)
                dve.sem_inc(M("o_ready"), 1)

            biased(0)
            for u in range(len(units)):
                if u + 1 < len(units):
                    biased(u + 1)
                normal(u)
                if u:
                    out_of(u - 1)
            out_of(len(units) - 1)
            dve.wait_ge(M("gates_ready"), 8)
            both = m.part(7168, 2, KT, T)
            for i in range(KT):
                where = gm["m", i]
                banks.wait_full(dve, where)
                ins = nc.vector.tensor_tensor(tmp, m.ps[:, where[0], :].rearrange("p (a b) -> p a b", a=2), both[:, :, i, :], ALU.mult)
                banks.free_chained(dve, ins, where)
                nc.vector.tensor_tensor(gates[:, i, :], tmp[:, 0, :], tmp[:, 1, :], ALU.add).then_inc(M("merged_ready"), 1)
                dve.wait_ge(M("merged_ready"), i + 1)
            dve.wait_ge(M("x_in"), 16)
            for i in range(4):
                half, t = i // 2, i % 2
                where = gx["x", i]
                banks.wait_full(dve, where)
                part = X[:, t, half * 512:(half + 1) * 512]
                ins = nc.vector.scalar_tensor_tensor(out=part, in0=part, scalar=ALPHA1, in1=m.ps[:, where[0], :], op0=ALU.mult, op1=ALU.add)
                banks.free_chained(dve, ins, where)



LN = {"sum": (16, 28), "mv": (28, 30), "var": (30, 31), "std": (31, 32), "rstd": (32, 33)}


def stat(m, name):
    a, b = LN[name]
    return m.stats[:, a:b]


def norm_dve(nc, dve, step, m, M, x, n, out=None):
    out = x if out is None else out
    width = x.shape[-1]
    pieces = max(1, width // 512)
    for i in range(pieces):
        piece = x[:, i * 512:(i + 1) * 512] if pieces > 1 else x
        step(nc.vector.bn_stats(m.stats[:, 16 + 6 * i:22 + 6 * i], piece))
    step(nc.vector.bn_aggr(stat(m, "mv"), m.stats[:, 16:16 + 6 * pieces]))
    step(nc.vector.tensor_scalar(stat(m, "var"), m.stats[:, 29:30], EPS, None, ALU.add), "variance_ready")
    dve.wait_ge(M("std_ready"), n)
    step(nc.vector.reciprocal(stat(m, "rstd"), stat(m, "std")))
    step(nc.vector.tensor_scalar(out, x, m.stats[:, 28:29], stat(m, "rstd"), ALU.subtract, ALU.mult))


def norm_act(nc, act, m, M, n):
    act.wait_ge(M("variance_ready"), n)
    nc.scalar.activation(stat(m, "std"), stat(m, "var"), ACT.Sqrt).then_inc(M("std_ready"), 1)


def row(m, i):
    return m.part(12288, 4, D)[:, i, :]


def load_rows(sp, M, m, sources):
    for i, src in enumerate(sources):
        sp.dma_start(row(m, i), src.to_broadcast([P, D])).then_inc(M("rows_in"), 16)
    m.rows_sent += 16 * len(sources)



class Experts:

    def __init__(self, m):
        self.yT = m.part(0, KT, T)
        self.router = m.part(4096, KT, NE)
        self.router_b = m.part(4352, NE)
        self.logits = m.part(4384, TT, NE)
        self.gates = m.part(4448, TT, NE)
        self.chosen = m.part(4512, TT, NE)
        self.place = m.part(4576, TT, NE + 1)
        self.onehot = m.part(4672, NE)
        self.top = m.part(4704, TT, 8)
        self.top_i = m.part(4720, TT, 8)
        self.top_at = m.arena[:, 4736:4744].bitcast(U32)
        self.exp = m.part(4752, 8)
        self.gatesT = m.part(4800, T)
        self.total = m.part(5056, NE + 2)
        self.b_gate = m.part(5120, D)
        self.b_up = m.part(6144, D)
        self.b_down = m.part(7168, D)
        self.pick = m.part(8192, TT, SLOTS)
        self.weigh = m.part(8320, TT, P)
        self.weighT = m.part(8576, T)
        self.xe = m.part(8832, KT, SLOTS)
        self.g = m.part(9344, 512)
        self.sig = m.part(9856, 512)
        self.u = m.part(10368, 512)
        self.h = m.part(10880, 512)
        self.hT = m.part(2048, 4, 2, SLOTS)
        self.ye = m.part(2560, 512)
        self.select = m.part(3072, SLOTS)


def route(nc, d, m, M, banks, ring):
    x = Experts(m)
    n0 = m.norms
    m.norms += TT
    turn = banks.plan([("t", i) for i in range(4)], [4, 5, 6, 7])
    small = banks.plan([("logit", t) for t in range(TT)] + [("place", t) for t in range(TT)] + ["total", "gT"], [0, 1, 2, 3])
    with nc.Block() as block:

        @block.sync
        def _(sp):
            load_rows(sp, M, m, [d["lns"][i:i + 1, :] for i in range(4)])
            for dst, src in ((x.router, d["router_w"]), (x.router_b[0:1, :], d["router_b"]), (x.b_gate[0:NE, :], d["b_gate"]),
                             (x.b_up[0:NE, :], d["b_up"]), (x.b_down[0:NE, :], d["b_down"])):
                sp.dma_start(dst, src).then_inc(M("router_in"), 16)
            ring.load(sp, ring.at["moe"] + NSLOT)

        @block.tensor
        def _(pe):
            ident = m.const("ident")
            for i in range(4):
                t, half = i // 2, i % 2
                where = turn["t", i]
                banks.wait_free(pe, where)
                pe.wait_ge(M("y_ready"), t + 1)
                for k in range(4):
                    c = (4 * half + k) * P
                    last = nc.tensor.transpose(m.ps[:, where[0], k * P:(k + 1) * P], m.X[:, t, c:c + P], ident)
                banks.fill(last, where)
            pe.wait_ge(M("router_in"), 5 * 16)
            pe.wait_ge(M("yT_ready"), 4)
            for t in range(TT):
                where = small["logit", t]
                banks.wait_free(pe, where)
                pairs = [(x.yT[:, k, t * P:(t + 1) * P], x.router[:, k, :]) for k in range(KT)]
                pairs.append((m.const("ones")[0:1, :], x.router_b[0:1, :]))
                banks.fill(products(nc, m.ps[:, where[0], 0:NE], pairs), where)
            pe.wait_ge(M("gates_known"), TT)
            for t in range(TT):
                where = small["place", t]
                banks.wait_free(pe, where)
                pairs = [(m.const("ones"), x.chosen[:, s, :]) for s in range(t)] + [(m.const("upto"), x.chosen[:, t, :])]
                banks.fill(products(nc, m.ps[:, where[0], 0:NE], pairs), where)
            where = small["total"]
            banks.wait_free(pe, where)
            banks.fill(products(nc, m.ps[0:1, where[0], 0:NE], [(m.const("ones")[:, 0:1], x.chosen[:, t, :]) for t in range(TT)]), where)
            where = small["gT"]
            banks.wait_free(pe, where)
            for t in range(TT):
                last = nc.tensor.transpose(m.ps[0:NE, where[0], t * P:(t + 1) * P], x.gates[:, t, :], ident)
            banks.fill(last, where)

        @block.scalar
        def _(act):
            for t in range(TT):
                norm_act(nc, act, m, M, n0 + t + 1)
            for i in range(4):
                t, half = i // 2, i % 2
                where = turn["t", i]
                banks.wait_full(act, where)
                ins = nc.scalar.activation(x.yT[:, 4 * half:4 * half + 4, t * P:(t + 1) * P],
                                           m.ps[:, where[0], :].rearrange("p (k c) -> p k c", k=4), ACT.Copy)
                banks.free_chained(act, ins, where)
                act.sem_inc(M("yT_ready"), 1)
            for t in range(TT):
                act.wait_ge(M("top_ready"), t + 1)
                nc.scalar.activation(x.exp[:, 0:TOPK], x.exp[:, 0:TOPK], ACT.Exp).then_inc(M("top_exp"), 1)

        @block.vector
        def _(dve):
            step = Chain(M, dve, "dve_step")
            dve.wait_ge(M("rows_in"), m.rows_sent)
            for t in range(TT):
                X = m.X[:, t, :]
                norm_dve(nc, dve, step, m, M, X, n0 + t + 1)
                step(nc.vector.tensor_tensor(X, X, row(m, 0), ALU.mult))
                step(nc.vector.tensor_tensor(X, X, row(m, 1), ALU.add), "y_ready")
            iota = m.const("iota")[:, 0:NE]
            for t in range(TT):
                where = small["logit", t]
                banks.wait_full(dve, where)
                banks.free_chained(dve, nc.vector.tensor_copy(x.logits[:, t, :], m.ps[:, where[0], 0:NE]), where)
                top = x.top[:, t, :]
                step(nc.vector.max(top, x.logits[:, t, :]))
                step(nc.vector.max_index(x.top_at, top, x.logits[:, t, :]))
                step(nc.vector.tensor_copy(x.top_i[:, t, :], x.top_at))
                step(nc.vector.tensor_scalar(x.exp[:, 0:TOPK], top[:, 0:TOPK], top[:, 0:1], None, ALU.subtract), "top_ready")
                dve.wait_ge(M("top_exp"), t + 1)
                step(nc.vector.tensor_reduce(x.exp[:, 4:5], x.exp[:, 0:TOPK], axis=AX.X, op=ALU.add))
                step(nc.vector.reciprocal(x.exp[:, 5:6], x.exp[:, 4:5]))
                step(nc.vector.tensor_scalar(x.exp[:, 0:TOPK], x.exp[:, 0:TOPK], x.exp[:, 5:6], None, ALU.mult))
                for k in range(TOPK):
                    at, gate = x.top_i[:, t, k:k + 1], x.exp[:, k:k + 1]
                    if k == 0:
                        step(nc.vector.tensor_scalar(x.gates[:, t, :], iota, at, gate, ALU.is_equal, ALU.mult))
                        step(nc.vector.tensor_scalar(x.chosen[:, t, :], iota, at, None, ALU.is_equal))
                    else:
                        step(nc.vector.tensor_scalar(x.onehot, iota, at, gate, ALU.is_equal, ALU.mult))
                        step(nc.vector.tensor_tensor(x.gates[:, t, :], x.gates[:, t, :], x.onehot, ALU.add))
                        step(nc.vector.scalar_tensor_tensor(out=x.chosen[:, t, :], in0=iota, scalar=at, in1=x.chosen[:, t, :],
                                                            op0=ALU.is_equal, op1=ALU.add))
                dve.sem_inc(M("gates_known"), 1)
            step(nc.vector.memset(x.place, -1.0))
            for t in range(TT):
                where = small["place", t]
                banks.wait_full(dve, where)
                ins = nc.vector.tensor_tensor(x.place[:, t, 0:NE], m.ps[:, where[0], 0:NE], x.chosen[:, t, :], ALU.mult)
                banks.free_chained(dve, ins, where)
                step(nc.vector.tensor_scalar(x.place[:, t, 0:NE], x.place[:, t, 0:NE], -1.0, None, ALU.add))
            where = small["total"]
            banks.wait_full(dve, where)
            ins = nc.vector.tensor_reduce(x.total[0:1, NE:NE + 1], m.ps[0:1, where[0], 0:NE], axis=AX.X, op=ALU.max)
            banks.free_chained(dve, ins, where)
            step(nc.vector.tensor_copy(m.count[0:1, 0:1], x.total[0:1, NE:NE + 1]))
            where = small["gT"]
            banks.wait_full(dve, where)
            banks.free_chained(dve, nc.vector.tensor_copy(x.gatesT[0:NE, :], m.ps[0:NE, where[0], 0:T]), where)


def moe(nc, d, m, M, banks, ring):
    x = Experts(m)
    ch0 = ring.at["moe"]
    slot = [(ch0 + c) % NSLOT for c in range(PER_EXPERT)]
    nth = [(ch0 + c) // NSLOT for c in range(PER_EXPERT)]
    w = [m.ring[:, s, :].rearrange("p (k j) -> p k j", k=KT // 2) for s in slot]
    n0 = m.norms
    m.norms += TT
    load_base = [f"chunk_in{s}" for s in slot]
    used_base = [f"chunk_used{s}" for s in slot]
    more = range(1, PASSES)

    def name(base, p):
        return base if p == 0 else base + "_more"

    def at(p, e, base=0):
        return e + base if p == 0 else (p - 1) * NE + e + base

    def primed(eng, p, *names):
        if p < 2:
            for n in names:
                eng.sem_inc(M(name(n, p)), 1)

    def picked(p, e, base=0):
        return e + base if p == 0 else (p - 1) * (NE + 1) + e + base

    def overflow(eng, body):
        count = eng.value_load(m.count[0:1, 0:1], min_val=0, max_val=T)
        with eng.If(count > SLOTS):
            for p in more:
                body(p)

    with nc.Block() as block:

        @block.sync
        def _(sp):
            with sp.Fori(1, NE) as e:
                for c in range(PER_EXPERT):
                    sp.wait_ge(M(used_base[c]), e + nth[c])
                    sp.dma_start(m.ring[:, slot[c], :], d["moe"][bass.ds(e, 1), c, :, :].rearrange("e p j -> (e p) j"))\
                        .then_inc(M(load_base[c]), 16)
            ring.sent = ch0 + PER_EXPERT * NE

            def body(p):
                if p == 1:
                    for c in range(PER_EXPERT):
                        sp.wait_ge(M(used_base[c]), NE + nth[c])
                with sp.Fori(0, NE) as e:
                    for c in range(PER_EXPERT):
                        sp.wait_ge(M(f"more_used{c}"), e + ((p - 1) * NE + 1))
                        sp.dma_start(m.ring[:, slot[c], :], d["moe"][bass.ds(e, 1), c, :, :].rearrange("e p j -> (e p) j"))\
                            .then_inc(M(f"more_in{c}"), 16)
                if p == PASSES - 1:
                    for c in range(PER_EXPERT):
                        sp.wait_ge(M(f"more_used{c}"), (PASSES - 1) * NE + 1)

            overflow(sp, body)
            ring.load(sp, ch0 + PER_EXPERT * NE + NSLOT)

        @block.tensor
        def _(pe):
            acc = [m.ps[:, 2 * t + n, :] for t in range(TT) for n in range(2)]
            for i in range(4):
                t, n = i // 2, i % 2
                nc.tensor.matmul(acc[i], x.gatesT[0:NE, t * P:(t + 1) * P], x.b_down[0:NE, n * 512:(n + 1) * 512],
                                 start=True, stop=False, skip_group_check=True)

            def gather(p, count):
                pe.wait_ge(M(name("pick_ready", p)), count)
                for k in range(KT):
                    for t in range(TT):
                        last = nc.tensor.matmul(m.ps[:, 7, k * SLOTS:(k + 1) * SLOTS], m.X[:, t, k * P:(k + 1) * P],
                                                x.pick[:, t, :], start=t == 0, stop=t == TT - 1)
                last.then_inc(M(name("gather_done", p)), 1)

            def scatter():
                for n in range(2):
                    rows = slice(n * SLOTS, (n + 1) * SLOTS)
                    for t in range(TT):
                        last = nc.tensor.matmul(acc[2 * t + n], x.weighT[rows, t * P:(t + 1) * P], x.ye[rows, :],
                                                start=False, stop=False, skip_group_check=True)
                return last

            def halves(bank, c, lhs, first):
                for k in range(KT // 2):
                    for n in range(2):
                        last = nc.tensor.matmul(m.ps[n * SLOTS:(n + 1) * SLOTS, bank, :], lhs(k + KT // 2 * (c % 2), n),
                                                w[c][:, k, n * 512:(n + 1) * 512],
                                                start=first and k == 0, stop=c % 2 == 1 and k == KT // 2 - 1, skip_group_check=True)
                return last

            def one_pass(p):
                arrived = lambda c, e: pe.wait_ge(M(load_base[c] if p == 0 else f"more_in{c}"),
                                                  16 * (e + nth[c] + 1) if p == 0 else 16 * (at(p, e) + 1))
                used = lambda ins, c: ins.then_inc(M(used_base[c] if p == 0 else f"more_used{c}"), 1)
                primed(pe, p, "added", "weigh_turned")
                if p == 1:
                    for c in range(PER_EXPERT):
                        pe.sem_inc(M(f"more_used{c}"), 1)
                gather(p, picked(p, 0, 1))
                with pe.Fori(0, NE) as e:
                    pe.wait_ge(M(name("select_ready", p)), picked(p, e, 1))
                    pe.wait_ge(M(name("xe_ready", p)), picked(p, e, 1))
                    for c in range(4):
                        bank = 4 + c // 2
                        if c % 2 == 0:
                            pe.wait_ge(M(name(("weighT_ready", "h_ready")[c // 2], p)), at(p, e, 1))
                            for n in range(2):
                                nc.tensor.matmul(m.ps[n * SLOTS:(n + 1) * SLOTS, bank, :],
                                                 x.select[0:NE, :],
                                                 (x.b_gate, x.b_up)[c // 2][0:NE, n * 512:(n + 1) * 512],
                                                 start=True, stop=False, skip_group_check=True)
                        arrived(c, e)
                        used(halves(bank, c, lambda k, n: x.xe[:, k, :], False), c)
                    gather(p, picked(p, e, 2))
                    pe.wait_ge(M(name("h_ready", p)), at(p, e, 2))
                    pe.wait_ge(M(name("ye_ready", p)), at(p, e, 1))
                    for j in range(4):
                        last = nc.tensor.transpose(m.ps[:, 6, j * P:(j + 1) * P], x.h[:, j * P:(j + 1) * P], m.const("ident"))
                    last.then_inc(M(name("h_turned", p)), 1)
                    last = scatter()
                    last.then_inc(M(name("added", p)), 1)
                    pe.wait_ge(M(name("weigh_ready", p)), at(p, e, 1))
                    for t in range(TT):
                        last = nc.tensor.matmul(m.ps[:, 4, t * P:(t + 1) * P], x.weigh[:, t, :], m.const("ident"), start=True, stop=True)
                    last.then_inc(M(name("weigh_turned", p)), 1)
                    pe.wait_ge(M(name("hT_ready", p)), at(p, e, 1))
                    for c in (4, 5):
                        arrived(c, e)
                        used(halves(6, c, lambda k, n: x.hT[:, k % 4, k // 4, :], c == 4), c)
                pe.wait_ge(M(name("weighT_ready", p)), at(p, NE, 1))
                pe.wait_ge(M(name("ye_ready", p)), at(p, NE, 1))

            pe.wait_ge(M("scatter_clear"), 1)
            one_pass(0)
            overflow(pe, one_pass)
            scatter()
            for i in range(4):
                last = nc.tensor.matmul(acc[i], m.const("zero"), x.xe.rearrange("p a b -> p (a b)"), start=False, stop=True, skip_group_check=True)
            last.then_inc(M("sums_done"), 1)

        @block.scalar
        def _(act):
            def xe_out(p, count):
                act.wait_ge(M(name("gather_done", p)), count)
                nc.scalar.activation(x.xe.rearrange("p a b -> p (a b)"), m.ps[:, 7, :], ACT.Copy).then_inc(M(name("xe_ready", p)), 1)

            def one_pass(p):
                primed(act, p, "weighT_ready", "ye_ready")
                xe_out(p, picked(p, 0, 1))
                with act.Fori(0, NE) as e:
                    act.wait_ge(M(name("g_ready", p)), at(p, e, 1))
                    nc.scalar.activation(x.sig, x.g, ACT.Sigmoid, scale=SW_ALPHA).then_inc(M(name("sig_ready", p)), 1)
                    xe_out(p, picked(p, e, 2))
                    act.wait_ge(M(name("h_turned", p)), at(p, e, 1))
                    nc.scalar.activation(x.hT.rearrange("p a b c -> p (a b c)"), m.ps[:, 6, :], ACT.Copy).then_inc(M(name("hT_ready", p)), 1)
                    act.wait_ge(M(name("added", p)), at(p, e, 2))
                    act.wait_ge(M(name("weigh_turned", p)), at(p, e, 2))
                    nc.scalar.activation(x.weighT, m.ps[:, 4, 0:T], ACT.Copy).then_inc(M(name("weighT_ready", p)), 1)
                    act.wait_ge(M(used_base[5] if p == 0 else "more_used5"), e + nth[5] + 1 if p == 0 else at(p, e, 2))
                    nc.scalar.activation(x.ye, m.ps[:, 6, :], ACT.Copy).then_inc(M(name("ye_ready", p)), 1)

            one_pass(0)
            overflow(act, one_pass)
            for t in range(TT):
                norm_act(nc, act, m, M, n0 + t + 1)

        @block.vector
        def _(dve):
            step = Chain(M, dve, "dve_step")
            iota = m.const("iota")
            step(nc.vector.memset(x.ye, 0.0))
            step(nc.vector.memset(x.weighT, 0.0), "scatter_clear")

            def pick(p, e):
                for t in range(TT):
                    last = nc.vector.tensor_scalar(x.pick[:, t, :], iota[:, 0:SLOTS], x.place[:, t, bass.ds(e, 1)], None, ALU.is_equal)
                last.then_inc(M(name("pick_ready", p)), 1)

            def select(p, e):
                nc.vector.tensor_copy(x.select[0:NE, :], m.const("ident")[0:NE, bass.ds(e, 1)].to_broadcast([NE, SLOTS]))\
                    .then_inc(M(name("select_ready", p)), 1)

            def weigh(p, e):
                for t in range(TT):
                    last = nc.vector.tensor_scalar(x.weigh[:, t, :], iota, x.place[:, t, bass.ds(e, 1)], x.gates[:, t, bass.ds(e, 1)],
                                                   ALU.is_equal, ALU.mult)
                last.then_inc(M(name("weigh_ready", p)), 1)

            def one_pass(p):
                if p:
                    before = p - 1
                    dve.wait_ge(M(name("weigh_ready", before)), at(before, NE))
                    dve.wait_ge(M(name("weigh_turned", before)), at(before, NE, 1))
                    dve.wait_ge(M(name("pick_ready", before)), picked(before, NE, 1))
                    dve.wait_ge(M(name("gather_done", before)), picked(before, NE, 1))
                    nc.vector.tensor_scalar(x.place, x.place, -float(SLOTS), None, ALU.add).then_inc(M("shifted_more"), 1)
                    dve.wait_ge(M("shifted_more"), p)
                primed(dve, p, "h_ready")
                pick(p, 0)
                select(p, 0)
                with dve.Fori(0, NE) as e:
                    dve.wait_ge(M(name("gather_done", p)), picked(p, e, 1))
                    pick(p, e + 1)
                    dve.wait_ge(M(used_base[1] if p == 0 else "more_used1"), e + nth[1] + 1 if p == 0 else at(p, e, 2))
                    dve.wait_ge(M(name("h_ready", p)), at(p, e, 1))
                    nc.vector.tensor_scalar(x.g, m.ps[:, 4, :], LIMIT, None, ALU.min).then_inc(M(name("g_ready", p)), 1)
                    dve.wait_ge(M(name("weigh_turned", p)), at(p, e, 1))
                    weigh(p, e)
                    dve.wait_ge(M(name("g_ready", p)), at(p, e, 1))
                    dve.wait_ge(M(name("sig_ready", p)), at(p, e, 1))
                    nc.vector.tensor_tensor(x.g, x.g, x.sig, ALU.mult).then_inc(M(name("gs_ready", p)), 1)
                    dve.wait_ge(M(used_base[3] if p == 0 else "more_used3"), e + nth[3] + 1 if p == 0 else at(p, e, 2))
                    nc.vector.tensor_scalar(x.u, m.ps[:, 5, :], LIMIT, -LIMIT, ALU.min, ALU.max).then_inc(M(name("u_ready", p)), 1)
                    dve.wait_ge(M(name("gs_ready", p)), at(p, e, 1))
                    dve.wait_ge(M(name("u_ready", p)), at(p, e, 1))
                    nc.vector.scalar_tensor_tensor(out=x.h, in0=x.u, scalar=1.0, in1=x.g, op0=ALU.add, op1=ALU.mult)\
                        .then_inc(M(name("h_ready", p)), 1)
                    select(p, e + 1)

            one_pass(0)
            overflow(dve, one_pass)
            dve.wait_ge(M("sums_done"), 1)
            for t in range(TT):
                X = m.X[:, t, :]
                step(nc.vector.scalar_tensor_tensor(out=X, in0=X, scalar=ALPHA1,
                                                    in1=m.ps[:, 2 * t:2 * t + 2, :].rearrange("p a b -> p (a b)"), op0=ALU.mult, op1=ALU.add))
                norm_dve(nc, dve, step, m, M, X, n0 + t + 1)
                step(nc.vector.tensor_tensor(X, X, row(m, 2), ALU.mult))
                step(nc.vector.tensor_tensor(X, X, row(m, 3), ALU.add))



SHIFT1, SCALE1, GATE1, SHIFT2, SCALE2, GATE2 = range(6)


def modulations(nc, d, m, M, banks, ring):
    bias = m.part(0, 2, 6 * D)
    c = m.H[:, 0, 0:KT * 2].rearrange("p (k s) -> p k s", k=KT)
    sc = m.H[:, 0, 16:16 + KT * 2].rearrange("p (k s) -> p k s", k=KT)
    stage = m.H[0:2, 1:4, :].rearrange("p a (b c) -> p (a b) c", b=2)
    n_stage = 6
    groups = [(layer, n) for layer in range(2) for n in range(12)]
    plan = banks.plan(groups, [0, 1, 2, 3])
    with nc.Block() as block:

        @block.sync
        def _(sp):
            sp.dma_start(c, d["c"]).then_inc(M("c_in"), 16)
            sp.dma_start(bias[0:1, :, :], d["b_mod"].rearrange("(o l) n -> o l n", o=1)).then_inc(M("c_in"), 16)
            sp.dma_start(m.X[:, 2:4, :], d["ctx"].rearrange("(t p) c -> p t c", p=P)).then_inc(M("ctx_in"), 16)
            for layer in range(2):
                for n in range(12):
                    i = 12 * layer + n
                    ring.load(sp, ring.at["w_mod0"] + i + NSLOT)
                    sp.wait_ge(M("mod_staged"), i + 1)
                    sp.dma_start(d["mod"][layer, :, n * 512:(n + 1) * 512], stage[:, i % n_stage, :]).then_inc(M(f"mod_out{i % n_stage}"), 16)
            for i in range(n_stage):
                sp.wait_ge(M(f"mod_out{i}"), 16 * (len(groups) // n_stage))
            sp.wait_ge(M("ctx_in"), 16)

        @block.tensor
        def _(pe):
            pe.wait_ge(M("c_in"), 32)
            pe.wait_ge(M("silu_c"), 1)
            for layer, n in groups:
                w = ring.wait(pe, "w_mod0", 12 * layer + n)
                where = plan[layer, n]
                banks.wait_free(pe, where)
                pairs = [(m.const("ones")[0:1, 0:2], bias[0:1, layer, n * 512:(n + 1) * 512])]
                pairs += [(sc[:, k, :], w[:, k, :]) for k in range(KT)]
                banks.fill(products(nc, m.ps[0:2, where[0], :], pairs), where)
                pe.wait_ge(M(f"bank_full{where[0]}"), where[1] + 1)
                pe.sem_inc(M(f"chunk_used{(ring.at['w_mod0'] + 12 * layer + n) % NSLOT}"), 1)

        @block.scalar
        def _(act):
            act.wait_ge(M("c_in"), 32)
            nc.scalar.activation(sc, c, ACT.Silu).then_inc(M("silu_c"), 1)
            for i, (layer, n) in enumerate(groups):
                where = plan[layer, n]
                banks.wait_full(act, where)
                if i >= n_stage:
                    act.wait_ge(M(f"mod_out{i % n_stage}"), 16 * (i // n_stage))
                ins = nc.scalar.activation(stage[:, i % n_stage, :], m.ps[0:2, where[0], :], ACT.Copy,
                                           bias=1.0 if n // 2 in (SCALE1, SCALE2) else 0.0)
                banks.free_chained(act, ins, where)
                act.sem_inc(M("mod_staged"), 1)


def mod_row(d, layer, stream, which):
    return d["mod"][layer, stream:stream + 1, which * D:(which + 1) * D]


def modulate(nc, d, m, M, banks, ring, layer, scale, shift, tiles):
    hT = m.part(0, KT, tiles * P)
    plan = banks.plan([(t, n) for t in range(tiles) for n in range(2)], list(range(8)))
    base = M.n.get("h_ready_now", 0)
    with nc.Block() as block:

        @block.sync
        def _(sp):
            load_rows(sp, M, m, [mod_row(d, layer, s, w) for s in range(tiles // 2) for w in (scale, shift)])
            if (layer, scale) == (1, SCALE1):
                ring.load(sp, ring.at["b_w_in"] + NSLOT)

        @block.vector
        def _(dve):
            step = Chain(M, dve, "dve_step")
            dve.wait_ge(M("rows_in"), m.rows_sent)
            for t in range(tiles):
                step(nc.vector.tensor_tensor(m.H[:, t, :], m.X[:, t, :], row(m, 2 * (t // 2)), ALU.mult))
                step(nc.vector.tensor_tensor(m.H[:, t, :], m.H[:, t, :], row(m, 2 * (t // 2) + 1), ALU.add), "h_ready_now")

        @block.tensor
        def _(pe):
            for t in range(tiles):
                pe.wait_ge(M("h_ready_now"), base + t + 1)
                for n in range(2):
                    where = plan[t, n]
                    banks.wait_free(pe, where)
                    for k in range(4):
                        last = nc.tensor.transpose(m.ps[:, where[0], k * P:(k + 1) * P],
                                                   m.H[:, t, (4 * n + k) * P:(4 * n + k + 1) * P], m.const("ident"))
                    banks.fill(last, where)

        @block.scalar
        def _(act):
            for t in range(tiles):
                for n in range(2):
                    where = plan[t, n]
                    banks.wait_full(act, where)
                    ins = nc.scalar.activation(hT[:, 4 * n:4 * n + 4, t * P:(t + 1) * P],
                                               m.ps[:, where[0], :].rearrange("p (k c) -> p k c", k=4), ACT.Copy)
                    banks.free(ins, where)


def residual(nc, d, m, M, banks, sums, layer, gate, which, tiles, out=None):
    n0 = m.norms
    m.norms += tiles
    tmp = m.part(4096, D)
    base = M.n.get("x_done", 0)
    with nc.Block() as block:

        @block.sync
        def _(sp):
            load_rows(sp, M, m, [mod_row(d, layer, 0, gate), mod_row(d, layer, tiles // 2 - 1, gate),
                                 d["ln_g"][2 * layer + which:2 * layer + which + 1, :], d["ln_b"][2 * layer + which:2 * layer + which + 1, :]])
            if out is not None:
                view = out.rearrange("a (t p) c -> p (a t) c", p=P)
                for t in range(tiles):
                    sp.wait_ge(M("x_done"), base + t + 1)
                    sp.dma_start(view[:, t, :], m.X[:, t, :]).then_inc(M("stored"), 16)
                sp.wait_ge(M("stored"), 16 * tiles)

        @block.scalar
        def _(act):
            for t in range(tiles):
                norm_act(nc, act, m, M, n0 + t + 1)

        @block.vector
        def _(dve):
            step = Chain(M, dve, "dve_step")
            dve.wait_ge(M("rows_in"), m.rows_sent)
            for t in range(tiles):
                X = m.X[:, t, :]
                for n in range(2):
                    where = sums[t, n]
                    banks.wait_full(dve, where)
                    half = slice(n * 512, (n + 1) * 512)
                    ins = nc.vector.tensor_tensor(tmp[:, half], m.ps[:, where[0], :], row(m, t // 2)[:, half], ALU.mult)
                    banks.free_chained(dve, ins, where)
                step(nc.vector.scalar_tensor_tensor(out=X, in0=X, scalar=ALPHA2, in1=tmp, op0=ALU.mult, op1=ALU.add))
                norm_dve(nc, dve, step, m, M, X, n0 + t + 1)
                step(nc.vector.tensor_tensor(X, X, row(m, 2), ALU.mult))
                step(nc.vector.tensor_tensor(X, X, row(m, 3), ALU.add), "x_done")



def chunk_mlp(nc, d, m, M, banks, ring):
    tiles = 4
    hT = m.part(0, KT, tiles * P)
    u = m.part(4096, tiles, D)
    v = m.part(8192, tiles, D)
    w_s = m.H[:, 0, :].rearrange("p (h c) -> p h c", h=8)
    b_s = m.H[:, 1, 0:8]
    tmp = m.H[:, 2, :]
    n0 = m.norms
    m.norms += tiles
    z = banks.plan([(n, t) for n in range(4) for t in range(tiles)], list(range(8)))
    mixed = banks.plan([(t, n) for t in range(tiles) for n in range(2)], list(range(8)))
    turned = banks.plan([(t, n) for t in range(tiles) for n in range(2)], list(range(8)))
    sums = banks.plan([(t, n) for t in range(tiles) for n in range(2)], list(range(8)))
    with nc.Block() as block:

        @block.sync
        def _(sp):
            sp.dma_start(w_s, d["a_w_s"]).then_inc(M("mlp_in"), 16)
            sp.dma_start(b_s, d["a_b_s"]).then_inc(M("mlp_in"), 16)
            load_rows(sp, M, m, [d["a_norm"][i:i + 1, :] for i in range(2)])
            ring.load(sp, ring.at["w_q0"] + 2 + NSLOT - FREE_SLOTS)

        @block.tensor
        def _(pe):
            for n in range(4):
                w = ring.wait(pe, "a_w_in", n)
                for t in range(tiles):
                    where = z[n, t]
                    banks.wait_free(pe, where)
                    last = products(nc, m.ps[:, where[0], :], [(hT[:, k, t * P:(t + 1) * P], w[:, k, :]) for k in range(KT)])
                    banks.fill(last, where)
                pe.wait_ge(M(f"bank_full{where[0]}"), where[1] + 1)
                pe.sem_inc(M(f"chunk_used{(ring.at['a_w_in'] + n) % NSLOT}"), 1)
            pe.wait_ge(M("mlp_in"), 32)
            for t in range(tiles):
                pe.wait_ge(M("v_normed"), t + 1)
                for n in range(2):
                    where = mixed[t, n]
                    banks.wait_free(pe, where)
                    for k in range(4):
                        head = 4 * n + k
                        last = nc.tensor.matmul(m.ps[:, where[0], k * P:(k + 1) * P], w_s[:, head, :],
                                                v[:, t, head * P:(head + 1) * P], start=True, stop=True)
                    banks.fill(last, where)
            for t in range(tiles):
                pe.wait_ge(M("gated_ready"), t + 1)
                for n in range(2):
                    where = turned[t, n]
                    banks.wait_free(pe, where)
                    for k in range(4):
                        c = (4 * n + k) * P
                        last = nc.tensor.transpose(m.ps[:, where[0], k * P:(k + 1) * P], u[:, t, c:c + P], m.const("ident"))
                    banks.fill(last, where)
            pe.wait_ge(M("gatedT_ready"), 2 * tiles)
            for n in range(2):
                w = ring.wait(pe, "a_w_out", n)
                for t in range(tiles):
                    where = sums[t, n]
                    banks.wait_free(pe, where)
                    last = products(nc, m.ps[:, where[0], :], [(hT[:, k, t * P:(t + 1) * P], w[:, k, :]) for k in range(KT)])
                    banks.fill(last, where)
                pe.wait_ge(M(f"bank_full{where[0]}"), where[1] + 1)
                pe.sem_inc(M(f"chunk_used{(ring.at['a_w_out'] + n) % NSLOT}"), 1)

        @block.scalar
        def _(act):
            def gelu(n, t):
                where = z[n, t]
                banks.wait_full(act, where)
                dst = (v if n < 2 else u)[:, t, (n % 2) * 512:(n % 2) * 512 + 512]
                banks.free_chained(act, nc.scalar.activation(dst, m.ps[:, where[0], :], ACT.Gelu_apprx_tanh), where)
                act.sem_inc(M("z_ready"), 1)

            for n in range(2):
                for t in range(tiles):
                    gelu(n, t)
            for t in range(tiles):
                norm_act(nc, act, m, M, n0 + t + 1)
            for n in range(2, 4):
                for t in range(tiles):
                    gelu(n, t)
            for t in range(tiles):
                for n in range(2):
                    where = turned[t, n]
                    banks.wait_full(act, where)
                    ins = nc.scalar.activation(hT[:, 4 * n:4 * n + 4, t * P:(t + 1) * P],
                                               m.ps[:, where[0], :].rearrange("p (k c) -> p k c", k=4), ACT.Copy)
                    banks.free_chained(act, ins, where)
                    act.sem_inc(M("gatedT_ready"), 1)

        @block.vector
        def _(dve):
            step = Chain(M, dve, "dve_step")
            dve.wait_ge(M("rows_in"), m.rows_sent)
            dve.wait_ge(M("mlp_in"), 32)
            for t in range(tiles):
                dve.wait_ge(M("z_ready"), tiles + t + 1)
                V = v[:, t, :]
                norm_dve(nc, dve, step, m, M, V, n0 + t + 1)
                step(nc.vector.tensor_tensor(V, V, row(m, 0), ALU.mult))
                step(nc.vector.tensor_tensor(V, V, row(m, 1), ALU.add), "v_normed")
            for t in range(tiles):
                dve.wait_ge(M("z_ready"), 3 * tiles + t + 1)
                for n in range(2):
                    where = mixed[t, n]
                    banks.wait_full(dve, where)
                    half = slice(n * 512, (n + 1) * 512)
                    bias = b_s[:, 4 * n:4 * n + 4].rearrange("p (h c) -> p h c", c=1).to_broadcast([P, 4, P])
                    ins = nc.vector.tensor_tensor(tmp[:, half].rearrange("p (h c) -> p h c", h=4),
                                                  m.ps[:, where[0], :].rearrange("p (h c) -> p h c", h=4), bias, ALU.add)
                    banks.free_chained(dve, ins, where)
                step(nc.vector.tensor_tensor(u[:, t, :], u[:, t, :], tmp, ALU.mult), "gated_ready")
    return sums



PAIRS = PH // 2
SCORES = 4 * NKEY
FREE_SLOTS = 3


def pair_scores(m):
    return m.ring[:, NSLOT - FREE_SLOTS:, :].rearrange("p a b -> p (a b)")


def scores(nc, d, m, M, banks, ring, layer, tiles):
    tok = tiles * P
    hT = m.part(0, KT, tok)
    qT = m.part(4096, PH, tok)
    keys = m.part(8192, NKEY)
    out = pair_scores(m)
    q = banks.plan([("q", h) for h in range(PH)], [0, 1, 2, 3])
    groups = [(t, p, i) for t in range(tiles) for i in range(2) for p in range(2)]
    sc = banks.plan(groups, [4, 5, 6, 7])
    L = f"_{layer}"
    with nc.Block() as block:

        @block.sync
        def _(sp):
            sp.dma_start(keys, d["keys"][layer]).then_inc(M("keys_in"), 16)
            ring.load(sp, ring.at[f"w_q{layer}"] + 2 + NSLOT - FREE_SLOTS)

        @block.tensor
        def _(pe):
            for h in range(PH):
                if h % 4 == 0:
                    w = ring.wait(pe, f"w_q{layer}", h // 4)
                where = q["q", h]
                banks.wait_free(pe, where)
                j = h % 4
                last = products(nc, m.ps[:, where[0], 0:tok], [(w[:, k, j * P:(j + 1) * P], hT[:, k, :]) for k in range(KT)])
                banks.fill(last, where)
                if j == 3:
                    pe.wait_ge(M(f"bank_full{where[0]}"), where[1] + 1)
                    pe.sem_inc(M(f"chunk_used{(ring.at[f'w_q{layer}'] + h // 4) % NSLOT}"), 1)
            pe.wait_ge(M("keys_in"), 16 * (layer + 1))
            for t, p, i in groups:
                if t == 0:
                    pe.wait_ge(M("qT_ready" + L), 4 * i + 4)
                where = sc[t, p, i]
                banks.wait_free(pe, where)
                rows_ = slice(p * HD, (p + 1) * HD)
                for k in range(4):
                    last = nc.tensor.matmul(m.ps[:, where[0], k * P:(k + 1) * P], qT[rows_, 4 * i + k, t * P:(t + 1) * P],
                                            keys[rows_, :], start=True, stop=True)
                banks.fill(last, where)

        @block.scalar
        def _(act):
            for h in range(PH):
                where = q["q", h]
                banks.wait_full(act, where)
                banks.free_chained(act, nc.scalar.activation(qT[:, h, :], m.ps[:, where[0], 0:tok], ACT.Copy), where)
                act.sem_inc(M("qT_ready" + L), 1)
            by_pair = out[:, 0:tiles * PAIRS * SCORES].rearrange("p (i a k) -> p i a k", a=2, k=SCORES // 2)
            for t, p, i in groups:
                where = sc[t, p, i]
                banks.wait_full(act, where)
                pair = t * PAIRS + 2 * i
                banks.free(nc.scalar.activation(by_pair[:, pair:pair + 2, p, :], m.ps[:, where[0], :].rearrange("p (i k) -> p i k", i=2),
                                                ACT.Copy), where)

        @block.vector
        def _(dve):
            at = tiles * PAIRS * SCORES
            dve.wait_ge(M("qT_ready" + L), PH)
            nc.vector.memset(out[:, at:at + SCORES], 0.0).then_inc(M("list_ended"), 1)
            dve.wait_ge(M("list_ended"), layer + 1)


class Search:

    def __init__(self, nc, dve, m, M, total):
        self.nc, self.dve, self.m, self.M, self.n, self.total = nc, dve, m, M, 0, total
        at = (4 * PAIRS + 1) * SCORES

        def part(size):
            nonlocal at
            at += size
            return pair_scores(m)[:, at - size:at]

        self.s = part(SCORES).rearrange("p (r k) -> p r k", r=4)
        self.rest = part(SCORES).rearrange("p (r k) -> p r k", r=4)
        self.best = part(4 * PK).rearrange("p (r k) -> p r k", r=4)
        self.best_at = part(4 * PK).bitcast(U32).rearrange("p (r k) -> p r k", r=4)
        self.best_i = part(4 * PK).rearrange("p (r k) -> p r k", r=4)
        self.sums = part(2 * PK * PK)
        self.sums_rest = part(2 * PK * PK).rearrange("p (h k) -> p h k", h=2)
        self.top = part(2 * PK).rearrange("p (h k) -> p h k", h=2)
        self.top_at = part(2 * PK).bitcast(U32).rearrange("p (h k) -> p h k", h=2)
        self.part_at = part(2 * PK).bitcast(U32)
        self.parts = part(4 * PK).rearrange("p (n k) -> p n k", n=2)
        self.found = part(4 * PK).rearrange("p (n k) -> p n k", n=2)
        self.hit = part(2 * PK * PK)
        self.z = part(4)

    def each(self, instructions):
        for ins in instructions:
            ins.then_inc(self.M("search_step"), 1)
            self.n += 1
        self.dve.wait_ge(self.M("search_step"), self.total(self.n))

    def stage(self, n, scores_at, exp_count):
        v = self.nc.vector
        s, rest, best, best_at, top, top_at = self.s, self.rest, self.best, self.best_at, self.top, self.top_at
        sums = self.sums.rearrange("p (h k) -> p h k", h=2)
        if n == 0:
            self.each([v.tensor_copy(s.rearrange("p r k -> p (r k)"), pair_scores(self.m)[:, scores_at])])
        elif n == 1:
            self.each([v.max(best[:, r, 0:8], s[:, r, :]) for r in range(4)])
        elif n == 2:
            self.each([v.max_index(best_at[:, r, 0:8], best[:, r, 0:8], s[:, r, :]) for r in range(4)])
        elif n == 3:
            self.each([v.match_replace(out=rest[:, r, :], in_to_replace=best[:, r, 0:8], in_values=s[:, r, :], imm_value=LOWEST)
                       for r in range(4)])
        elif n == 4:
            self.each([v.max(best[:, r, 8:16], rest[:, r, :]) for r in range(4)])
        elif n == 5:
            self.each([v.max_index(best_at[:, r, 8:16], best[:, r, 8:16], rest[:, r, :]) for r in range(4)])
        elif n == 6:
            four = best.rearrange("p (a h) k -> p a h k", a=2)
            first = four[:, 0, :, :].rearrange("p h (k o) -> p h k o", o=1).to_broadcast([P, 2, PK, PK])
            second = four[:, 1, :, :].rearrange("p h (o k) -> p h o k", o=1).to_broadcast([P, 2, PK, PK])
            self.each([v.tensor_copy(self.best_i, best_at),
                       v.tensor_tensor(self.sums.rearrange("p (h a b) -> p h a b", h=2, a=PK), first, second, ALU.add)])
        elif n == 7:
            self.each([v.max(top[:, h, 0:8], sums[:, h, :]) for h in range(2)])
        elif n == 8:
            self.each([v.max_index(top_at[:, h, 0:8], top[:, h, 0:8], sums[:, h, :]) for h in range(2)])
        elif n == 9:
            self.each([v.match_replace(out=self.sums_rest[:, h, :], in_to_replace=top[:, h, 0:8], in_values=sums[:, h, :],
                                       imm_value=LOWEST) for h in range(2)])
        elif n == 10:
            self.each([v.max(top[:, h, 8:16], self.sums_rest[:, h, :]) for h in range(2)])
        elif n == 11:
            self.each([v.max_index(top_at[:, h, 8:16], top[:, h, 8:16], self.sums_rest[:, h, :]) for h in range(2)])
        elif n in (12, 13):
            op, by = ((ALU.logical_shift_right, 4), (ALU.bitwise_and, 15))[n - 12]
            self.each([v.tensor_scalar(self.part_at, top_at.rearrange("p h k -> p (h k)"), by, None, op)])
            self.each([v.tensor_copy(self.parts[:, n - 12, :], self.part_at)])
        elif n in (14, 15):
            half, rows_ = n - 14, 2 * PK
            at = self.parts[:, half, :].rearrange("p (r o) -> p r o", o=1).to_broadcast([P, rows_, PK])
            hit = self.hit.rearrange("p (r j) -> p r j", j=PK)
            iota = self.m.const("iota")[:, 0:PK].rearrange("p (o j) -> p o j", o=1)
            self.each([v.tensor_tensor(hit, at, iota.to_broadcast([P, rows_, PK]), ALU.is_equal)])
            keys_i = self.best_i[:, 2 * half:2 * half + 2, :].rearrange("p h (o k) -> p h o k", o=1).to_broadcast([P, 2, PK, PK])
            hit4 = self.hit.rearrange("p (h k j) -> p h k j", h=2, j=PK)
            self.each([v.tensor_tensor(hit4, hit4, keys_i, ALU.mult)])
            self.each([v.tensor_reduce(self.found[:, half, :], hit, axis=AX.X, op=ALU.add)])
        elif n == 16:
            z3 = self.z.rearrange("p (a h o) -> p a h o", a=2, o=1)
            self.each([v.tensor_copy(self.z[:, 0:2], top[:, :, 0])])
            v.tensor_tensor(top, top, z3[:, 0, :, :].to_broadcast([P, 2, PK]), ALU.subtract).then_inc(self.M("peer_top"), 1)
        elif n == 17:
            self.dve.wait_ge(self.M("peer_exp"), exp_count)
            self.each([v.tensor_reduce(self.z[:, 0:2], top, axis=AX.X, op=ALU.add)])
            self.each([v.reciprocal(self.z[:, 2:4], self.z[:, 0:2])])
        elif n == 18:
            z3 = self.z.rearrange("p (a h o) -> p a h o", a=2, o=1)
            self.each([v.tensor_tensor(self.m.wts[:, 2 * PK:4 * PK].rearrange("p (h k) -> p h k", h=2), top,
                                       z3[:, 1, :, :].to_broadcast([P, 2, PK]), ALU.mult)])
        elif n == 19:
            self.each([v.scalar_tensor_tensor(out=self.m.idx, in0=self.found[:, 0, :], scalar=float(NKEY), in1=self.found[:, 1, :],
                                              op0=ALU.mult, op1=ALU.add)])


SEARCH_END = 19
SEARCH_STEPS = 1 + 4 * 5 + 2 + 2 * 5 + 4 + 6 + 1 + 2 + 1 + 1


BUFS, LOT = 8, 4


def peer(nc, d, m, M, banks, layer, tiles, first):
    u_buf = [m.part(b * D, D) for b in range(BUFS)]
    v_buf = [m.part((BUFS + b) * D, D) for b in range(BUFS)]
    cur = [m.cur_idx[:, 0:PK], m.cur_idx[:, PK:2 * PK]]
    sums = banks.plan([(t, n) for t in range(tiles) for n in range(2)], list(range(2 * tiles)))
    pairs = PH // 2
    slots = PH * PK

    with nc.Block() as block:

        @block.gpsimd
        def _(pool):
            for t in range(tiles):
                with pool.Fori(0, pairs) as i:
                    for hh in range(2):
                        done = i * 2 * PK + ((first + t) * slots + hh * PK)
                        pool.wait_ge(M("idx_ready"), i * 2 + ((first + t) * PH + layer + hh + 1))
                        for lot in range(PK // LOT):
                            for table, bufs, free, arrived in ((d[f"u{layer}"], u_buf, "u_free", "u_in"),
                                                               (d[f"v{layer}"], v_buf, "v_free", "v_in")):
                                for j in range(LOT):
                                    k = lot * LOT + j
                                    b = k % BUFS
                                    pool.wait_ge(M(free), done + k + 1)
                                    pool.sem_inc(M("gather_ticket"), 1)
                                    pool.indirect_dma_start(bufs[b], None, table, bass.IndirectOffsetOnAxis(cur[hh][:, k:k + 1], 0))\
                                        .then_inc(M(f"{arrived}{b}"), 16)

        @block.vector
        def _(dve):
            def arrivals(t, i, hh, k):
                return 16 * (((first + t) * slots + hh * PK + k) // BUFS + 1) + i * (16 * 2 * PK // BUFS)

            if first == 0:
                dve.sem_inc(M("u_free"), BUFS)
            searched = first * PAIRS + layer
            head = Search(nc, dve, m, M, lambda n: searched * SEARCH_STEPS + n)
            for n in range(SEARCH_END + 1):
                head.stage(n, slice(0, SCORES), searched + 1)
            nc.vector.tensor_copy(m.wts[:, 0:2 * PK], m.wts[:, 2 * PK:4 * PK]).then_inc(M("wts_moved"), 1)
            nc.vector.tensor_copy(cur[0], m.idx[:, 0:PK]).then_inc(M("idx_ready"), 1)
            dve.wait_ge(M("wts_moved"), searched + 1)
            for t in range(tiles):
                with dve.Fori(0, pairs) as i:
                    done = searched + t * PAIRS + 1
                    following = Search(nc, dve, m, M, lambda n: i * SEARCH_STEPS + (done * SEARCH_STEPS + n))

                    def stage(n):
                        following.stage(n, bass.ds(i * SCORES + (t * PAIRS + 1) * SCORES, SCORES), i + (done + 1))

                    for hh in range(2):
                        for k in range(PK):
                            b = k % BUFS
                            dve.wait_ge(M(f"u_in{b}"), arrivals(t, i, hh, k))
                            nc.vector.scalar_tensor_tensor(out=u_buf[b], in0=u_buf[b], scalar=1.0, in1=m.H[:, t, :], op0=ALU.mult,
                                                           op1=ALU.mult, accum_out=m.dots[:, k:k + 1]).then_inc(M("u_free"), 1)
                            if k % LOT == LOT - 1:
                                lots = ((first + t) * slots + hh * PK + k) // LOT + i * (2 * PK // LOT)
                                dve.wait_ge(M("gelu_done"), lots + 1)
                                a = m.act[:, k + 1 - LOT:k + 1]
                                nc.vector.tensor_tensor(a, a, m.wts[:, hh * PK + k + 1 - LOT:hh * PK + k + 1], ALU.mult)\
                                    .then_inc(M("act_ready"), 1)
                            if hh == 0:
                                stage(k)
                            elif k < LOT:
                                stage(PK + k)
                            if k == LOT - 1:
                                dve.wait_ge(M("v_free"), i * 2 * PK + ((first + t) * slots + hh * PK + BUFS))
                                nc.vector.tensor_copy(cur[1 - hh], m.idx[:, (1 - hh) * PK:(2 - hh) * PK]).then_inc(M("idx_ready"), 1)
                    dve.wait_ge(M("act_ready"), i * (2 * PK // LOT) + ((first + t + 1) * slots // LOT - (pairs - 1) * 2 * PK // LOT))
                    nc.vector.tensor_copy(m.wts[:, 0:2 * PK], m.wts[:, 2 * PK:4 * PK]).then_inc(M("wts_moved"), 1)
                    dve.wait_ge(M("wts_moved"), i + (done + 1))

        @block.scalar
        def _(act):
            searched = first * PAIRS + layer
            top = Search(nc, None, m, M, None).top

            def search_exp(count):
                act.wait_ge(M("peer_top"), count)
                nc.scalar.activation(top, top, ACT.Exp).then_inc(M("peer_exp"), 1)

            search_exp(searched + 1)
            for t in range(tiles):
                with act.Fori(0, pairs) as i:
                    for hh in range(2):
                        if hh == 1:
                            search_exp(i + (searched + t * PAIRS + 2))
                        for k in range(PK):
                            n = (first + t) * slots + hh * PK + k
                            if k % LOT == 0:
                                act.wait_ge(M("u_free"), i * 2 * PK + (n + LOT + BUFS))
                                a = slice(k, k + LOT)
                                nc.scalar.activation(m.act[:, a], m.dots[:, a], ACT.Gelu_apprx_tanh).then_inc(M("gelu_done"), 1)
                                act.wait_ge(M("act_ready"), i * (2 * PK // LOT) + (n // LOT + 1))
                            act.wait_ge(M("v_free"), i * 2 * PK + (n - 3 + BUFS))
                            nc.scalar.activation(m.diag[k % 4], m.const("ident"), ACT.Copy, scale=m.act[:, k:k + 1]).then_inc(M("diag_ready"), 1)

        @block.tensor
        def _(pe):
            if first == 0:
                pe.sem_inc(M("v_free"), BUFS)
            for t in range(tiles):
                out = [m.ps[:, sums[t, n][0], :] for n in range(2)]
                for n in range(2):
                    banks.wait_free(pe, sums[t, n])
                    nc.tensor.matmul(out[n], m.const("zero"), m.H[:, t, 0:512], start=True, stop=False, skip_group_check=True)
                with pe.Fori(0, pairs) as i:
                    for hh in range(2):
                        for k in range(PK):
                            n_ = (first + t) * slots + hh * PK + k
                            b = k % BUFS
                            pe.wait_ge(M("diag_ready"), i * 2 * PK + (n_ + 1))
                            pe.wait_ge(M(f"v_in{b}"), i * (16 * 2 * PK // BUFS) + 16 * (n_ // BUFS + 1))
                            for n in range(2):
                                last = nc.tensor.matmul(out[n], m.diag[k % 4], v_buf[b][:, n * 512:(n + 1) * 512],
                                                        start=False, stop=False, skip_group_check=True)
                            last.then_inc(M("v_free"), 1)
                for n in range(2):
                    last = nc.tensor.matmul(out[n], m.const("zero"), m.H[:, t, 0:512], start=False, stop=True, skip_group_check=True)
                    banks.fill(last, sums[t, n])
    return sums



def gla(nc, d, m, M, banks, ring):
    tiles = 4
    hT = m.part(0, KT, tiles * P)
    k_end = m.part(0, tiles, 2, GH * DK)
    v = m.part(4096, tiles, D)
    g = m.part(8192, tiles, 2, GH * DK)
    k = m.part(12288, tiles, GH * DK)
    o = m.part(12288, TT, D)
    r = m.part(14336, TT, D)
    yT = m.part(0, KT, T)
    H = m.H[:, :, :].rearrange("p a b -> p (a b)")
    qT = H[:, 0:1024].rearrange("p (h t) -> p h t", h=GH)
    kT = H[:, 1024:2048].rearrange("p (h t) -> p h t", h=GH)
    glT = H[:, 2048:3072].rearrange("p (j t) -> p j t", j=2)
    gn = H[:, 3072:4096]
    X2 = m.X[:, 2:4, :].rearrange("p a b -> p (a b)")
    w_gl = X2[:, 0:256].rearrange("p (k j) -> p k j", k=KT)
    w_gate = X2[:, 256:1280].rearrange("p (j n) -> p j n", j=2)
    E = m.ring[:, 4:6, :].rearrange("p a b -> p (a b)")
    q_in = E[:, 0:2048].rearrange("p (j h t) -> p j h t", j=2, h=GH)
    k_in = E[:, 2048:4096].rearrange("p (j h t) -> p j h t", j=2, h=GH)
    S = E[:, 4096:5120].rearrange("p (j b e) -> p j b e", j=2, b=2)
    att = E[:, 5120:6144].rearrange("p (b c) -> p b c", b=2)
    decay = E[:, 6144:6208]
    ab = E[:, 6208:7232].rearrange("p (b c) -> p b c", b=2)
    low = X2[:, 1280:1792]
    assert [(ring.at["b_w_in"] + n) % NSLOT for n in (4, 5)] == [4, 5]

    n0 = m.norms
    m.norms += TT * GH
    jobs = [("k", 0, t) for t in range(tiles)] + [("kT", 0, i) for i in range(2)]
    jobs += [("v", 1 + n, t) for n in range(2) for t in range(tiles)] + [("qT", 3, i) for i in range(2)]
    jobs += [("r", 4 + n, t) for n in range(2) for t in range(TT)]
    proj = banks.plan([("gl", j) for j in range(2)] + jobs, [0, 1, 2, 3])
    zs = banks.plan([("z", t, j) for t in range(tiles) for j in range(2)], [4, 5])
    cums = banks.plan([("b", j, i) for j in range(2) for i in range(2)], [6, 7])
    sufs = banks.plan([("e", t, j) for t in range(tiles) for j in range(2)] + ["decay"], [6, 7])
    atts = banks.plan([("att", h) for h in range(GH)], [2, 3])
    outs = banks.plan([("o", h) for h in range(GH)], [0, 1])
    steps = [[(2 + c // 2, c % 2) for c in order] + [(c // 2, c % 2) for c in order]
             for order in (range(4), range(3, -1, -1))]
    kv = {}
    for h in range(GH):
        for s in range(7):
            for j in range(2):
                kv[h, s, j] = banks.plan(["x"], [4 + 2 * j + steps[j][s][1]])["x"]
    turned = banks.plan([(t, n) for t in range(TT) for n in range(2)], [4, 5, 6, 7])
    sums = banks.plan([(t, n) for t in range(TT) for n in range(2)], [0, 1, 2, 3])

    with nc.Block() as block:

        @block.sync
        def _(sp):
            sp.dma_start(w_gl, d["b_w_gl"]).then_inc(M("gla_in"), 16)
            sp.dma_start(w_gate[0:RANK + 1, :, :], d["b_w_gate"]).then_inc(M("gla_in"), 16)
            sp.dma_start(gn, d["b_gn_g"].to_broadcast([P, D])).then_inc(M("gla_in"), 16)
            ring.load(sp, ring.at["b_w_out"] + 2 + NSLOT)

        @block.tensor
        def _(pe):
            pe.wait_ge(M("gla_in"), 48)
            for j in range(2):
                where = proj["gl", j]
                banks.wait_free(pe, where)
                banks.fill(products(nc, m.ps[0:RANK, where[0], :], [(w_gl[:, c, j * RANK:(j + 1) * RANK], hT[:, c, :]) for c in range(KT)]), where)
            for n, job in enumerate(jobs):
                kind, chunk, i = job
                w = ring.wait(pe, "b_w_in", chunk)
                where = proj[job]
                banks.wait_free(pe, where)
                if kind in ("kT", "qT"):
                    for half in range(2):
                        col = (2 * i + half) * P
                        last = products(nc, m.ps[:, where[0], half * T:(half + 1) * T],
                                        [(w[:, c, col:col + P], hT[:, c, 0:T]) for c in range(KT)])
                else:
                    last = products(nc, m.ps[:, where[0], :], [(hT[:, c, i * P:(i + 1) * P], w[:, c, :]) for c in range(KT)])
                banks.fill(last, where)
                if n + 1 == len(jobs) or jobs[n + 1][1] != chunk:
                    pe.wait_ge(M(f"bank_full{where[0]}"), where[1] + 1)
                    pe.sem_inc(M(f"chunk_used{(ring.at['b_w_in'] + chunk) % NSLOT}"), 1)
                    if n + 1 == len(jobs):
                        pe.sem_inc(M("projected"), 1)
            pe.wait_ge(M("glT_ready"), 2)
            for t in range(tiles):
                for j in range(2):
                    where = zs["z", t, j]
                    banks.wait_free(pe, where)
                    banks.fill(nc.tensor.matmul(m.ps[:, where[0], :], glT[0:RANK + 1, j, t * P:(t + 1) * P], w_gate[0:RANK + 1, j, :],
                                                start=True, stop=True), where)
            pe.wait_ge(M("g_ready_gla"), tiles * 2)
            for j in range(2):
                for i in range(2):
                    where = cums["b", j, i]
                    banks.wait_free(pe, where)
                    for half in range(2):
                        for t in range(TT):
                            c = (2 * i + half) * DK
                            last = nc.tensor.matmul(m.ps[:, where[0], half * T + t * P:half * T + (t + 1) * P], g[:, t, j, c:c + DK],
                                                    m.const(("fwd", "bwd")[j]), start=True, stop=True)
                    banks.fill(last, where)
            for t in range(tiles):
                for j in range(2):
                    where = sufs["e", t, j]
                    banks.wait_free(pe, where)
                    banks.fill(nc.tensor.matmul(m.ps[:, where[0], :], m.const(("after", "before")[j]), g[:, t, j, :], start=True, stop=True), where)
            where = sufs["decay"]
            banks.wait_free(pe, where)
            for t in range(tiles):
                for j in range(2):
                    for h in range(GH):
                        col = (j * GH + h) * 8 + 2 * t
                        last = nc.tensor.matmul(m.ps[:, where[0], col:col + 2], g[:, t, j, h * DK:(h + 1) * DK], m.const("chunk"),
                                                start=True, stop=True)
            banks.fill(last, where)

            def scores(h):
                where = atts["att", h]
                banks.wait_free(pe, where)
                for j in range(2):
                    for t in range(TT):
                        cols = slice(t * P, (t + 1) * P)
                        last = nc.tensor.matmul(m.ps[:, where[0], (j * TT + t) * P:(j * TT + t + 1) * P], k_in[:, j, h, cols],
                                                q_in[:, j, h, cols], start=True, stop=True)
                banks.fill(last, where)

            pe.wait_ge(M("in_ready"), 8)
            pe.wait_ge(M("k_end_ready"), tiles * 2)
            scores(0)
            for h in range(GH):
                if h + 1 < GH:
                    scores(h + 1)
                e = slice(h * DV, (h + 1) * DV)
                where = outs["o", h]
                banks.wait_free(pe, where)
                pe.wait_ge(M("att_masked"), h + 1)
                for t in range(TT):
                    for j in range(2):
                        nc.tensor.matmul(m.ps[:, where[0], t * DV:(t + 1) * DV], att[:, h % 2, (j * TT + t) * P:(j * TT + t + 1) * P],
                                         v[:, t, e], start=t == 0 and j == 0, stop=False, skip_group_check=True)
                for s in range(8):
                    for j in range(2):
                        t, c = steps[j][s]
                        rows_ = slice(c * CH, (c + 1) * CH)
                        if s >= 4:
                            pe.wait_ge(M(f"state_ready{j}"), 7 * h + s)
                            last = nc.tensor.matmul(m.ps[rows_, where[0], t * DV:(t + 1) * DV],
                                                    q_in[:, j, h, t * P + c * CH:t * P + (c + 1) * CH], S[:, j, (s - 1) % 2, :],
                                                    start=False, stop=s == 7, skip_group_check=True)
                            if s == 7 and j == 1:
                                banks.fill(last, where)
                            else:
                                last.then_inc(M(f"state_read{j}"), 1)
                        if s < 7:
                            there = kv[h, s, j]
                            banks.wait_free(pe, there)
                            banks.fill(nc.tensor.matmul(m.ps[:, there[0], 0:DV], k_end[rows_, t, j, h * DK:(h + 1) * DK], v[rows_, t, e],
                                                        start=True, stop=True), there)
            for t in range(TT):
                pe.wait_ge(M("y_gla"), t + 1)
                for n in range(2):
                    where = turned[t, n]
                    banks.wait_free(pe, where)
                    for c in range(4):
                        at = (4 * n + c) * P
                        last = nc.tensor.transpose(m.ps[:, where[0], c * P:(c + 1) * P], o[:, t, at:at + P], m.const("ident"))
                    banks.fill(last, where)
            pe.wait_ge(M("yT_gla"), 2 * TT)
            for n in range(2):
                w = ring.wait(pe, "b_w_out", n)
                for t in range(TT):
                    where = sums[t, n]
                    banks.wait_free(pe, where)
                    last = products(nc, m.ps[:, where[0], :], [(yT[:, c, t * P:(t + 1) * P], w[:, c, :]) for c in range(KT)])
                    banks.fill(last, where)
                pe.wait_ge(M(f"bank_full{where[0]}"), where[1] + 1)
                pe.sem_inc(M(f"chunk_used{(ring.at['b_w_out'] + n) % NSLOT}"), 1)

        @block.scalar
        def _(act):
            act.wait_ge(M("glT_ones"), 1)
            for j in range(2):
                where = proj["gl", j]
                banks.wait_full(act, where)
                banks.free_chained(act, nc.scalar.activation(glT[0:RANK, j, :], m.ps[0:RANK, where[0], :], ACT.Copy), where)
                act.sem_inc(M("glT_ready"), 1)
            for job in jobs:
                kind, chunk, i = job
                where = proj[job]
                banks.wait_full(act, where)
                src = m.ps[:, where[0], :]
                func, scale = ACT.Copy, 1.0
                if kind == "k":
                    dst = k[:, i, :]
                elif kind == "v":
                    dst = v[:, i, (chunk - 1) * 512:chunk * 512]
                elif kind == "r":
                    dst, func = r[:, i, (chunk - 4) * 512:(chunk - 3) * 512], ACT.Silu
                else:
                    dst = (kT if kind == "kT" else qT)[:, 2 * i:2 * i + 2, :].rearrange("p a b -> p (a b)")
                    scale = 1.0 if kind == "kT" else DK ** -0.5
                banks.free_chained(act, nc.scalar.activation(dst, src, func, scale=scale), where)
                act.sem_inc(M("gla_proj"), 1)
            for n in range(tiles * 2):
                act.wait_ge(M("abs_ready"), n + 1)
                a = ab[:, n % 2, :]
                nc.scalar.activation(a, a, ACT.Exp, scale=-1.0).then_inc(M("act_step"), 1)
                act.wait_ge(M("act_step"), n + 1)
                nc.scalar.activation(a, a, ACT.Ln, bias=1.0).then_inc(M("log_ready"), 1)
            for n, (j, i) in enumerate([(j, i) for j in range(2) for i in range(2)]):
                where = cums["b", j, i]
                banks.wait_full(act, where)
                for sign in range(2):
                    if n or sign:
                        pass
                    if 2 * n + sign >= 2:
                        act.wait_ge(M("in_ready"), 2 * n + sign - 1)
                    ins = nc.scalar.activation(ab[:, sign, :], m.ps[:, where[0], :], ACT.Exp, scale=(1 - 2 * sign) / TAU)
                    if sign:
                        banks.free_chained(act, ins, where)
                        act.sem_inc(M("exp_ready_gla"), 1)
                    else:
                        ins.then_inc(M("exp_ready_gla"), 1)
                        act.wait_ge(M("exp_ready_gla"), 2 * n + 1)
            for n, (t, j) in enumerate([(t, j) for t in range(tiles) for j in range(2)]):
                where = sufs["e", t, j]
                banks.wait_full(act, where)
                if n < 2:
                    act.wait_ge(M("in_ready"), 8)
                else:
                    act.wait_ge(M("k_end_ready"), n - 1)
                banks.free_chained(act, nc.scalar.activation(ab[:, n % 2, :], m.ps[:, where[0], :], ACT.Exp, scale=1.0 / TAU), where)
                act.sem_inc(M("suffix_ready"), 1)
            where = sufs["decay"]
            banks.wait_full(act, where)
            banks.free_chained(act, nc.scalar.activation(decay, m.ps[:, where[0], 0:64], ACT.Exp, scale=1.0 / TAU), where)
            act.sem_inc(M("decay_ready"), 1)
            for n in range(TT * GH):
                norm_act(nc, act, m, M, n0 + n + 1)
            for t in range(TT):
                for n in range(2):
                    where = turned[t, n]
                    banks.wait_full(act, where)
                    ins = nc.scalar.activation(yT[:, 4 * n:4 * n + 4, t * P:(t + 1) * P],
                                               m.ps[:, where[0], :].rearrange("p (c q) -> p c q", c=4), ACT.Copy)
                    banks.free_chained(act, ins, where)
                    act.sem_inc(M("yT_gla"), 1)

        @block.vector
        def _(dve):
            step = Chain(M, dve, "dve_step")
            step(nc.vector.memset(glT[0:RANK + 1, :, :], 1.0), "glT_ones")
            dve.wait_ge(M("projected"), 1)
            for n, (t, j) in enumerate([(t, j) for t in range(tiles) for j in range(2)]):
                where = zs["z", t, j]
                banks.wait_full(dve, where)
                z = m.ps[:, where[0], :]
                step(nc.vector.tensor_copy(low, z))
                a = ab[:, n % 2, :]
                ins = nc.vector.scalar_tensor_tensor(out=a, in0=z, scalar=-1.0, in1=low, op0=ALU.mult, op1=ALU.max)
                banks.free_chained(dve, ins, where)
                dve.sem_inc(M("abs_ready"), 1)
                dve.wait_ge(M("log_ready"), n + 1)
                step(nc.vector.scalar_tensor_tensor(out=g[:, t, j, :], in0=low, scalar=0.0, in1=a, op0=ALU.min, op1=ALU.subtract), "g_ready_gla")
            dve.wait_ge(M("gla_proj"), len(jobs))
            for n, (j, i) in enumerate([(j, i) for j in range(2) for i in range(2)]):
                for sign, (dst, src) in enumerate(((q_in, qT), (k_in, kT))):
                    dve.wait_ge(M("exp_ready_gla"), 2 * n + sign + 1)
                    step(nc.vector.tensor_tensor(dst[:, j, 2 * i:2 * i + 2, :].rearrange("p a b -> p (a b)"),
                                                 src[:, 2 * i:2 * i + 2, :].rearrange("p a b -> p (a b)"), ab[:, sign, :], ALU.mult), "in_ready")
            for n, (t, j) in enumerate([(t, j) for t in range(tiles) for j in range(2)]):
                dve.wait_ge(M("suffix_ready"), n + 1)
                step(nc.vector.tensor_tensor(k_end[:, t, j, :], k[:, t, :], ab[:, n % 2, :], ALU.mult), "k_end_ready")
            dve.wait_ge(M("decay_ready"), 1)

            def masked(h):
                where = atts["att", h]
                banks.wait_full(dve, where)
                if h >= 2:
                    banks.wait_full(dve, outs["o", h - 2])
                a = att[:, h % 2, :]
                banks.free_chained(dve, nc.vector.tensor_scalar(a, m.ps[:, where[0], :], -LOWEST, LOWEST, ALU.min, ALU.max), where)
                for j in range(2):
                    part = a[:, j * T:(j + 1) * T].rearrange("p (t i) -> p t i", t=TT)
                    mask = m.const(("fwd", "bwd")[j]).rearrange("p (o i) -> p o i", o=1).to_broadcast([P, TT, P])
                    ins = nc.vector.tensor_tensor(part, part, mask, ALU.mult)
                    if j == 0:
                        step(ins)
                    else:
                        step(ins, "att_masked")

            masked(0)
            for h in range(GH):
                if h + 1 < GH:
                    masked(h + 1)
                for s in range(7):
                    for j in range(2):
                        t, c = steps[j][s]
                        there = kv[h, s, j]
                        banks.wait_full(dve, there)
                        if s >= 5:
                            dve.wait_ge(M(f"state_read{j}"), (4 - j) * h + s - 4)
                        elif s <= 1 and h:
                            banks.wait_full(dve, outs["o", h - 1])
                        new, kv_ = S[:, j, s % 2, :], m.ps[:, there[0], 0:DV]
                        if s == 0:
                            ins = nc.vector.tensor_copy(new, kv_)
                        else:
                            col = (j * GH + h) * 8 + 2 * t + c
                            ins = nc.vector.scalar_tensor_tensor(out=new, in0=S[:, j, (s - 1) % 2, :], scalar=decay[:, col:col + 1], in1=kv_,
                                                                 op0=ALU.mult, op1=ALU.add)
                        banks.free_chained(dve, ins, there)
                        dve.sem_inc(M(f"state_ready{j}"), 1)
                where = outs["o", h]
                banks.wait_full(dve, where)
                for t in range(TT):
                    norm_dve(nc, dve, step, m, M, m.ps[:, where[0], t * DV:(t + 1) * DV], n0 + TT * h + t + 1,
                             out=o[:, t, h * DV:(h + 1) * DV])
                banks.free_chained(dve, nc.vector.memset(m.stats[:, 40:41], 0.0), where)
            dve.wait_ge(M("gla_in"), 48)
            for t in range(TT):
                step(nc.vector.tensor_tensor(o[:, t, :], o[:, t, :], gn, ALU.mult))
                step(nc.vector.tensor_tensor(o[:, t, :], o[:, t, :], r[:, t, :], ALU.mult), "y_gla")
    return sums


LASTING = ("bank_", "chunk_", "dve_step", "rows_in", "variance_ready", "std_ready", "consts_in")



def program(nc, d, out):
    with ExitStack() as ctx:
        m = Memory(nc, ctx)
        d = dict(d, mod=nc.dram_tensor("mod_rows", [2, 2, 6 * D], F32, kind="Internal").ap())
        M = Marks(nc, ctx)
        banks = Banks(M)
        chunks = [("w_in", d["w_in"][n], SLOT) for n in range(N_IN)]
        chunks += [("w_proj_a", d["w_proj_a"], 2 * D)]
        chunks += [("w_proj_b", d["w_proj_b"][n], SLOT) for n in range(2)]
        chunks += [("w_out", d["w_out"][n], SLOT) for n in range(2)]
        chunks += [("moe", d["moe"][n // PER_EXPERT, n % PER_EXPERT], SLOT) for n in range(PER_EXPERT * NE)]
        for layer in range(2):
            chunks += [(f"w_mod{layer}", d["w_mod"][layer, n], SLOT) for n in range(12)]
        chunks += [("a_w_in", d["a_w_in"][n], SLOT) for n in range(4)]
        chunks += [("a_w_out", d["a_w_out"][n], SLOT) for n in range(2)]
        chunks += [("w_q0", d["w_q"][0, n], SLOT) for n in range(2)]
        chunks += [("b_w_in", d["b_w_in"][n], SLOT) for n in range(6)]
        chunks += [("b_w_out", d["b_w_out"][n], SLOT) for n in range(2)]
        chunks += [("w_q1", d["w_q"][1, n], SLOT) for n in range(2)]
        ring = Ring(M, m.ring, chunks)
        attention(nc, d, m, M, banks, ring)
        route(nc,d,m,M,banks,ring)
        moe(nc,d,m,M,banks,ring)
        M.retire(LASTING)
        modulations(nc, d, m, M, banks, ring)
        modulate(nc, d, m, M, banks, ring, 0, SCALE1, SHIFT1, 4)
        sums = chunk_mlp(nc, d, m, M, banks, ring)
        residual(nc, d, m, M, banks, sums, 0, GATE1, 0, 4)
        modulate(nc, d, m, M, banks, ring, 0, SCALE2, SHIFT2, 4)
        scores(nc, d, m, M, banks, ring, 0, 4)
        sums = peer(nc, d, m, M, banks, 0, 4, 0)
        residual(nc, d, m, M, banks, sums, 0, GATE2, 1, 4)
        modulate(nc, d, m, M, banks, ring, 1, SCALE1, SHIFT1, 4)
        sums = gla(nc, d, m, M, banks, ring)
        residual(nc, d, m, M, banks, sums, 1, GATE1, 0, 2)
        modulate(nc, d, m, M, banks, ring, 1, SCALE2, SHIFT2, 2)
        scores(nc, d, m, M, banks, ring, 1, 2)
        sums = peer(nc, d, m, M, banks, 1, 2, 4)
        residual(nc, d, m, M, banks, sums, 1, GATE2, 1, 2, out)


def chunked(w):
    lead = w.shape[:-2]
    n = w.shape[-1] // 512
    w = w.reshape(*lead, KT, P, n, 512)
    k = len(lead)
    return np.ascontiguousarray(w.transpose(*range(k), k + 2, k + 1, k, k + 3)).reshape(*lead, n, P, KT * 512)


def pair_heads(w, axis):
    w = np.moveaxis(w, axis, -1)
    w = w.reshape(*w.shape[:-1], 2, SWA_PAIRS, HD).swapaxes(-3, -2).reshape(*w.shape[:-1], -1)
    return np.moveaxis(w, -1, axis)


def layout(i):
    w = i["w_in"][0]
    qa, ka, va, qb, kb, vb, ga, gb = np.split(w, np.cumsum([768, 768, 768, 1024, 128, 128, 1024]), axis=1)
    w_in = np.concatenate([qa, ka, pair_heads(qb, 1), kb, va, vb, ga, gb], axis=1)
    moe = np.stack([i[n][0] for n in ("w_gate", "w_up", "w_down")], 1).reshape(NE, PER_EXPERT, KT // 2, P, D)
    moe = moe.transpose(0, 1, 3, 2, 4).reshape(NE, PER_EXPERT, P, SLOT)
    out = {
        "x": i["x"][0],
        "xT": i["x"][0].T.reshape(KT, P, T).transpose(1, 0, 2),
        "w_in": chunked(w_in),
        "w_proj_a": i["w_proj_a"][0].reshape(2, P, D).transpose(1, 0, 2).reshape(P, 2 * D),
        "w_proj_b": chunked(pair_heads(i["w_proj_b"][0], 0)),
        "w_out": chunked(i["w_out"][0]),
        "sinks": i["sinks"],
        "moe": moe,
        "lns": np.stack([i["ln1_g"][0], i["ln1_b"][0], i["ln2_g"][0], i["ln2_b"][0]]),
        "router_w": i["router_w"][0].reshape(KT, P, NE).transpose(1, 0, 2),
        "router_b": i["router_b"],
        "b_gate": i["b_gate"][0],
        "b_up": i["b_up"][0],
        "b_down": i["b_down"][0],
        "c": np.stack([i["c_2"][0], i["c_ctx_2"]]).reshape(2, KT, P).transpose(2, 1, 0),
        "ctx": i["ctx_2"][0],
        "w_mod": chunked(i["w_mod_2"]),
        "b_mod": i["b_mod_2"],
        "ln_g": i["ln_g_2"].reshape(4, D),
        "ln_b": i["ln_b_2"].reshape(4, D),
        "a_w_in": chunked(np.concatenate([i["a_w_in_2"][0][:, D:], i["a_w_in_2"][0][:, :D]], 1)),
        "a_norm": np.stack([i["a_norm_g_2"][0], i["a_norm_b_2"][0]]),
        "a_w_s": i["a_w_s_2"][0].transpose(2, 0, 1),
        "a_b_s": i["a_b_s_2"][0].T,
        "a_w_out": chunked(i["a_w_out_2"][0]),
        "b_w_in": chunked(np.concatenate([i["b_w_in_2"][0][:, a:b] for a, b in ((512, 1024), (1024, 2048), (0, 512), (2048, 3072))], 1)),
        "b_w_gl": i["b_w_in_2"][0][:, 3072:].reshape(KT, P, 2 * RANK).transpose(1, 0, 2),
        "b_w_gate": np.concatenate([i["b_w_gate_2"][0], i["b_gate_bias_2"][0][:, None, :]], 1).transpose(1, 0, 2),
        "b_gn_g": i["b_gn_g_2"],
        "b_w_out": chunked(i["b_w_out_2"][0]),
        "w_q": chunked(i["p_w_q_2"]),
        "keys": i["p_keys_2"].transpose(0, 1, 3, 2).reshape(2, P, NKEY),
        "u0": i["p_u_2"][0], "u1": i["p_u_2"][1], "v0": i["p_v_2"][0], "v1": i["p_v_2"][1],
    }
    out["consts"] = np.concatenate([np.asarray(a, np.float32) for a in constants().values()], 1)
    out["dist"] = distances()
    return out


def kernel(**inputs):
    import numpy as _np
    import concourse.bacc as _bacc
    from concourse import mybir as _mybir
    from concourse.bass_utils import run_bass_kernel_spmd as _run

    nc = _bacc.Bacc("TRN2", target_bir_lowering=False, num_devices=1)
    arrays, aps = {}, {}
    for name, a in layout({k: _np.asarray(v) for k, v in inputs.items()}).items():
        a = _np.ascontiguousarray(a)
        arrays[f"in_{name}"] = a
        aps[name] = nc.dram_tensor(f"in_{name}", a.shape, _mybir.dt.from_np(a.dtype), kind="ExternalInput").ap()
    out = nc.dram_tensor("out_0", (1, T, D), _mybir.dt.float32, kind="ExternalOutput").ap()
    program(nc, aps, out)
    r = _run(nc, [arrays], core_ids=[0])
    return r.results[0]["out_0"]
```

```python
from contextlib import ExitStack

import numpy as np
import concourse.bass as bass
from concourse import mybir

F32 = mybir.dt.float32
U32 = mybir.dt.uint32
I32 = mybir.dt.int32
ALU = mybir.AluOpType
ACT = mybir.ActivationFunctionType
AX = mybir.AxisListType

P = 128
D = 1024
KT = D // P
T = 256
TT = T // P
HD = 64
EPS = 1e-5
DIL_HEADS, DIL_GROUPS, SWA_PAIRS = 4, 3, 8
N_SLOPES = 28
SLOPES = [float(np.float32(2.0 ** (-8.0 * (h + 1) / N_SLOPES))) for h in range(N_SLOPES)]
Q_A, K_A, Q_B, K_B, V_T, GATE = 0, 6, 12, 20, 21, 28
V_COLS = 896
N_IN = 11
ALPHA1 = 2.0 ** 0.25
FAR = -1e34
NE, TOPK, SLOTS = 32, 4, 64
PASSES = T // SLOTS
PER_EXPERT = 6
LIMIT, SW_ALPHA = 7.0, 1.702
ALPHA2 = 4.0 ** 0.25
SHIFT1, SCALE1, GATE1, SHIFT2, SCALE2, GATE2 = range(6)
PH, PK, NKEY = 8, 16, 128
GH, DK, DV, RANK, TAU = 4, 128, 256, 16, 16.0
CH = 64
LOWEST = -3.0e38
SLOT = KT * 512
NSLOT = 6


class Marks:

    def __init__(self, nc, ctx):
        self.nc, self.ctx, self.sems, self.n, self.spare = nc, ctx, {}, {}, []

    def __call__(self, name):
        if name not in self.sems:
            self.sems[name] = self.spare.pop() if self.spare else self.ctx.enter_context(self.nc.semaphore(name))
        return self.sems[name]

    def retire(self, kept):
        names = [n for n in self.sems if not n.startswith(kept)]
        with self.nc.Block() as block:

            @block.sync
            def _(sp):
                for name in names:
                    sp.sem_clear(self.sems[name])

        for name in names:
            self.spare.append(self.sems.pop(name))
            self.n.pop(name, None)

    def up(self, ins, name, by=1):
        ins.then_inc(self(name), by)
        self.n[name] = self.n.get(name, 0) + by
        return self.n[name]


class Chain:

    def __init__(self, marks, eng, name):
        self.marks, self.eng, self.name = marks, eng, name

    def __call__(self, ins, name=None):
        name = name or self.name
        value = self.marks.up(ins, name)
        self.eng.wait_ge(self.marks(name), value)


class Banks:

    def __init__(self, marks):
        self.marks, self.used = marks, [0] * 8

    def plan(self, names, banks):
        table = {}
        for i, name in enumerate(names):
            bank = banks[i % len(banks)]
            table[name] = (bank, self.used[bank])
            self.used[bank] += 1
        return table

    def wait_free(self, pe, where):
        bank, nth = where
        if nth:
            pe.wait_ge(self.marks(f"bank_free{bank}"), nth)

    def fill(self, ins, where):
        ins.then_inc(self.marks(f"bank_full{where[0]}"), 1)

    def wait_full(self, eng, where):
        eng.wait_ge(self.marks(f"bank_full{where[0]}"), where[1] + 1)

    def free(self, ins, where):
        ins.then_inc(self.marks(f"bank_free{where[0]}"), 1)

    def free_chained(self, eng, ins, where):
        ins.then_inc(self.marks(f"bank_free{where[0]}"), 1)
        eng.wait_ge(self.marks(f"bank_free{where[0]}"), where[1] + 1)


class Ring:

    def __init__(self, marks, mem, chunks):
        self.marks, self.mem, self.chunks, self.sent = marks, mem, chunks, 0
        self.at = {}
        for n, (name, _, _) in enumerate(chunks):
            self.at.setdefault(name, n)

    def load(self, sp, end):
        for n in range(self.sent, min(end, len(self.chunks))):
            slot, nth = n % NSLOT, n // NSLOT
            _, src, size = self.chunks[n]
            if nth:
                sp.wait_ge(self.marks(f"chunk_used{slot}"), nth)
            sp.dma_start(self.mem[:, slot, 0:size], src).then_inc(self.marks(f"chunk_in{slot}"), 16)
        self.sent = max(self.sent, min(end, len(self.chunks)))

    def upto(self, name, count):
        return self.at[name] + count + NSLOT

    def wait(self, pe, name, i=0):
        n = self.at[name] + i
        pe.wait_ge(self.marks(f"chunk_in{n % NSLOT}"), 16 * (n // NSLOT + 1))
        return self.mem[:, n % NSLOT, :].rearrange("p (k j) -> p k j", k=KT)

    def used(self, ins, name, i=0):
        ins.then_inc(self.marks(f"chunk_used{(self.at[name] + i) % NSLOT}"), 1)


def products(nc, out, pairs):
    for i, (lhs, rhs) in enumerate(pairs):
        last = nc.tensor.matmul(out, lhs, rhs, start=i == 0, stop=i == len(pairs) - 1)
    return last


class Memory:

    def __init__(self, nc, ctx):
        def sb(name, shape, dtype=F32):
            return ctx.enter_context(nc.sbuf_tensor("sb_" + name, shape, dtype))

        self.ring = sb("ring", [P, NSLOT, SLOT])
        self.arena = sb("arena", [P, 16384])
        self.H = sb("H", [P, 4, D])
        self.X = sb("X", [P, 4, D])
        self.consts = sb("consts", [P, CONST_COLS])
        self.idx = sb("idx", [P, 2 * PK], U32)[:, :]
        self.wts = sb("wts", [P, 4 * PK])
        self.diag = [sb(f"diag{i}", [P, P])[:, :] for i in range(4)]
        self.cur_idx = sb("cur_idx", [P, 2 * PK], U32)
        self.dots = sb("dots", [P, PK])
        self.act = sb("act", [P, PK])
        self.stats = sb("stats", [P, 64])
        self.count = sb("count", [1, 2], I32)
        self.norms, self.rows_sent = 0, 0
        self.ps = ctx.enter_context(nc.psum_tensor("ps", [P, 8, 512], F32))

    def const(self, name):
        a, n = CONST_AT[name]
        return self.consts[:, a:a + n]

    def part(self, start, *dims):
        size = int(np.prod(dims))
        flat = self.arena[:, start:start + size]
        names = "abcd"[:len(dims)]
        if len(dims) == 1:
            return flat
        return flat.rearrange(f"p ({' '.join(names)}) -> p {' '.join(names)}",
                              **{n: d for n, d in zip(names, dims)})


def constants():
    j, i = np.arange(P)[:, None], np.arange(P)[None, :]
    same = (j // CH) == (i // CH)
    parts = {
        "ident": (j == i),
        "upto": (j <= i),
        "ones": np.ones((P, P)),
        "fwd": (j <= i) & same,
        "bwd": (j >= i) & same,
        "after": (j > i) & same,
        "before": (j < i) & same,
        "chunk": j // CH == np.arange(2)[None, :],
        "iota": np.broadcast_to(np.arange(P) % CH, (P, P)),
        "zero": np.zeros((P, P)),
    }
    return parts


CONST_AT, CONST_COLS = {}, 0
for _name, _a in constants().items():
    CONST_AT[_name] = (CONST_COLS, _a.shape[1])
    CONST_COLS += _a.shape[1]


def distances():
    out = np.full((P, 4, 384), FAR, np.float32)
    for block, (at, nk) in enumerate(((0, 128), (128, 256))):
        i, j = block * P + np.arange(P)[:, None], np.arange(nk)[None, :]
        d = i - j
        seen = [(d >= 0) & (d <= 127), (d >= 0) & (d <= 128), (d >= 0) & (d % 4 == 0), (d >= 0) & (d % 16 == 0)]
        for kind, s in enumerate(seen):
            out[:, kind, at:at + nk] = np.where(s, -d, FAR)
    return out



def attention(nc, d, m, M, banks, ring):
    qk = m.part(0, 21, T)
    v = m.part(5376, TT, V_COLS)
    gates = m.part(7168, 16, T)
    oT = m.part(11264, 10, T)
    pT = m.part(13824, 2, 6, P)
    tmp = m.part(15360, 2, T)
    rows = m.H[:, :, :].rearrange("p a b -> p (a b)")
    xT = rows[:, 0:2048].rearrange("p (k t) -> p k t", k=KT)
    sc = rows[:, 2048:2048 + 2 * 772].rearrange("p (u c) -> p u c", u=2)
    spare = m.X[:, 2:4, :].rearrange("p a b -> p (a b)")
    dist = spare[:, 0:1536].rearrange("p (k c) -> p k c", k=4)
    sinks = spare[:, 1536:1552]
    X = m.X
    ident = m.const("ident")

    norm_rows = [m.H[:, 2, :], m.H[:, 3, :]]
    n0 = m.norms
    m.norms += TT

    units = [("dil", h, b) for b in range(TT) for h in range(DIL_HEADS)]
    units += [("swa", t, b) for b in range(TT) for t in range(SWA_PAIRS)]

    def blocks(unit):
        return (DIL_GROUPS if unit[0] == "dil" else 2), unit[2] + 1

    proj = [("qk", n) for n in range(10)] + [("kb", 0)] + [("v", i) for i in range(4)]
    proj += [("gate", n) for n in range(8)]
    gp = banks.plan(proj, [0, 1, 2, 3])
    go = banks.plan([("o", u) for u in range(len(units))], [6])

    c = rows[:, 3592:3608].rearrange("p (k s) -> p k s", k=KT)
    silu_c = rows[:, 3608:3624].rearrange("p (k s) -> p k s", k=KT)
    bias = m.part(15872, 512)
    stage = rows[:, 0:1024].rearrange("p (a b) -> p a b", a=2)
    n_mod = 2 * 6 * D // (4 * 512)
    assert len(units) == 4 * n_mod
    mods = banks.plan([("mod", i) for i in range(n_mod)], [7])
    gm = banks.plan([("m", i) for i in range(KT)], [0, 1, 2, 3])
    gx = banks.plan([("x", i) for i in range(4)], [4, 5, 6, 7])

    with nc.Block() as block:

        @block.gpsimd
        def _(pool):
            for i in range(n_mod):
                pool.wait_ge(M("mod_staged"), i + 1)
                for g in range(4):
                    col = (4 * (i % (n_mod // 2)) + g) * 512
                    pool.dma_start(d["mod"][i // (n_mod // 2), :, col:col + 512], stage[32 * g:32 * g + 2, i % 2, :])\
                        .then_inc(M(f"mod_out{i % 2}"), 16)
            for i in range(2):
                pool.wait_ge(M(f"mod_out{i}"), 64 * (n_mod // 2))

        @block.sync
        def _(sp):
            sp.dma_start(xT, d["xT"]).then_inc(M("xT_in"), 16)
            ring.load(sp, 2)
            sp.dma_start(m.consts[:, :], d["consts"]).then_inc(M("consts_in"), 16)
            sp.dma_start(dist, d["dist"]).then_inc(M("dist_in"), 16)
            sp.dma_start(sinks, d["sinks"].to_broadcast([P, 16])).then_inc(M("dist_in"), 16)
            sp.dma_start(c, d["c"]).then_inc(M("c_in"), 16)
            sp.dma_start(bias[0:4 * n_mod, :], d["b_mod"]).then_inc(M("c_in"), 16)
            sp.dma_start(X[:, 0:TT, :], d["x"].rearrange("(t p) c -> p t c", p=P)).then_inc(M("x_in"), 16)
            ring.load(sp, ring.upto("w_out", 2) - 2)
            sp.wait_ge(M("merged_ready"), KT)
            load_rows(sp, M, m, [d["lns"][i:i + 1, :] for i in range(2)], norm_rows)
            ring.load(sp, ring.upto("w_out", 2))

        @block.tensor
        def _(pe):
            pe.wait_ge(M("xT_in"), 16)

            def channel_tile(chunk, j, out):
                return products(nc, out, [(w[:, k, j * P:(j + 1) * P], xT[:, k, :]) for k in range(KT)])

            w = ring.wait(pe, "w_in", 0)
            for n in range(10):
                if n and n % 2 == 0:
                    w = ring.wait(pe, "w_in", n // 2)
                where = gp["qk", n]
                banks.wait_free(pe, where)
                channel_tile(w, 2 * (n % 2), m.ps[:, where[0], 0:T])
                last = channel_tile(w, 2 * (n % 2) + 1, m.ps[:, where[0], T:2 * T])
                banks.fill(last, where)
                if n % 2:
                    pe.wait_ge(M(f"bank_full{where[0]}"), where[1] + 1)
                    pe.sem_inc(M(f"chunk_used{(ring.at['w_in'] + n // 2) % NSLOT}"), 1)
            w = ring.wait(pe, "w_in", 5)
            where = gp["kb", 0]
            banks.wait_free(pe, where)
            banks.fill(channel_tile(w, 0, m.ps[:, where[0], 0:T]), where)
            for i in range(4):
                t, piece = i % 2, i // 2
                if i == 2:
                    w = ring.wait(pe, "w_in", 6)
                cols = slice(P, 512) if piece == 0 else slice(0, 512)
                where = gp["v", i]
                banks.wait_free(pe, where)
                last = products(nc, m.ps[:, where[0], 0:cols.stop - cols.start],
                                [(xT[:, k, t * P:(t + 1) * P], w[:, k, cols]) for k in range(KT)])
                banks.fill(last, where)
                if t:
                    pe.wait_ge(M(f"bank_full{where[0]}"), where[1] + 1)
                    pe.sem_inc(M(f"chunk_used{(ring.at['w_in'] + 5 + piece) % NSLOT}"), 1)
            for n in range(8):
                if n % 2 == 0:
                    w = ring.wait(pe, "w_in", 7 + n // 2)
                where = gp["gate", n]
                banks.wait_free(pe, where)
                channel_tile(w, 2 * (n % 2), m.ps[:, where[0], 0:T])
                last = channel_tile(w, 2 * (n % 2) + 1, m.ps[:, where[0], T:2 * T])
                banks.fill(last, where)
                if n % 2:
                    pe.wait_ge(M(f"bank_full{where[0]}"), where[1] + 1)
                    pe.sem_inc(M(f"chunk_used{(ring.at['w_in'] + 7 + n // 2) % NSLOT}"), 1)

            def scores(u):
                kind, h, b = units[u]
                nk = P * (b + 1)
                out = m.ps[:, 2 * (u % 2):2 * (u % 2) + 2, :].rearrange("p a b -> p (a b)")
                if u >= 2:
                    pe.wait_ge(M("scores_read"), u - 1)
                for g in range(blocks(units[u])[0]):
                    if kind == "dil":
                        rows_ = slice((h % 2) * HD, (h % 2) * HD + HD)
                        qt, kt = Q_A + 2 * g + h // 2, K_A + 2 * g + h // 2
                    else:
                        rows_ = slice(g * HD, (g + 1) * HD)
                        qt, kt = Q_B + h, K_B
                    at = g * nk if kind == "dil" else g * 512
                    last = nc.tensor.matmul(out[:, at:at + nk], qk[rows_, qt, b * P:(b + 1) * P],
                                            qk[rows_, kt, 0:nk], start=True, stop=True)
                last.then_inc(M("scores_done"), 1)

            def modulation(u):
                i, quarter = u // 4, u % 4
                where = mods["mod", i]
                w = ring.wait(pe, "w_mod", u).rearrange("p k j -> p (k j)").rearrange("p (k j) -> p k j", k=2)
                if quarter == 0:
                    banks.wait_free(pe, where)
                    for g in range(4):
                        nc.tensor.matmul(m.ps[32 * g:32 * g + 2, where[0], :], ident[0:4 * n_mod, 4 * i + g:4 * i + g + 1].to_broadcast([4 * n_mod, 2]),
                                         bias[0:4 * n_mod, :], start=True, stop=False, skip_group_check=True)
                for k in range(2):
                    for g in range(4):
                        last = nc.tensor.matmul(m.ps[32 * g:32 * g + 2, where[0], :], silu_c[:, 2 * quarter + k, :],
                                                w[:, k, g * 512:(g + 1) * 512], start=False, stop=quarter == 3 and k == 1,
                                                skip_group_check=True)
                if quarter == 3:
                    banks.fill(last, where)
                    pe.wait_ge(M(f"bank_full{where[0]}"), where[1] + 1)
                    pe.sem_inc(M(f"chunk_used{(ring.at['w_mod'] + u) % NSLOT}"), 1)
                else:
                    ring.used(last, "w_mod", u)

            pe.wait_ge(M("qkv_ready"), 15)
            pe.wait_ge(M("consts_in"), 16)
            pe.wait_ge(M("gates_ready"), 8)
            pe.wait_ge(M("c_in"), 32)
            pe.wait_ge(M("silu_ready"), 1)
            scores(0)
            scores(1)
            for u, unit in enumerate(units):
                n_seg, nb = blocks(unit)
                turned = m.ps[:, 4:6, :].rearrange("p a b -> p (a b)")
                pe.wait_ge(M("probs_ready"), u + 1)
                if u:
                    pe.wait_ge(M("probsT_ready"), u)
                stride = nb * P + (1 if unit[0] == "swa" else 0)
                for g in range(n_seg):
                    for kb in range(nb):
                        at = g * stride + kb * P
                        i = g * nb + kb
                        last = nc.tensor.transpose(turned[:, i * P:(i + 1) * P], sc[:, u % 2, at:at + P], ident)
                last.then_inc(M("probsT_done"), 1)
                if u + 2 < len(units):
                    scores(u + 2)
                modulation(u)
                pe.wait_ge(M("probsT_ready"), u + 1)
                where = go["o", u]
                banks.wait_free(pe, where)
                kind, h, b = unit
                for g in range(n_seg):
                    for kb in range(nb):
                        i = g * nb + kb
                        if kind == "dil":
                            rows_ = slice((h % 2) * HD, (h % 2) * HD + HD)
                            col, start, stop = g * 256 + h * HD, i == 0, i == n_seg * nb - 1
                        else:
                            rows_ = slice(g * HD, (g + 1) * HD)
                            col, start, stop = 768 + g * HD, kb == 0, kb == nb - 1
                        last = nc.tensor.matmul(m.ps[rows_, where[0], 0:P], v[:, kb, col:col + HD],
                                                pT[:, u % 2, i, :], start=start, stop=stop)
                banks.fill(last, where)

            wa = ring.wait(pe, "w_proj_a", 0)
            wa = ring.mem[:, ring.at["w_proj_a"] % NSLOT, 0:2048].rearrange("p (k j) -> p k j", k=2)
            pe.wait_ge(M("o_ready"), len(units))
            for i in range(KT):
                if i % 4 == 0:
                    wb = ring.wait(pe, "w_proj_b", i // 4)
                where = gm["m", i]
                banks.wait_free(pe, where)
                products(nc, m.ps[:, where[0], 0:T], [(wa[:, k, i * P:(i + 1) * P], oT[:, k, :]) for k in range(2)])
                j = i % 4
                last = products(nc, m.ps[:, where[0], T:2 * T],
                                [(wb[:, k, j * P:(j + 1) * P], oT[:, 2 + k, :]) for k in range(KT)])
                banks.fill(last, where)
                if j == 3:
                    pe.wait_ge(M(f"bank_full{where[0]}"), where[1] + 1)
                    pe.sem_inc(M(f"chunk_used{(ring.at['w_proj_b'] + i // 4) % NSLOT}"), 1)
                    if i == KT - 1:
                        pe.sem_inc(M(f"chunk_used{ring.at['w_proj_a'] % NSLOT}"), 1)
            pe.wait_ge(M("merged_ready"), KT)
            for i in range(4):
                t, half = i // 2, i % 2
                w = ring.wait(pe, "w_out", half)
                where = gx["x", i]
                banks.wait_free(pe, where)
                last = products(nc, m.ps[:, where[0], :], [(gates[:, k, t * P:(t + 1) * P], w[:, k, :]) for k in range(KT)])
                banks.fill(last, where)
                if t:
                    pe.wait_ge(M(f"bank_full{where[0]}"), where[1] + 1)
                    pe.sem_inc(M(f"chunk_used{(ring.at['w_out'] + half) % NSLOT}"), 1)

        @block.scalar
        def _(act):
            act.wait_ge(M("c_in"), 32)
            nc.scalar.activation(silu_c, c, ACT.Silu).then_inc(M("silu_ready"), 1)
            for n in range(10):
                where = gp["qk", n]
                banks.wait_full(act, where)
                is_q = n < 3 or n >= 6
                ins = nc.scalar.activation(qk[:, 2 * n:2 * n + 2, :].rearrange("p a b -> p (a b)"), m.ps[:, where[0], :],
                                           ACT.Copy, scale=HD ** -0.5 if is_q else 1.0)
                banks.free_chained(act, ins, where)
                act.sem_inc(M("qkv_ready"), 1)
            where = gp["kb", 0]
            banks.wait_full(act, where)
            banks.free_chained(act, nc.scalar.activation(qk[:, K_B, :], m.ps[:, where[0], 0:T], ACT.Copy), where)
            act.sem_inc(M("qkv_ready"), 1)
            for i in range(4):
                t, piece = i % 2, i // 2
                where = gp["v", i]
                banks.wait_full(act, where)
                dst = v[:, t, 0:384] if piece == 0 else v[:, t, 384:V_COLS]
                banks.free_chained(act, nc.scalar.activation(dst, m.ps[:, where[0], 0:384 if piece == 0 else 512], ACT.Copy), where)
                act.sem_inc(M("qkv_ready"), 1)
            for n in range(8):
                where = gp["gate", n]
                banks.wait_full(act, where)
                ins = nc.scalar.activation(gates[:, 2 * n:2 * n + 2, :].rearrange("p a b -> p (a b)"), m.ps[:, where[0], :], ACT.Sigmoid)
                banks.free_chained(act, ins, where)
                act.sem_inc(M("gates_ready"), 1)

            def exps(u):
                kind, h, b = units[u]
                nk = P * (b + 1)
                act.wait_ge(M("max_ready"), u + 1)
                n, width = (1, 3 * nk) if kind == "dil" else (2, nk + 1)
                for s in range(n):
                    part = sc[:, u % 2, s * width:(s + 1) * width]
                    ins = nc.scalar.activation(part, part, ACT.Exp, bias=m.stats[:, 4 + 2 * (u % 2) + s:5 + 2 * (u % 2) + s],
                                               accum_out=m.stats[:, 8 + 2 * (u % 2) + s:9 + 2 * (u % 2) + s])
                ins.then_inc(M("exp_done"), 1)

            def turn(u):
                n_seg, nb = blocks(units[u])
                act.wait_ge(M("probsT_done"), u + 1)
                if u >= 2:
                    banks.wait_full(act, go["o", u - 2])
                n = n_seg * nb * P
                nc.scalar.activation(pT[:, u % 2, :, :].rearrange("p a b -> p (a b)")[:, 0:n],
                                     m.ps[:, 4:6, :].rearrange("p a b -> p (a b)")[:, 0:n], ACT.Copy)\
                    .then_inc(M("probsT_ready"), 1)

            def mod_out(i):
                where = mods["mod", i]
                banks.wait_full(act, where)
                if i >= 2:
                    act.wait_ge(M(f"mod_out{i % 2}"), 64 * (i // 2))
                for g in range(4):
                    which = (4 * (i % (n_mod // 2)) + g) // 2
                    rows_ = slice(32 * g, 32 * g + 2)
                    last = nc.scalar.activation(stage[rows_, i % 2, :], m.ps[rows_, where[0], :], ACT.Copy,
                                                bias=1.0 if which in (SCALE1, SCALE2) else 0.0)
                banks.free(last, where)
                act.wait_ge(M(f"bank_free{where[0]}"), where[1] + 1)
                act.sem_inc(M("mod_staged"), 1)

            exps(0)
            for u in range(len(units)):
                if u + 1 < len(units):
                    exps(u + 1)
                turn(u)
                if u % 4 == 0 and u:
                    mod_out(u // 4 - 1)
            mod_out(n_mod - 1)
            for t in range(TT):
                norm_act(nc, act, m, M, n0 + t + 1)

        @block.vector
        def _(dve):
            step = Chain(M, dve, "dve_step")
            dve.wait_ge(M("dist_in"), 32)

            def biased(u):
                kind, h, b = units[u]
                nk = P * (b + 1)
                dve.wait_ge(M("scores_done"), u + 1)
                if u >= 2:
                    dve.wait_ge(M("probsT_done"), u - 1)
                scores_ = m.ps[:, 2 * (u % 2):2 * (u % 2) + 2, :].rearrange("p a b -> p (a b)")
                at = 0 if b == 0 else P
                n_seg = blocks(units[u])[0]
                for g in range(n_seg):
                    if kind == "dil":
                        kindd, slope, col, src = 1 + g, SLOPES[16 + 4 * g + h], g * nk, g * nk
                    else:
                        kindd, slope, col, src = 0, SLOPES[8 * g + h], g * (nk + 1), g * 512
                        nc.vector.tensor_copy(sc[:, u % 2, col + nk:col + nk + 1], sinks[:, 8 * g + h:8 * g + h + 1]).then_inc(M("sink_set"), 1)
                    last = nc.vector.scalar_tensor_tensor(
                        out=sc[:, u % 2, col:col + nk], in0=dist[:, kindd, at:at + nk], scalar=slope,
                        in1=scores_[:, src:src + nk], op0=ALU.mult, op1=ALU.add)
                last.then_inc(M("scores_read"), 1)
                dve.wait_ge(M("scores_read"), u + 1)
                n, width = (1, 3 * nk) if kind == "dil" else (2, nk + 1)
                step(nc.vector.tensor_reduce(m.stats[:, 0:n], sc[:, u % 2, 0:n * width].rearrange("p (s c) -> p s c", s=n),
                                             axis=AX.X, op=ALU.max))
                nc.vector.tensor_scalar(m.stats[:, 4 + 2 * (u % 2):4 + 2 * (u % 2) + n], m.stats[:, 0:n], -1.0, None, ALU.mult)\
                    .then_inc(M("max_ready"), 1)
                dve.wait_ge(M("max_ready"), u + 1)

            def normal(u):
                kind, h, b = units[u]
                nk = P * (b + 1)
                dve.wait_ge(M("exp_done"), u + 1)
                n, width = (1, 3 * nk) if kind == "dil" else (2, nk + 1)
                den = m.stats[:, 8 + 2 * (u % 2):8 + 2 * (u % 2) + n]
                step(nc.vector.reciprocal(m.stats[:, 12:12 + n], den))
                p3 = sc[:, u % 2, 0:n * width].rearrange("p (s c) -> p s c", s=n)
                nc.vector.tensor_tensor(p3, p3, m.stats[:, 12:12 + n].rearrange("p (s c) -> p s c", c=1).to_broadcast([P, n, width]),
                                        ALU.mult).then_inc(M("probs_ready"), 1)
                dve.wait_ge(M("probs_ready"), u + 1)

            def out_of(u):
                kind, h, b = units[u]
                where = go["o", u]
                banks.wait_full(dve, where)
                if kind == "dil":
                    rows_, tile = slice((h % 2) * HD, (h % 2) * HD + HD), h // 2
                else:
                    rows_, tile = slice(0, P), 2 + h
                ins = nc.vector.tensor_copy(oT[rows_, tile, b * P:(b + 1) * P], m.ps[rows_, where[0], 0:P])
                banks.free_chained(dve, ins, where)
                dve.sem_inc(M("o_ready"), 1)

            biased(0)
            for u in range(len(units)):
                if u + 1 < len(units):
                    biased(u + 1)
                normal(u)
                if u:
                    out_of(u - 1)
            out_of(len(units) - 1)
            dve.wait_ge(M("gates_ready"), 8)
            both = m.part(7168, 2, KT, T)
            for i in range(KT):
                where = gm["m", i]
                banks.wait_full(dve, where)
                ins = nc.vector.tensor_tensor(tmp, m.ps[:, where[0], :].rearrange("p (a b) -> p a b", a=2), both[:, :, i, :], ALU.mult)
                banks.free_chained(dve, ins, where)
                nc.vector.tensor_tensor(gates[:, i, :], tmp[:, 0, :], tmp[:, 1, :], ALU.add).then_inc(M("merged_ready"), 1)
                dve.wait_ge(M("merged_ready"), i + 1)
            dve.wait_ge(M("x_in"), 16)
            dve.wait_ge(M("rows_in"), m.rows_sent)
            for i in range(4):
                t, half = i // 2, i % 2
                where = gx["x", i]
                banks.wait_full(dve, where)
                part = X[:, t, half * 512:(half + 1) * 512]
                ins = nc.vector.scalar_tensor_tensor(out=part, in0=part, scalar=ALPHA1, in1=m.ps[:, where[0], :], op0=ALU.mult, op1=ALU.add)
                banks.free_chained(dve, ins, where)
                if half:
                    norm_dve(nc, dve, step, m, M, X[:, t, :], n0 + t + 1)
                    step(nc.vector.tensor_tensor(X[:, t, :], X[:, t, :], norm_rows[0], ALU.mult))
                    step(nc.vector.tensor_tensor(X[:, t, :], X[:, t, :], norm_rows[1], ALU.add), "y_ready")



LN = {"sum": (16, 28), "mv": (28, 30), "var": (30, 31), "std": (31, 32), "rstd": (32, 33)}


def stat(m, name):
    a, b = LN[name]
    return m.stats[:, a:b]


def norm_dve(nc, dve, step, m, M, x, n, out=None):
    out = x if out is None else out
    width = x.shape[-1]
    pieces = max(1, width // 512)
    for i in range(pieces):
        piece = x[:, i * 512:(i + 1) * 512] if pieces > 1 else x
        step(nc.vector.bn_stats(m.stats[:, 16 + 6 * i:22 + 6 * i], piece))
    step(nc.vector.bn_aggr(stat(m, "mv"), m.stats[:, 16:16 + 6 * pieces]))
    step(nc.vector.tensor_scalar(stat(m, "var"), m.stats[:, 29:30], EPS, None, ALU.add), "variance_ready")
    dve.wait_ge(M("std_ready"), n)
    step(nc.vector.reciprocal(stat(m, "rstd"), stat(m, "std")))
    step(nc.vector.tensor_scalar(out, x, m.stats[:, 28:29], stat(m, "rstd"), ALU.subtract, ALU.mult))


def norm_act(nc, act, m, M, n):
    act.wait_ge(M("variance_ready"), n)
    nc.scalar.activation(stat(m, "std"), stat(m, "var"), ACT.Sqrt).then_inc(M("std_ready"), 1)


def row(m, i):
    return m.part(12288, 4, D)[:, i, :]


def load_rows(sp, M, m, sources, places=None):
    for i, src in enumerate(sources):
        sp.dma_start(places[i] if places else row(m, i), src.to_broadcast([P, D])).then_inc(M("rows_in"), 16)
    m.rows_sent += 16 * len(sources)


def residual_rows(d, layer, which, gate, streams):
    n = 2 * layer + which
    return [mod_row(d, layer, s, gate) for s in range(streams)] + [d["ln_g"][n:n + 1, :], d["ln_b"][n:n + 1, :]]



class Experts:

    def __init__(self, m):
        self.yT = m.part(0, KT, T)
        self.router = m.part(4096, KT, NE)
        self.router_b = m.part(4352, NE)
        self.logits = m.part(4384, TT, NE)
        self.gates = m.part(4448, TT, NE)
        self.chosen = m.part(4512, TT, NE)
        self.place = m.part(4576, TT, NE + 1)
        self.onehot = m.part(4672, NE)
        self.top = m.part(4704, TT, 8)
        self.top_i = m.part(4720, TT, 8)
        self.top_at = m.arena[:, 4736:4744].bitcast(U32)
        self.exp = m.part(4752, 8)
        self.gatesT = m.part(4800, T)
        self.total = m.part(5056, NE + 2)
        self.b_gate = m.part(5120, D)
        self.b_up = m.part(6144, D)
        self.b_down = m.part(7168, D)
        self.pick = m.part(8192, TT, SLOTS)
        self.weigh = m.part(8320, TT, P)
        self.weighT = m.part(8576, T)
        self.xe = m.part(8832, KT, SLOTS)
        self.g = m.part(9344, 512)
        self.sig = m.part(9856, 512)
        self.u = m.part(10368, 512)
        self.h = m.part(10880, 512)
        self.hT = m.part(2048, 4, 2, SLOTS)
        self.ye = m.part(2560, 512)
        self.select = m.part(3072, SLOTS)


def route(nc, d, m, M, banks, ring):
    x = Experts(m)
    turn = banks.plan([("t", i) for i in range(4)], [4, 5, 6, 7])
    small = banks.plan([("logit", t) for t in range(TT)] + [("place", t) for t in range(TT)] + ["total", "gT"], [0, 1, 2, 3])
    with nc.Block() as block:

        @block.sync
        def _(sp):
            load_rows(sp, M, m, [d["lns"][i:i + 1, :] for i in range(2, 4)], [row(m, 2), row(m, 3)])
            for dst, src in ((x.router, d["router_w"]), (x.router_b[0:1, :], d["router_b"]), (x.b_gate[0:NE, :], d["b_gate"]),
                             (x.b_up[0:NE, :], d["b_up"]), (x.b_down[0:NE, :], d["b_down"])):
                sp.dma_start(dst, src).then_inc(M("router_in"), 16)
            ring.load(sp, ring.at["moe"] + NSLOT)
            sp.dma_start(m.X[:, 2:4, :], d["ctx"].rearrange("(t p) c -> p t c", p=P)).then_inc(M("ctx_in"), 16)
            sp.wait_ge(M("ctx_in"), 16)

        @block.tensor
        def _(pe):
            ident = m.const("ident")
            for i in range(4):
                t, half = i // 2, i % 2
                where = turn["t", i]
                banks.wait_free(pe, where)
                pe.wait_ge(M("y_ready"), t + 1)
                for k in range(4):
                    c = (4 * half + k) * P
                    last = nc.tensor.transpose(m.ps[:, where[0], k * P:(k + 1) * P], m.X[:, t, c:c + P], ident)
                banks.fill(last, where)
            pe.wait_ge(M("router_in"), 5 * 16)
            pe.wait_ge(M("yT_ready"), 4)
            for t in range(TT):
                where = small["logit", t]
                banks.wait_free(pe, where)
                pairs = [(x.yT[:, k, t * P:(t + 1) * P], x.router[:, k, :]) for k in range(KT)]
                pairs.append((m.const("ones")[0:1, :], x.router_b[0:1, :]))
                banks.fill(products(nc, m.ps[:, where[0], 0:NE], pairs), where)
            pe.wait_ge(M("gates_known"), TT)
            for t in range(TT):
                where = small["place", t]
                banks.wait_free(pe, where)
                pairs = [(m.const("ones"), x.chosen[:, s, :]) for s in range(t)] + [(m.const("upto"), x.chosen[:, t, :])]
                banks.fill(products(nc, m.ps[:, where[0], 0:NE], pairs), where)
            where = small["total"]
            banks.wait_free(pe, where)
            banks.fill(products(nc, m.ps[0:1, where[0], 0:NE], [(m.const("ones")[:, 0:1], x.chosen[:, t, :]) for t in range(TT)]), where)
            where = small["gT"]
            banks.wait_free(pe, where)
            for t in range(TT):
                last = nc.tensor.transpose(m.ps[0:NE, where[0], t * P:(t + 1) * P], x.gates[:, t, :], ident)
            banks.fill(last, where)

        @block.scalar
        def _(act):
            for i in range(4):
                t, half = i // 2, i % 2
                where = turn["t", i]
                banks.wait_full(act, where)
                ins = nc.scalar.activation(x.yT[:, 4 * half:4 * half + 4, t * P:(t + 1) * P],
                                           m.ps[:, where[0], :].rearrange("p (k c) -> p k c", k=4), ACT.Copy)
                banks.free_chained(act, ins, where)
                act.sem_inc(M("yT_ready"), 1)
            for t in range(TT):
                act.wait_ge(M("top_ready"), t + 1)
                nc.scalar.activation(x.exp[:, 0:TOPK], x.exp[:, 0:TOPK], ACT.Exp).then_inc(M("top_exp"), 1)

        @block.vector
        def _(dve):
            step = Chain(M, dve, "dve_step")
            iota = m.const("iota")[:, 0:NE]
            for t in range(TT):
                where = small["logit", t]
                banks.wait_full(dve, where)
                banks.free_chained(dve, nc.vector.tensor_copy(x.logits[:, t, :], m.ps[:, where[0], 0:NE]), where)
                top = x.top[:, t, :]
                step(nc.vector.max(top, x.logits[:, t, :]))
                step(nc.vector.max_index(x.top_at, top, x.logits[:, t, :]))
                step(nc.vector.tensor_copy(x.top_i[:, t, :], x.top_at))
                step(nc.vector.tensor_scalar(x.exp[:, 0:TOPK], top[:, 0:TOPK], top[:, 0:1], None, ALU.subtract), "top_ready")
                dve.wait_ge(M("top_exp"), t + 1)
                step(nc.vector.tensor_reduce(x.exp[:, 4:5], x.exp[:, 0:TOPK], axis=AX.X, op=ALU.add))
                step(nc.vector.reciprocal(x.exp[:, 5:6], x.exp[:, 4:5]))
                step(nc.vector.tensor_scalar(x.exp[:, 0:TOPK], x.exp[:, 0:TOPK], x.exp[:, 5:6], None, ALU.mult))
                for k in range(TOPK):
                    at, gate = x.top_i[:, t, k:k + 1], x.exp[:, k:k + 1]
                    if k == 0:
                        step(nc.vector.tensor_scalar(x.gates[:, t, :], iota, at, gate, ALU.is_equal, ALU.mult))
                        step(nc.vector.tensor_scalar(x.chosen[:, t, :], iota, at, None, ALU.is_equal))
                    else:
                        step(nc.vector.tensor_scalar(x.onehot, iota, at, gate, ALU.is_equal, ALU.mult))
                        step(nc.vector.tensor_tensor(x.gates[:, t, :], x.gates[:, t, :], x.onehot, ALU.add))
                        step(nc.vector.scalar_tensor_tensor(out=x.chosen[:, t, :], in0=iota, scalar=at, in1=x.chosen[:, t, :],
                                                            op0=ALU.is_equal, op1=ALU.add))
                dve.sem_inc(M("gates_known"), 1)
            step(nc.vector.memset(x.place, -1.0))
            for t in range(TT):
                where = small["place", t]
                banks.wait_full(dve, where)
                ins = nc.vector.tensor_tensor(x.place[:, t, 0:NE], m.ps[:, where[0], 0:NE], x.chosen[:, t, :], ALU.mult)
                banks.free_chained(dve, ins, where)
                step(nc.vector.tensor_scalar(x.place[:, t, 0:NE], x.place[:, t, 0:NE], -1.0, None, ALU.add))
            where = small["total"]
            banks.wait_full(dve, where)
            ins = nc.vector.tensor_reduce(x.total[0:1, NE:NE + 1], m.ps[0:1, where[0], 0:NE], axis=AX.X, op=ALU.max)
            banks.free_chained(dve, ins, where)
            step(nc.vector.tensor_copy(m.count[0:1, 0:1], x.total[0:1, NE:NE + 1]))
            where = small["gT"]
            banks.wait_full(dve, where)
            banks.free_chained(dve, nc.vector.tensor_copy(x.gatesT[0:NE, :], m.ps[0:NE, where[0], 0:T]), where)


def moe(nc, d, m, M, banks, ring):
    x = Experts(m)
    ch0 = ring.at["moe"]
    slot = [(ch0 + c) % NSLOT for c in range(PER_EXPERT)]
    nth = [(ch0 + c) // NSLOT for c in range(PER_EXPERT)]
    w = [m.ring[:, s, :].rearrange("p (k j) -> p k j", k=KT // 2) for s in slot]
    n0 = m.norms
    m.norms += TT
    load_base = [f"chunk_in{s}" for s in slot]
    used_base = [f"chunk_used{s}" for s in slot]
    more = range(1, PASSES)
    order = [2, 3, 0, 1]
    turned = banks.plan([(t, n) for t in order for n in range(2)], [4, 5, 6, 7, 0, 1, 2, 3])
    hT = m.part(0, KT, 4 * P)
    mods = [row(m, 0), row(m, 1), m.H[:, 0, :], m.H[:, 1, :]]

    def name(base, p):
        return base if p == 0 else base + "_more"

    def at(p, e, base=0):
        return e + base if p == 0 else (p - 1) * NE + e + base

    def primed(eng, p, *names):
        if p < 2:
            for n in names:
                eng.sem_inc(M(name(n, p)), 1)

    def picked(p, e, base=0):
        return e + base if p == 0 else (p - 1) * (NE + 1) + e + base

    def overflow(eng, body):
        count = eng.value_load(m.count[0:1, 0:1], min_val=0, max_val=T)
        with eng.If(count > SLOTS):
            for p in more:
                body(p)

    with nc.Block() as block:

        @block.sync
        def _(sp):
            load_rows(sp, M, m, [mod_row(d, 0, s, w) for s in range(2) for w in (SCALE1, SHIFT1)], mods)
            with sp.Fori(1, NE) as e:
                for c in range(PER_EXPERT):
                    sp.wait_ge(M(used_base[c]), e + nth[c])
                    sp.dma_start(m.ring[:, slot[c], :], d["moe"][bass.ds(e, 1), c, :, :].rearrange("e p j -> (e p) j"))\
                        .then_inc(M(load_base[c]), 16)
            ring.sent = ch0 + PER_EXPERT * NE

            def body(p):
                if p == 1:
                    for c in range(PER_EXPERT):
                        sp.wait_ge(M(used_base[c]), NE + nth[c])
                with sp.Fori(0, NE) as e:
                    for c in range(PER_EXPERT):
                        sp.wait_ge(M(f"more_used{c}"), e + ((p - 1) * NE + 1))
                        sp.dma_start(m.ring[:, slot[c], :], d["moe"][bass.ds(e, 1), c, :, :].rearrange("e p j -> (e p) j"))\
                            .then_inc(M(f"more_in{c}"), 16)
                if p == PASSES - 1:
                    for c in range(PER_EXPERT):
                        sp.wait_ge(M(f"more_used{c}"), (PASSES - 1) * NE + 1)

            overflow(sp, body)
            ring.load(sp, ch0 + PER_EXPERT * NE + NSLOT)

        @block.tensor
        def _(pe):
            acc = [m.ps[:, 2 * t + n, :] for t in range(TT) for n in range(2)]
            for i in range(4):
                t, n = i // 2, i % 2
                nc.tensor.matmul(acc[i], x.gatesT[0:NE, t * P:(t + 1) * P], x.b_down[0:NE, n * 512:(n + 1) * 512],
                                 start=True, stop=False, skip_group_check=True)

            def gather(p, count):
                pe.wait_ge(M(name("pick_ready", p)), count)
                for k in range(KT):
                    for t in range(TT):
                        last = nc.tensor.matmul(m.ps[:, 7, k * SLOTS:(k + 1) * SLOTS], m.X[:, t, k * P:(k + 1) * P],
                                                x.pick[:, t, :], start=t == 0, stop=t == TT - 1)
                last.then_inc(M(name("gather_done", p)), 1)

            def scatter():
                for n in range(2):
                    rows = slice(n * SLOTS, (n + 1) * SLOTS)
                    for t in range(TT):
                        last = nc.tensor.matmul(acc[2 * t + n], x.weighT[rows, t * P:(t + 1) * P], x.ye[rows, :],
                                                start=False, stop=False, skip_group_check=True)
                return last

            def halves(bank, c, lhs, first):
                for k in range(KT // 2):
                    for n in range(2):
                        last = nc.tensor.matmul(m.ps[n * SLOTS:(n + 1) * SLOTS, bank, :], lhs(k + KT // 2 * (c % 2), n),
                                                w[c][:, k, n * 512:(n + 1) * 512],
                                                start=first and k == 0, stop=c % 2 == 1 and k == KT // 2 - 1, skip_group_check=True)
                return last

            def one_pass(p):
                arrived = lambda c, e: pe.wait_ge(M(load_base[c] if p == 0 else f"more_in{c}"),
                                                  16 * (e + nth[c] + 1) if p == 0 else 16 * (at(p, e) + 1))
                used = lambda ins, c: ins.then_inc(M(used_base[c] if p == 0 else f"more_used{c}"), 1)
                primed(pe, p, "added", "weigh_turned")
                if p == 1:
                    for c in range(PER_EXPERT):
                        pe.sem_inc(M(f"more_used{c}"), 1)
                gather(p, picked(p, 0, 1))
                with pe.Fori(0, NE) as e:
                    pe.wait_ge(M(name("select_ready", p)), picked(p, e, 1))
                    pe.wait_ge(M(name("xe_ready", p)), picked(p, e, 1))
                    for c in range(4):
                        bank = 4 + c // 2
                        if c % 2 == 0:
                            pe.wait_ge(M(name(("weighT_ready", "h_ready")[c // 2], p)), at(p, e, 1))
                            for n in range(2):
                                nc.tensor.matmul(m.ps[n * SLOTS:(n + 1) * SLOTS, bank, :],
                                                 x.select[0:NE, :],
                                                 (x.b_gate, x.b_up)[c // 2][0:NE, n * 512:(n + 1) * 512],
                                                 start=True, stop=False, skip_group_check=True)
                        arrived(c, e)
                        used(halves(bank, c, lambda k, n: x.xe[:, k, :], False), c)
                    gather(p, picked(p, e, 2))
                    pe.wait_ge(M(name("h_ready", p)), at(p, e, 2))
                    pe.wait_ge(M(name("ye_ready", p)), at(p, e, 1))
                    for j in range(4):
                        last = nc.tensor.transpose(m.ps[:, 6, j * P:(j + 1) * P], x.h[:, j * P:(j + 1) * P], m.const("ident"))
                    last.then_inc(M(name("h_turned", p)), 1)
                    last = scatter()
                    last.then_inc(M(name("added", p)), 1)
                    pe.wait_ge(M(name("weigh_ready", p)), at(p, e, 1))
                    for t in range(TT):
                        last = nc.tensor.matmul(m.ps[:, 4, t * P:(t + 1) * P], x.weigh[:, t, :], m.const("ident"), start=True, stop=True)
                    last.then_inc(M(name("weigh_turned", p)), 1)
                    pe.wait_ge(M(name("hT_ready", p)), at(p, e, 1))
                    for c in (4, 5):
                        arrived(c, e)
                        used(halves(6, c, lambda k, n: x.hT[:, k % 4, k // 4, :], c == 4), c)
                pe.wait_ge(M(name("xe_ready", p)), picked(p, NE, 1))
                pe.wait_ge(M(name("weighT_ready", p)), at(p, NE, 1))
                pe.wait_ge(M(name("ye_ready", p)), at(p, NE, 1))

            pe.wait_ge(M("scatter_clear"), 1)
            one_pass(0)
            overflow(pe, one_pass)
            scatter()
            for i in range(4):
                last = nc.tensor.matmul(acc[i], m.const("zero"), x.xe.rearrange("p a b -> p (a b)"), start=False, stop=True, skip_group_check=True)
            last.then_inc(M("sums_done"), 1)
            for n, t in enumerate(order):
                turn_h(nc, pe, m, M, banks, turned, t, n + 1)

        @block.scalar
        def _(act):
            def xe_out(p, count):
                act.wait_ge(M(name("gather_done", p)), count)
                nc.scalar.activation(x.xe.rearrange("p a b -> p (a b)"), m.ps[:, 7, :], ACT.Copy).then_inc(M(name("xe_ready", p)), 1)

            def one_pass(p):
                primed(act, p, "weighT_ready", "ye_ready")
                xe_out(p, picked(p, 0, 1))
                with act.Fori(0, NE) as e:
                    act.wait_ge(M(name("g_ready", p)), at(p, e, 1))
                    nc.scalar.activation(x.sig, x.g, ACT.Sigmoid, scale=SW_ALPHA).then_inc(M(name("sig_ready", p)), 1)
                    xe_out(p, picked(p, e, 2))
                    act.wait_ge(M(name("h_turned", p)), at(p, e, 1))
                    nc.scalar.activation(x.hT.rearrange("p a b c -> p (a b c)"), m.ps[:, 6, :], ACT.Copy).then_inc(M(name("hT_ready", p)), 1)
                    act.wait_ge(M(name("added", p)), at(p, e, 2))
                    act.wait_ge(M(name("weigh_turned", p)), at(p, e, 2))
                    nc.scalar.activation(x.weighT, m.ps[:, 4, 0:T], ACT.Copy).then_inc(M(name("weighT_ready", p)), 1)
                    act.wait_ge(M(used_base[5] if p == 0 else "more_used5"), e + nth[5] + 1 if p == 0 else at(p, e, 2))
                    nc.scalar.activation(x.ye, m.ps[:, 6, :], ACT.Copy).then_inc(M(name("ye_ready", p)), 1)

            one_pass(0)
            overflow(act, one_pass)
            for t in order[0:2]:
                hT_out(nc, act, m, banks, turned, hT, t)
            for t in range(TT):
                norm_act(nc, act, m, M, n0 + t + 1)
            for t in order[2:4]:
                hT_out(nc, act, m, banks, turned, hT, t)

        @block.vector
        def _(dve):
            step = Chain(M, dve, "dve_step")
            iota = m.const("iota")
            step(nc.vector.memset(x.ye, 0.0))
            step(nc.vector.memset(x.weighT, 0.0), "scatter_clear")

            def pick(p, e):
                for t in range(TT):
                    last = nc.vector.tensor_scalar(x.pick[:, t, :], iota[:, 0:SLOTS], x.place[:, t, bass.ds(e, 1)], None, ALU.is_equal)
                last.then_inc(M(name("pick_ready", p)), 1)

            def select(p, e):
                nc.vector.tensor_copy(x.select[0:NE, :], m.const("ident")[0:NE, bass.ds(e, 1)].to_broadcast([NE, SLOTS]))\
                    .then_inc(M(name("select_ready", p)), 1)

            def weigh(p, e):
                for t in range(TT):
                    last = nc.vector.tensor_scalar(x.weigh[:, t, :], iota, x.place[:, t, bass.ds(e, 1)], x.gates[:, t, bass.ds(e, 1)],
                                                   ALU.is_equal, ALU.mult)
                last.then_inc(M(name("weigh_ready", p)), 1)

            def one_pass(p):
                if p:
                    before = p - 1
                    dve.wait_ge(M(name("weigh_ready", before)), at(before, NE))
                    dve.wait_ge(M(name("weigh_turned", before)), at(before, NE, 1))
                    dve.wait_ge(M(name("pick_ready", before)), picked(before, NE, 1))
                    dve.wait_ge(M(name("gather_done", before)), picked(before, NE, 1))
                    nc.vector.tensor_scalar(x.place, x.place, -float(SLOTS), None, ALU.add).then_inc(M("shifted_more"), 1)
                    dve.wait_ge(M("shifted_more"), p)
                primed(dve, p, "h_ready")
                pick(p, 0)
                select(p, 0)
                with dve.Fori(0, NE) as e:
                    dve.wait_ge(M(name("gather_done", p)), picked(p, e, 1))
                    pick(p, e + 1)
                    dve.wait_ge(M(used_base[1] if p == 0 else "more_used1"), e + nth[1] + 1 if p == 0 else at(p, e, 2))
                    dve.wait_ge(M(name("h_ready", p)), at(p, e, 1))
                    nc.vector.tensor_scalar(x.g, m.ps[:, 4, :], LIMIT, None, ALU.min).then_inc(M(name("g_ready", p)), 1)
                    dve.wait_ge(M(name("weigh_turned", p)), at(p, e, 1))
                    weigh(p, e)
                    dve.wait_ge(M(name("g_ready", p)), at(p, e, 1))
                    dve.wait_ge(M(name("sig_ready", p)), at(p, e, 1))
                    nc.vector.tensor_tensor(x.g, x.g, x.sig, ALU.mult).then_inc(M(name("gs_ready", p)), 1)
                    dve.wait_ge(M(used_base[3] if p == 0 else "more_used3"), e + nth[3] + 1 if p == 0 else at(p, e, 2))
                    nc.vector.tensor_scalar(x.u, m.ps[:, 5, :], LIMIT, -LIMIT, ALU.min, ALU.max).then_inc(M(name("u_ready", p)), 1)
                    dve.wait_ge(M(name("gs_ready", p)), at(p, e, 1))
                    dve.wait_ge(M(name("u_ready", p)), at(p, e, 1))
                    nc.vector.scalar_tensor_tensor(out=x.h, in0=x.u, scalar=1.0, in1=x.g, op0=ALU.add, op1=ALU.mult)\
                        .then_inc(M(name("h_ready", p)), 1)
                    select(p, e + 1)

            one_pass(0)
            overflow(dve, one_pass)
            dve.wait_ge(M("rows_in"), m.rows_sent)
            for t in order[0:2]:
                modulate_tile(nc, step, m, t, mods[2], mods[3])
            dve.wait_ge(M("sums_done"), 1)
            for t in range(TT):
                X = m.X[:, t, :]
                step(nc.vector.scalar_tensor_tensor(out=X, in0=X, scalar=ALPHA1,
                                                    in1=m.ps[:, 2 * t:2 * t + 2, :].rearrange("p a b -> p (a b)"), op0=ALU.mult, op1=ALU.add))
                norm_dve(nc, dve, step, m, M, X, n0 + t + 1)
                step(nc.vector.tensor_tensor(X, X, row(m, 2), ALU.mult))
                step(nc.vector.tensor_tensor(X, X, row(m, 3), ALU.add))
                modulate_tile(nc, step, m, t, mods[0], mods[1])



def mod_row(d, layer, stream, which):
    return d["mod"][layer, stream:stream + 1, which * D:(which + 1) * D]


def residual_tile(nc, dve, step, m, M, banks, sums, t, n, gate, g, b):
    X, tmp = m.X[:, t, :], m.H[:, t, :]
    banks.wait_full(dve, sums[t, 0])
    banks.wait_full(dve, sums[t, 1])
    for half in range(2):
        where = sums[t, half]
        cols = slice(half * 512, (half + 1) * 512)
        ins = nc.vector.tensor_tensor(tmp[:, cols], m.ps[:, where[0], :], gate[:, cols], ALU.mult)
        banks.free_chained(dve, ins, where)
    step(nc.vector.scalar_tensor_tensor(out=X, in0=X, scalar=ALPHA2, in1=tmp, op0=ALU.mult, op1=ALU.add))
    norm_dve(nc, dve, step, m, M, X, n)
    step(nc.vector.tensor_tensor(X, X, g, ALU.mult))
    step(nc.vector.tensor_tensor(X, X, b, ALU.add), "x_done")


def modulate_tile(nc, step, m, t, scale, shift):
    step(nc.vector.tensor_tensor(m.H[:, t, :], m.X[:, t, :], scale, ALU.mult))
    step(nc.vector.tensor_tensor(m.H[:, t, :], m.H[:, t, :], shift, ALU.add), "h_ready_now")


def turn_h(nc, pe, m, M, banks, plan, t, count):
    pe.wait_ge(M("h_ready_now"), count)
    for n in range(2):
        where = plan[t, n]
        banks.wait_free(pe, where)
        for k in range(4):
            last = nc.tensor.transpose(m.ps[:, where[0], k * P:(k + 1) * P],
                                       m.H[:, t, (4 * n + k) * P:(4 * n + k + 1) * P], m.const("ident"))
        banks.fill(last, where)


def hT_out(nc, act, m, banks, plan, hT, t):
    for n in range(2):
        where = plan[t, n]
        banks.wait_full(act, where)
        banks.free(nc.scalar.activation(hT[:, 4 * n:4 * n + 4, t * P:(t + 1) * P],
                                        m.ps[:, where[0], :].rearrange("p (k c) -> p k c", k=4), ACT.Copy), where)



def chunk_mlp(nc, d, m, M, banks, ring):
    tiles = 4
    hT = m.part(0, KT, tiles * P)
    u = m.part(4096, tiles, D)
    v = m.part(8192, tiles, D)
    w_s = m.H[:, 0, :].rearrange("p (h c) -> p h c", h=8)
    b_s = m.H[:, 1, 0:8]
    tmp = m.H[:, 2, :]
    n0 = m.norms
    m.norms += 2 * tiles
    ends = [m.part(8192 + i * D, D) for i in range(4)]
    mods = [m.part(12288 + i * D, D) for i in range(4)]
    new_hT = m.part(4096, KT, tiles * P)
    norm_rows = m.rows_sent + 32
    base = M.n.get("h_ready_now", 0)
    z = banks.plan([(n, t) for n in range(4) for t in range(tiles)], list(range(8)))
    mixed = banks.plan([(t, n) for t in range(tiles) for n in range(2)], list(range(8)))
    turned = banks.plan([(t, n) for t in range(tiles) for n in range(2)], list(range(8)))
    sums = banks.plan([(t, n) for t in range(tiles) for n in range(2)], list(range(8)))
    back = banks.plan([(t, n) for t in range(tiles) for n in range(2)], list(range(8)))
    with nc.Block() as block:

        @block.sync
        def _(sp):
            sp.dma_start(w_s, d["a_w_s"]).then_inc(M("mlp_in"), 16)
            sp.dma_start(b_s, d["a_b_s"]).then_inc(M("mlp_in"), 16)
            load_rows(sp, M, m, [d["a_norm"][i:i + 1, :] for i in range(2)])
            sp.wait_ge(M("gated_ready"), tiles)
            load_rows(sp, M, m, residual_rows(d, 0, 0, GATE1, 2), ends)
            load_rows(sp, M, m, [mod_row(d, 0, s, w) for s in range(2) for w in (SCALE2, SHIFT2)], mods)
            ring.load(sp, ring.at["w_q0"] + 2 + NSLOT - FREE_SLOTS)

        @block.tensor
        def _(pe):
            for n in range(4):
                w = ring.wait(pe, "a_w_in", n)
                for t in range(tiles):
                    where = z[n, t]
                    banks.wait_free(pe, where)
                    last = products(nc, m.ps[:, where[0], :], [(hT[:, k, t * P:(t + 1) * P], w[:, k, :]) for k in range(KT)])
                    banks.fill(last, where)
                pe.wait_ge(M(f"bank_full{where[0]}"), where[1] + 1)
                pe.sem_inc(M(f"chunk_used{(ring.at['a_w_in'] + n) % NSLOT}"), 1)
            pe.wait_ge(M("mlp_in"), 32)
            for t in range(tiles):
                pe.wait_ge(M("v_normed"), t + 1)
                for n in range(2):
                    where = mixed[t, n]
                    banks.wait_free(pe, where)
                    for k in range(4):
                        head = 4 * n + k
                        last = nc.tensor.matmul(m.ps[:, where[0], k * P:(k + 1) * P], w_s[:, head, :],
                                                v[:, t, head * P:(head + 1) * P], start=True, stop=True)
                    banks.fill(last, where)
            for t in range(tiles):
                pe.wait_ge(M("gated_ready"), t + 1)
                for n in range(2):
                    where = turned[t, n]
                    banks.wait_free(pe, where)
                    for k in range(4):
                        c = (4 * n + k) * P
                        last = nc.tensor.transpose(m.ps[:, where[0], k * P:(k + 1) * P], u[:, t, c:c + P], m.const("ident"))
                    banks.fill(last, where)
            pe.wait_ge(M("gatedT_ready"), 2 * tiles)
            w = [ring.wait(pe, "a_w_out", n) for n in range(2)]
            for t in range(tiles):
                for n in range(2):
                    where = sums[t, n]
                    banks.wait_free(pe, where)
                    last = products(nc, m.ps[:, where[0], :], [(hT[:, k, t * P:(t + 1) * P], w[n][:, k, :]) for k in range(KT)])
                    banks.fill(last, where)
                if t >= 2:
                    turn_h(nc, pe, m, M, banks, back, t - 2, base + t - 1)
            for n in range(2):
                pe.wait_ge(M(f"bank_full{sums[tiles - 1, n][0]}"), sums[tiles - 1, n][1] + 1)
                pe.sem_inc(M(f"chunk_used{(ring.at['a_w_out'] + n) % NSLOT}"), 1)
            for t in range(tiles - 2, tiles):
                turn_h(nc, pe, m, M, banks, back, t, base + t + 1)

        @block.scalar
        def _(act):
            def gelu(n, t):
                where = z[n, t]
                banks.wait_full(act, where)
                dst = (v if n < 2 else u)[:, t, (n % 2) * 512:(n % 2) * 512 + 512]
                banks.free_chained(act, nc.scalar.activation(dst, m.ps[:, where[0], :], ACT.Gelu_apprx_tanh), where)
                act.sem_inc(M("z_ready"), 1)

            for n in range(2):
                for t in range(tiles):
                    gelu(n, t)
            for t in range(tiles):
                norm_act(nc, act, m, M, n0 + t + 1)
            for n in range(2, 4):
                for t in range(tiles):
                    gelu(n, t)
            for t in range(tiles):
                for n in range(2):
                    where = turned[t, n]
                    banks.wait_full(act, where)
                    ins = nc.scalar.activation(hT[:, 4 * n:4 * n + 4, t * P:(t + 1) * P],
                                               m.ps[:, where[0], :].rearrange("p (k c) -> p k c", k=4), ACT.Copy)
                    banks.free_chained(act, ins, where)
                    act.sem_inc(M("gatedT_ready"), 1)
            for t in range(tiles):
                norm_act(nc, act, m, M, n0 + tiles + t + 1)
                if t >= 2:
                    hT_out(nc, act, m, banks, back, new_hT, t - 2)
            for t in range(tiles - 2, tiles):
                hT_out(nc, act, m, banks, back, new_hT, t)

        @block.vector
        def _(dve):
            step = Chain(M, dve, "dve_step")
            dve.wait_ge(M("rows_in"), norm_rows)
            dve.wait_ge(M("mlp_in"), 32)
            for t in range(tiles):
                dve.wait_ge(M("z_ready"), tiles + t + 1)
                V = v[:, t, :]
                norm_dve(nc, dve, step, m, M, V, n0 + t + 1)
                step(nc.vector.tensor_tensor(V, V, row(m, 0), ALU.mult))
                step(nc.vector.tensor_tensor(V, V, row(m, 1), ALU.add), "v_normed")
            for t in range(tiles):
                dve.wait_ge(M("z_ready"), 3 * tiles + t + 1)
                for n in range(2):
                    where = mixed[t, n]
                    banks.wait_full(dve, where)
                    half = slice(n * 512, (n + 1) * 512)
                    bias = b_s[:, 4 * n:4 * n + 4].rearrange("p (h c) -> p h c", c=1).to_broadcast([P, 4, P])
                    ins = nc.vector.tensor_tensor(tmp[:, half].rearrange("p (h c) -> p h c", h=4),
                                                  m.ps[:, where[0], :].rearrange("p (h c) -> p h c", h=4), bias, ALU.add)
                    banks.free_chained(dve, ins, where)
                step(nc.vector.tensor_tensor(u[:, t, :], u[:, t, :], tmp, ALU.mult), "gated_ready")
            dve.wait_ge(M("rows_in"), m.rows_sent)
            for t in range(tiles):
                residual_tile(nc, dve, step, m, M, banks, sums, t, n0 + tiles + t + 1, ends[t // 2], ends[2], ends[3])
                modulate_tile(nc, step, m, t, mods[2 * (t // 2)], mods[2 * (t // 2) + 1])



PAIRS = PH // 2
SCORES = 4 * NKEY
FREE_SLOTS = 5


class PeerPlace:

    def __init__(self, m, layer):
        slot = lambda n: m.ring[:, n, :]
        tiles = 4 if layer == 0 else 2
        self.ends = [slot(1)[:, i * D:(i + 1) * D] for i in range(4)]
        first, scratch = (3, 2) if layer == 0 else (4, 0)
        size = (tiles * PAIRS + 1) * SCORES
        self.scores = m.ring[:, first:NSLOT, :].rearrange("p a b -> p (a b)")[:, 0:size]
        self.scratch = slot(scratch)
        if layer == 0:
            self.mods = [slot(5)[:, SCORES + i * D:SCORES + (i + 1) * D] for i in range(3)] + [slot(2)[:, SLOT - D:SLOT]]


def scores(nc, d, m, M, banks, ring, layer, tiles):
    tok = tiles * P
    hT = m.part(4096, KT, tok)
    qT = m.part(0, PH, tok)
    keys = m.part(8192, NKEY)
    place = PeerPlace(m, layer)
    out = place.scores
    searched = (0, 4)[layer] * PAIRS + layer
    q = banks.plan([("q", h) for h in range(PH)], [0, 1, 2, 3])
    groups = [(t, p, i) for t in range(tiles) for i in range(2) for p in range(2)]
    early, late = groups[:2], groups[2:]
    sc = banks.plan(groups, [4, 5, 6, 7])
    L = f"_{layer}"
    with nc.Block() as block:

        @block.sync
        def _(sp):
            sp.dma_start(keys, d["keys"][layer]).then_inc(M("keys_in"), 16)
            ring.load(sp, ring.at[f"w_q{layer}"] + 2 + NSLOT - FREE_SLOTS)

        @block.tensor
        def _(pe):
            def score(t, p, i):
                where = sc[t, p, i]
                banks.wait_free(pe, where)
                rows_ = slice(p * HD, (p + 1) * HD)
                for k in range(4):
                    last = nc.tensor.matmul(m.ps[:, where[0], k * P:(k + 1) * P], qT[rows_, 4 * i + k, t * P:(t + 1) * P],
                                            keys[rows_, :], start=True, stop=True)
                banks.fill(last, where)

            for h in range(PH):
                if h % 4 == 0:
                    w = ring.wait(pe, f"w_q{layer}", h // 4)
                where = q["q", h]
                banks.wait_free(pe, where)
                j = h % 4
                last = products(nc, m.ps[:, where[0], 0:tok], [(w[:, k, j * P:(j + 1) * P], hT[:, k, :]) for k in range(KT)])
                banks.fill(last, where)
                if j == 3:
                    pe.wait_ge(M(f"bank_full{where[0]}"), where[1] + 1)
                    pe.sem_inc(M(f"chunk_used{(ring.at[f'w_q{layer}'] + h // 4) % NSLOT}"), 1)
                if h == 4:
                    pe.wait_ge(M("qT_ready" + L), 4)
                    pe.wait_ge(M("keys_in"), 16 * (layer + 1))
                    for group in early:
                        score(*group)
            pe.wait_ge(M("qT_ready" + L), PH)
            for group in late:
                score(*group)

        @block.scalar
        def _(act):
            by_pair = out[:, 0:tiles * PAIRS * SCORES].rearrange("p (i a k) -> p i a k", a=2, k=SCORES // 2)
            top = Search(nc, None, m, M, None, place).top

            def score_out(t, p, i):
                where = sc[t, p, i]
                banks.wait_full(act, where)
                pair = t * PAIRS + 2 * i
                banks.free(nc.scalar.activation(by_pair[:, pair:pair + 2, p, :], m.ps[:, where[0], :].rearrange("p (i k) -> p i k", i=2),
                                                ACT.Copy), where)

            for h in range(PH):
                where = q["q", h]
                banks.wait_full(act, where)
                banks.free_chained(act, nc.scalar.activation(qT[:, h, :], m.ps[:, where[0], 0:tok], ACT.Copy), where)
                act.sem_inc(M("qT_ready" + L), 1)
                if h == 4:
                    for group in early:
                        score_out(*group)
            for group in late:
                score_out(*group)
            act.wait_ge(M("peer_top"), searched + 1)
            nc.scalar.activation(top, top, ACT.Exp).then_inc(M("peer_exp"), 1)

        @block.vector
        def _(dve):
            for group in early:
                where = sc[group]
                dve.wait_ge(M(f"bank_free{where[0]}"), where[1] + 1)
            head = Search(nc, dve, m, M, lambda n: searched * SEARCH_STEPS + n, place)
            for n in range(SEARCH_END + 1):
                head.stage(n, slice(0, SCORES), searched + 1)
            dve.wait_ge(M("qT_ready" + L), PH)
            at = tiles * PAIRS * SCORES
            nc.vector.memset(out[:, at:at + SCORES], 0.0).then_inc(M("list_ended"), 1)
            dve.wait_ge(M("list_ended"), layer + 1)


class Search:

    def __init__(self, nc, dve, m, M, total, place):
        self.nc, self.dve, self.m, self.M, self.n, self.total, self.place = nc, dve, m, M, 0, total, place
        at = 0

        def part(size):
            nonlocal at
            at += size
            return place.scratch[:, at - size:at]

        self.s = part(SCORES).rearrange("p (r k) -> p r k", r=4)
        self.rest = part(SCORES).rearrange("p (r k) -> p r k", r=4)
        self.best = part(4 * PK).rearrange("p (r k) -> p r k", r=4)
        self.best_at = part(4 * PK).bitcast(U32).rearrange("p (r k) -> p r k", r=4)
        self.best_i = part(4 * PK).rearrange("p (r k) -> p r k", r=4)
        self.sums = part(2 * PK * PK)
        self.sums_rest = part(2 * PK * PK).rearrange("p (h k) -> p h k", h=2)
        self.top = part(2 * PK).rearrange("p (h k) -> p h k", h=2)
        self.top_at = part(2 * PK).bitcast(U32).rearrange("p (h k) -> p h k", h=2)
        self.part_at = part(2 * PK).bitcast(U32)
        self.parts = part(4 * PK).rearrange("p (n k) -> p n k", n=2)
        self.found = part(4 * PK).rearrange("p (n k) -> p n k", n=2)
        self.hit = part(2 * PK * PK)
        self.z = part(4)
        assert at <= SLOT - D

    def each(self, instructions):
        for ins in instructions:
            ins.then_inc(self.M("search_step"), 1)
            self.n += 1
        self.dve.wait_ge(self.M("search_step"), self.total(self.n))

    def stage(self, n, scores_at, exp_count):
        v = self.nc.vector
        s, rest, best, best_at, top, top_at = self.s, self.rest, self.best, self.best_at, self.top, self.top_at
        sums = self.sums.rearrange("p (h k) -> p h k", h=2)
        if n == 0:
            self.each([v.tensor_copy(s.rearrange("p r k -> p (r k)"), self.place.scores[:, scores_at])])
        elif n == 1:
            self.each([v.max(best[:, r, 0:8], s[:, r, :]) for r in range(4)])
        elif n == 2:
            self.each([v.max_index(best_at[:, r, 0:8], best[:, r, 0:8], s[:, r, :]) for r in range(4)])
        elif n == 3:
            self.each([v.match_replace(out=rest[:, r, :], in_to_replace=best[:, r, 0:8], in_values=s[:, r, :], imm_value=LOWEST)
                       for r in range(4)])
        elif n == 4:
            self.each([v.max(best[:, r, 8:16], rest[:, r, :]) for r in range(4)])
        elif n == 5:
            self.each([v.max_index(best_at[:, r, 8:16], best[:, r, 8:16], rest[:, r, :]) for r in range(4)])
        elif n == 6:
            four = best.rearrange("p (a h) k -> p a h k", a=2)
            first = four[:, 0, :, :].rearrange("p h (k o) -> p h k o", o=1).to_broadcast([P, 2, PK, PK])
            second = four[:, 1, :, :].rearrange("p h (o k) -> p h o k", o=1).to_broadcast([P, 2, PK, PK])
            self.each([v.tensor_copy(self.best_i, best_at),
                       v.tensor_tensor(self.sums.rearrange("p (h a b) -> p h a b", h=2, a=PK), first, second, ALU.add)])
        elif n == 7:
            self.each([v.max(top[:, h, 0:8], sums[:, h, :]) for h in range(2)])
        elif n == 8:
            self.each([v.max_index(top_at[:, h, 0:8], top[:, h, 0:8], sums[:, h, :]) for h in range(2)])
        elif n == 9:
            self.each([v.match_replace(out=self.sums_rest[:, h, :], in_to_replace=top[:, h, 0:8], in_values=sums[:, h, :],
                                       imm_value=LOWEST) for h in range(2)])
        elif n == 10:
            self.each([v.max(top[:, h, 8:16], self.sums_rest[:, h, :]) for h in range(2)])
        elif n == 11:
            self.each([v.max_index(top_at[:, h, 8:16], top[:, h, 8:16], self.sums_rest[:, h, :]) for h in range(2)])
        elif n in (12, 13):
            op, by = ((ALU.logical_shift_right, 4), (ALU.bitwise_and, 15))[n - 12]
            self.each([v.tensor_scalar(self.part_at, top_at.rearrange("p h k -> p (h k)"), by, None, op)])
            self.each([v.tensor_copy(self.parts[:, n - 12, :], self.part_at)])
        elif n in (14, 15):
            half, rows_ = n - 14, 2 * PK
            at = self.parts[:, half, :].rearrange("p (r o) -> p r o", o=1).to_broadcast([P, rows_, PK])
            hit = self.hit.rearrange("p (r j) -> p r j", j=PK)
            iota = self.m.const("iota")[:, 0:PK].rearrange("p (o j) -> p o j", o=1)
            self.each([v.tensor_tensor(hit, at, iota.to_broadcast([P, rows_, PK]), ALU.is_equal)])
            keys_i = self.best_i[:, 2 * half:2 * half + 2, :].rearrange("p h (o k) -> p h o k", o=1).to_broadcast([P, 2, PK, PK])
            hit4 = self.hit.rearrange("p (h k j) -> p h k j", h=2, j=PK)
            self.each([v.tensor_tensor(hit4, hit4, keys_i, ALU.mult)])
            self.each([v.tensor_reduce(self.found[:, half, :], hit, axis=AX.X, op=ALU.add)])
        elif n == 16:
            z3 = self.z.rearrange("p (a h o) -> p a h o", a=2, o=1)
            self.each([v.tensor_copy(self.z[:, 0:2], top[:, :, 0])])
            v.tensor_tensor(top, top, z3[:, 0, :, :].to_broadcast([P, 2, PK]), ALU.subtract).then_inc(self.M("peer_top"), 1)
        elif n == 17:
            self.dve.wait_ge(self.M("peer_exp"), exp_count)
            self.each([v.tensor_reduce(self.z[:, 0:2], top, axis=AX.X, op=ALU.add)])
            self.each([v.reciprocal(self.z[:, 2:4], self.z[:, 0:2])])
        elif n == 18:
            z3 = self.z.rearrange("p (a h o) -> p a h o", a=2, o=1)
            self.each([v.tensor_tensor(self.m.wts[:, 2 * PK:4 * PK].rearrange("p (h k) -> p h k", h=2), top,
                                       z3[:, 1, :, :].to_broadcast([P, 2, PK]), ALU.mult)])
        elif n == 19:
            self.each([v.scalar_tensor_tensor(out=self.m.idx, in0=self.found[:, 0, :], scalar=float(NKEY), in1=self.found[:, 1, :],
                                              op0=ALU.mult, op1=ALU.add)])


SEARCH_END = 19
SEARCH_STEPS = 1 + 4 * 5 + 2 + 2 * 5 + 4 + 6 + 1 + 2 + 1 + 1


BUFS, LOT = 8, 4


def peer(nc, d, m, M, banks, layer, tiles, first, out_dram=None):
    n0 = m.norms
    m.norms += tiles
    streams = tiles // 2
    place = PeerPlace(m, layer)
    rows = place.ends
    x_base = M.n.get("x_done", 0)
    u_buf = [m.part(b * D, D) for b in range(BUFS)]
    v_buf = [m.part((BUFS + b) * D, D) for b in range(BUFS)]
    cur = [m.cur_idx[:, 0:PK], m.cur_idx[:, PK:2 * PK]]
    sums = banks.plan([(t, n) for t in range(tiles) for n in range(2)], list(range(2 * tiles)))
    pairs = PH // 2
    slots = PH * PK

    with nc.Block() as block:

        @block.sync
        def _(sp):
            load_rows(sp, M, m, residual_rows(d, layer, 1, GATE2, streams), rows)
            if layer == 0:
                load_rows(sp, M, m, [mod_row(d, 1, s, w) for s in range(2) for w in (SCALE1, SHIFT1)], place.mods)
            if out_dram is not None:
                view = out_dram.rearrange("a (t p) c -> p (a t) c", p=P)
                for t in range(tiles):
                    sp.wait_ge(M("x_done"), x_base + t + 1)
                    sp.dma_start(view[:, t, :], m.X[:, t, :]).then_inc(M("stored"), 16)
                sp.wait_ge(M("stored"), 16 * tiles)

        @block.gpsimd
        def _(pool):
            for t in range(tiles):
                with pool.Fori(0, pairs) as i:
                    for hh in range(2):
                        done = i * 2 * PK + ((first + t) * slots + hh * PK)
                        pool.wait_ge(M("idx_ready"), i * 2 + ((first + t) * PH + layer + hh + 1))
                        for lot in range(PK // LOT):
                            for table, bufs, free, arrived in ((d[f"u{layer}"], u_buf, "u_free", "u_in"),
                                                               (d[f"v{layer}"], v_buf, "v_free", "v_in")):
                                for j in range(LOT):
                                    k = lot * LOT + j
                                    b = k % BUFS
                                    pool.wait_ge(M(free), done + k + 1)
                                    pool.sem_inc(M("gather_ticket"), 1)
                                    pool.indirect_dma_start(bufs[b], None, table, bass.IndirectOffsetOnAxis(cur[hh][:, k:k + 1], 0))\
                                        .then_inc(M(f"{arrived}{b}"), 16)

        @block.vector
        def _(dve):
            def arrivals(t, i, hh, k):
                return 16 * (((first + t) * slots + hh * PK + k) // BUFS + 1) + i * (16 * 2 * PK // BUFS)

            if first == 0:
                dve.sem_inc(M("u_free"), BUFS)
            searched = first * PAIRS + layer
            nc.vector.tensor_copy(m.wts[:, 0:2 * PK], m.wts[:, 2 * PK:4 * PK]).then_inc(M("wts_moved"), 1)
            nc.vector.tensor_copy(cur[0], m.idx[:, 0:PK]).then_inc(M("idx_ready"), 1)
            dve.wait_ge(M("wts_moved"), searched + 1)
            dve.wait_ge(M("rows_in"), m.rows_sent)
            step = Chain(M, dve, "dve_step")

            def finish(t):
                residual_tile(nc, dve, step, m, M, banks, sums, t, n0 + t + 1, rows[t // 2], rows[streams], rows[streams + 1])
                if layer == 0:
                    modulate_tile(nc, step, m, t, place.mods[2 * (t // 2)], place.mods[2 * (t // 2) + 1])

            for t in range(tiles):
                if t:
                    finish(t - 1)
                with dve.Fori(0, pairs) as i:
                    done = searched + t * PAIRS + 1
                    following = Search(nc, dve, m, M, lambda n: i * SEARCH_STEPS + (done * SEARCH_STEPS + n), place)

                    def stage(n):
                        following.stage(n, bass.ds(i * SCORES + (t * PAIRS + 1) * SCORES, SCORES), i + (done + 1))

                    for hh in range(2):
                        for k in range(PK):
                            b = k % BUFS
                            dve.wait_ge(M(f"u_in{b}"), arrivals(t, i, hh, k))
                            nc.vector.scalar_tensor_tensor(out=u_buf[b], in0=u_buf[b], scalar=1.0, in1=m.H[:, t, :], op0=ALU.mult,
                                                           op1=ALU.mult, accum_out=m.dots[:, k:k + 1]).then_inc(M("u_free"), 1)
                            if k % LOT == LOT - 1:
                                lots = ((first + t) * slots + hh * PK + k) // LOT + i * (2 * PK // LOT)
                                dve.wait_ge(M("gelu_done"), lots + 1)
                                a = m.act[:, k + 1 - LOT:k + 1]
                                nc.vector.tensor_tensor(a, a, m.wts[:, hh * PK + k + 1 - LOT:hh * PK + k + 1], ALU.mult)\
                                    .then_inc(M("act_ready"), 1)
                            if hh == 0:
                                stage(k)
                            elif k < LOT:
                                stage(PK + k)
                            if k == LOT - 1:
                                dve.wait_ge(M("v_free"), i * 2 * PK + ((first + t) * slots + hh * PK + BUFS))
                                nc.vector.tensor_copy(cur[1 - hh], m.idx[:, (1 - hh) * PK:(2 - hh) * PK]).then_inc(M("idx_ready"), 1)
                    dve.wait_ge(M("act_ready"), i * (2 * PK // LOT) + ((first + t + 1) * slots // LOT - (pairs - 1) * 2 * PK // LOT))
                    nc.vector.tensor_copy(m.wts[:, 0:2 * PK], m.wts[:, 2 * PK:4 * PK]).then_inc(M("wts_moved"), 1)
                    dve.wait_ge(M("wts_moved"), i + (done + 1))
            finish(tiles - 1)

        @block.scalar
        def _(act):
            searched = first * PAIRS + layer
            top = Search(nc, None, m, M, None, place).top

            def search_exp(count):
                act.wait_ge(M("peer_top"), count)
                nc.scalar.activation(top, top, ACT.Exp).then_inc(M("peer_exp"), 1)

            for t in range(tiles):
                if t:
                    norm_act(nc, act, m, M, n0 + t)
                with act.Fori(0, pairs) as i:
                    for hh in range(2):
                        if hh == 1:
                            search_exp(i + (searched + t * PAIRS + 2))
                        for k in range(PK):
                            n = (first + t) * slots + hh * PK + k
                            if k % LOT == 0:
                                act.wait_ge(M("u_free"), i * 2 * PK + (n + LOT + BUFS))
                                a = slice(k, k + LOT)
                                nc.scalar.activation(m.act[:, a], m.dots[:, a], ACT.Gelu_apprx_tanh).then_inc(M("gelu_done"), 1)
                                act.wait_ge(M("act_ready"), i * (2 * PK // LOT) + (n // LOT + 1))
                            act.wait_ge(M("v_free"), i * 2 * PK + (n - 3 + BUFS))
                            nc.scalar.activation(m.diag[k % 4], m.const("ident"), ACT.Copy, scale=m.act[:, k:k + 1]).then_inc(M("diag_ready"), 1)
            norm_act(nc, act, m, M, n0 + tiles)

        @block.tensor
        def _(pe):
            if first == 0:
                pe.sem_inc(M("v_free"), BUFS)
            for t in range(tiles):
                out = [m.ps[:, sums[t, n][0], :] for n in range(2)]
                for n in range(2):
                    banks.wait_free(pe, sums[t, n])
                    nc.tensor.matmul(out[n], m.const("zero"), m.H[:, t, 0:512], start=True, stop=False, skip_group_check=True)
                with pe.Fori(0, pairs) as i:
                    for hh in range(2):
                        for k in range(PK):
                            n_ = (first + t) * slots + hh * PK + k
                            b = k % BUFS
                            pe.wait_ge(M("diag_ready"), i * 2 * PK + (n_ + 1))
                            pe.wait_ge(M(f"v_in{b}"), i * (16 * 2 * PK // BUFS) + 16 * (n_ // BUFS + 1))
                            for n in range(2):
                                last = nc.tensor.matmul(out[n], m.diag[k % 4], v_buf[b][:, n * 512:(n + 1) * 512],
                                                        start=False, stop=False, skip_group_check=True)
                            last.then_inc(M("v_free"), 1)
                for n in range(2):
                    last = nc.tensor.matmul(out[n], m.const("zero"), m.H[:, t, 0:512], start=False, stop=True, skip_group_check=True)
                    banks.fill(last, sums[t, n])



def gla(nc, d, m, M, banks, ring):
    tiles = 4
    hT = m.part(0, KT, tiles * P)
    k_end = m.part(0, tiles, 2, GH * DK)
    v = m.part(4096, tiles, D)
    g = m.part(8192, tiles, 2, GH * DK)
    k = m.part(12288, tiles, GH * DK)
    o = m.part(12288, TT, D)
    r = m.part(14336, TT, D)
    yT = m.part(0, KT, T)
    H = m.H[:, :, :].rearrange("p a b -> p (a b)")
    qT = H[:, 0:1024].rearrange("p (h t) -> p h t", h=GH)
    kT = H[:, 1024:2048].rearrange("p (h t) -> p h t", h=GH)
    glT = H[:, 2048:3072].rearrange("p (j t) -> p j t", j=2)
    gn = H[:, 3072:4096]
    X2 = m.X[:, 2:4, :].rearrange("p a b -> p (a b)")
    w_gl = X2[:, 0:256].rearrange("p (k j) -> p k j", k=KT)
    w_gate = X2[:, 256:1280].rearrange("p (j n) -> p j n", j=2)
    E = m.ring[:, 4:6, :].rearrange("p a b -> p (a b)")
    q_in = E[:, 0:2048].rearrange("p (j h t) -> p j h t", j=2, h=GH)
    k_in = E[:, 2048:4096].rearrange("p (j h t) -> p j h t", j=2, h=GH)
    S = E[:, 4096:5120].rearrange("p (j b e) -> p j b e", j=2, b=2)
    att = E[:, 5120:6144].rearrange("p (b c) -> p b c", b=2)
    decay = E[:, 6144:6208]
    ab = E[:, 6208:7232].rearrange("p (b c) -> p b c", b=2)
    low = X2[:, 1280:1792]
    assert [(ring.at["b_w_in"] + n) % NSLOT for n in (4, 5)] == [4, 5]

    n0 = m.norms
    m.norms += TT * GH + TT
    new_hT = m.part(4096, KT, T)
    ends = [m.part(8192 + i * D, D) for i in range(4)] + [m.part(2048, D)]
    base = M.n.get("h_ready_now", 0)
    jobs = [("k", 0, t) for t in range(tiles)] + [("kT", 0, i) for i in range(2)]
    jobs += [("v", 1 + n, t) for n in range(2) for t in range(tiles)] + [("qT", 3, i) for i in range(2)]
    jobs += [("r", 4 + n, t) for n in range(2) for t in range(TT)]
    hs = banks.plan([(t, n) for t in range(tiles) for n in range(2)], [4, 5, 6, 7])
    proj = banks.plan([("gl", j) for j in range(2)] + jobs, [0, 1, 2, 3])
    gate_jobs = [(t, j) for t in range(tiles) for j in range(2)]
    zs = banks.plan([("z", t, j) for t, j in gate_jobs], [4, 5])
    early_ab = m.part(15360, 2, 512)
    cums = banks.plan([("b", j, i) for j in range(2) for i in range(2)], [6, 7])
    sufs = banks.plan([("e", t, j) for t in range(tiles) for j in range(2)] + ["decay"], [6, 7])
    atts = banks.plan([("att", h) for h in range(GH)], [2, 3])
    outs = banks.plan([("o", h) for h in range(GH)], [0, 1])
    steps = [[(2 + c // 2, c % 2) for c in order] + [(c // 2, c % 2) for c in order]
             for order in (range(4), range(3, -1, -1))]
    kv = {}
    for h in range(GH):
        for s in range(7):
            for j in range(2):
                kv[h, s, j] = banks.plan(["x"], [4 + 2 * j + steps[j][s][1]])["x"]
    turned = banks.plan([(t, n) for t in range(TT) for n in range(2)], [4, 5, 6, 7])
    sums = banks.plan([(t, n) for t in range(TT) for n in range(2)], [0, 1, 2, 3])
    back = banks.plan([(t, n) for t in range(TT) for n in range(2)], [4, 5, 6, 7])

    with nc.Block() as block:

        @block.sync
        def _(sp):
            sp.dma_start(w_gl, d["b_w_gl"]).then_inc(M("gla_in"), 16)
            sp.dma_start(w_gate[0:RANK + 1, :, :], d["b_w_gate"]).then_inc(M("gla_in"), 16)
            ring.load(sp, ring.at["b_w_in"] + NSLOT)
            banks.wait_full(sp, hs[3, 1])
            sp.dma_start(gn, d["b_gn_g"].to_broadcast([P, D])).then_inc(M("gn_in"), 16)
            ring.load(sp, ring.at["b_w_out"] + 2 + NSLOT)
            sp.wait_ge(M("y_gla"), 1)
            load_rows(sp, M, m, residual_rows(d, 1, 0, GATE1, 1) + [mod_row(d, 1, 0, w) for w in (SCALE2, SHIFT2)], ends)

        @block.tensor
        def _(pe):
            for t in range(tiles):
                turn_h(nc, pe, m, M, banks, hs, t, base)
            pe.wait_ge(M("gla_in"), 32)
            for t in range(tiles):
                for n in range(2):
                    pe.wait_ge(M(f"bank_free{hs[t, n][0]}"), hs[t, n][1] + 1)
            for j in range(2):
                where = proj["gl", j]
                banks.wait_free(pe, where)
                banks.fill(products(nc, m.ps[0:RANK, where[0], :], [(w_gl[:, c, j * RANK:(j + 1) * RANK], hT[:, c, :]) for c in range(KT)]), where)
            for n, job in enumerate(jobs):
                kind, chunk, i = job
                if n % 2 == 0 and n // 2 < len(gate_jobs):
                    if n == 0:
                        pe.wait_ge(M("glT_ready"), 2)
                    t, j = gate_jobs[n // 2]
                    where = zs["z", t, j]
                    banks.wait_free(pe, where)
                    banks.fill(nc.tensor.matmul(m.ps[:, where[0], :], glT[0:RANK + 1, j, t * P:(t + 1) * P], w_gate[0:RANK + 1, j, :],
                                                start=True, stop=True), where)
                w = ring.wait(pe, "b_w_in", chunk)
                where = proj[job]
                banks.wait_free(pe, where)
                if kind in ("kT", "qT"):
                    for half in range(2):
                        col = (2 * i + half) * P
                        last = products(nc, m.ps[:, where[0], half * T:(half + 1) * T],
                                        [(w[:, c, col:col + P], hT[:, c, 0:T]) for c in range(KT)])
                else:
                    last = products(nc, m.ps[:, where[0], :], [(hT[:, c, i * P:(i + 1) * P], w[:, c, :]) for c in range(KT)])
                banks.fill(last, where)
                if n + 1 == len(jobs) or jobs[n + 1][1] != chunk:
                    pe.wait_ge(M(f"bank_full{where[0]}"), where[1] + 1)
                    pe.sem_inc(M(f"chunk_used{(ring.at['b_w_in'] + chunk) % NSLOT}"), 1)
                    if n + 1 == len(jobs):
                        pe.sem_inc(M("projected"), 1)
            pe.wait_ge(M("g_ready_gla"), tiles * 2)
            for j in range(2):
                for i in range(2):
                    where = cums["b", j, i]
                    banks.wait_free(pe, where)
                    for half in range(2):
                        for t in range(TT):
                            c = (2 * i + half) * DK
                            last = nc.tensor.matmul(m.ps[:, where[0], half * T + t * P:half * T + (t + 1) * P], g[:, t, j, c:c + DK],
                                                    m.const(("fwd", "bwd")[j]), start=True, stop=True)
                    banks.fill(last, where)
            for t in range(tiles):
                for j in range(2):
                    where = sufs["e", t, j]
                    banks.wait_free(pe, where)
                    banks.fill(nc.tensor.matmul(m.ps[:, where[0], :], m.const(("after", "before")[j]), g[:, t, j, :], start=True, stop=True), where)
            where = sufs["decay"]
            banks.wait_free(pe, where)
            for t in range(tiles):
                for j in range(2):
                    for h in range(GH):
                        col = (j * GH + h) * 8 + 2 * t
                        last = nc.tensor.matmul(m.ps[:, where[0], col:col + 2], g[:, t, j, h * DK:(h + 1) * DK], m.const("chunk"),
                                                start=True, stop=True)
            banks.fill(last, where)

            def scores(h):
                where = atts["att", h]
                banks.wait_free(pe, where)
                for j in range(2):
                    for t in range(TT):
                        cols = slice(t * P, (t + 1) * P)
                        last = nc.tensor.matmul(m.ps[:, where[0], (j * TT + t) * P:(j * TT + t + 1) * P], k_in[:, j, h, cols],
                                                q_in[:, j, h, cols], start=True, stop=True)
                banks.fill(last, where)

            pe.wait_ge(M("in_ready"), 8)
            pe.wait_ge(M("k_end_ready"), tiles * 2)
            scores(0)
            for h in range(GH):
                if h + 1 < GH:
                    scores(h + 1)
                e = slice(h * DV, (h + 1) * DV)
                where = outs["o", h]
                banks.wait_free(pe, where)
                pe.wait_ge(M("att_masked"), h + 1)
                for t in range(TT):
                    for j in range(2):
                        nc.tensor.matmul(m.ps[:, where[0], t * DV:(t + 1) * DV], att[:, h % 2, (j * TT + t) * P:(j * TT + t + 1) * P],
                                         v[:, t, e], start=t == 0 and j == 0, stop=False, skip_group_check=True)
                for s in range(8):
                    for j in range(2):
                        t, c = steps[j][s]
                        rows_ = slice(c * CH, (c + 1) * CH)
                        if s >= 4:
                            pe.wait_ge(M(f"state_ready{j}"), 7 * h + s)
                            last = nc.tensor.matmul(m.ps[rows_, where[0], t * DV:(t + 1) * DV],
                                                    q_in[:, j, h, t * P + c * CH:t * P + (c + 1) * CH], S[:, j, (s - 1) % 2, :],
                                                    start=False, stop=s == 7, skip_group_check=True)
                            if s == 7 and j == 1:
                                banks.fill(last, where)
                            else:
                                last.then_inc(M(f"state_read{j}"), 1)
                        if s < 7:
                            there = kv[h, s, j]
                            banks.wait_free(pe, there)
                            banks.fill(nc.tensor.matmul(m.ps[:, there[0], 0:DV], k_end[rows_, t, j, h * DK:(h + 1) * DK], v[rows_, t, e],
                                                        start=True, stop=True), there)
            for t in range(TT):
                pe.wait_ge(M("y_gla"), t + 1)
                for n in range(2):
                    where = turned[t, n]
                    banks.wait_free(pe, where)
                    for c in range(4):
                        at = (4 * n + c) * P
                        last = nc.tensor.transpose(m.ps[:, where[0], c * P:(c + 1) * P], o[:, t, at:at + P], m.const("ident"))
                    banks.fill(last, where)
            pe.wait_ge(M("yT_gla"), 2 * TT)
            w = [ring.wait(pe, "b_w_out", n) for n in range(2)]
            for t in range(TT):
                for n in range(2):
                    where = sums[t, n]
                    banks.wait_free(pe, where)
                    last = products(nc, m.ps[:, where[0], :], [(yT[:, c, t * P:(t + 1) * P], w[n][:, c, :]) for c in range(KT)])
                    banks.fill(last, where)
            for n in range(2):
                pe.wait_ge(M(f"bank_full{sums[TT - 1, n][0]}"), sums[TT - 1, n][1] + 1)
                pe.sem_inc(M(f"chunk_used{(ring.at['b_w_out'] + n) % NSLOT}"), 1)
            for t in range(TT):
                turn_h(nc, pe, m, M, banks, back, t, base + t + 1)

        @block.scalar
        def _(act):
            for t in range(tiles):
                hT_out(nc, act, m, banks, hs, hT, t)
            act.wait_ge(M("glT_ones"), 1)
            for j in range(2):
                where = proj["gl", j]
                banks.wait_full(act, where)
                banks.free_chained(act, nc.scalar.activation(glT[0:RANK, j, :], m.ps[0:RANK, where[0], :], ACT.Copy), where)
                act.sem_inc(M("glT_ready"), 1)
            for n, job in enumerate(jobs):
                kind, chunk, i = job
                if n % 2 == 0 and n // 2 < len(gate_jobs):
                    act.wait_ge(M("abs_ready"), n // 2 + 1)
                    a = early_ab[:, n // 2 % 2, :]
                    nc.scalar.activation(a, a, ACT.Exp, scale=-1.0).then_inc(M("act_step"), 1)
                    act.wait_ge(M("act_step"), n // 2 + 1)
                    nc.scalar.activation(a, a, ACT.Ln, bias=1.0).then_inc(M("log_ready"), 1)
                if kind == "r":
                    act.wait_ge(M("g_ready_gla"), len(gate_jobs))
                where = proj[job]
                banks.wait_full(act, where)
                src = m.ps[:, where[0], :]
                func, scale = ACT.Copy, 1.0
                if kind == "k":
                    dst = k[:, i, :]
                elif kind == "v":
                    dst = v[:, i, (chunk - 1) * 512:chunk * 512]
                elif kind == "r":
                    dst, func = r[:, i, (chunk - 4) * 512:(chunk - 3) * 512], ACT.Silu
                else:
                    dst = (kT if kind == "kT" else qT)[:, 2 * i:2 * i + 2, :].rearrange("p a b -> p (a b)")
                    scale = 1.0 if kind == "kT" else DK ** -0.5
                banks.free_chained(act, nc.scalar.activation(dst, src, func, scale=scale), where)
                act.sem_inc(M("gla_proj"), 1)
            act.wait_ge(M("projected"), 1)
            for n, (j, i) in enumerate([(j, i) for j in range(2) for i in range(2)]):
                where = cums["b", j, i]
                banks.wait_full(act, where)
                for sign in range(2):
                    if n or sign:
                        pass
                    if 2 * n + sign >= 2:
                        act.wait_ge(M("in_ready"), 2 * n + sign - 1)
                    ins = nc.scalar.activation(ab[:, sign, :], m.ps[:, where[0], :], ACT.Exp, scale=(1 - 2 * sign) / TAU)
                    if sign:
                        banks.free_chained(act, ins, where)
                        act.sem_inc(M("exp_ready_gla"), 1)
                    else:
                        ins.then_inc(M("exp_ready_gla"), 1)
                        act.wait_ge(M("exp_ready_gla"), 2 * n + 1)
            for n, (t, j) in enumerate([(t, j) for t in range(tiles) for j in range(2)]):
                where = sufs["e", t, j]
                banks.wait_full(act, where)
                if n < 2:
                    act.wait_ge(M("in_ready"), 8)
                else:
                    act.wait_ge(M("k_end_ready"), n - 1)
                banks.free_chained(act, nc.scalar.activation(ab[:, n % 2, :], m.ps[:, where[0], :], ACT.Exp, scale=1.0 / TAU), where)
                act.sem_inc(M("suffix_ready"), 1)
            where = sufs["decay"]
            banks.wait_full(act, where)
            banks.free_chained(act, nc.scalar.activation(decay, m.ps[:, where[0], 0:64], ACT.Exp, scale=1.0 / TAU), where)
            act.sem_inc(M("decay_ready"), 1)
            for n in range(TT * GH):
                norm_act(nc, act, m, M, n0 + n + 1)
            for t in range(TT):
                for n in range(2):
                    where = turned[t, n]
                    banks.wait_full(act, where)
                    ins = nc.scalar.activation(yT[:, 4 * n:4 * n + 4, t * P:(t + 1) * P],
                                               m.ps[:, where[0], :].rearrange("p (c q) -> p c q", c=4), ACT.Copy)
                    banks.free_chained(act, ins, where)
                    act.sem_inc(M("yT_gla"), 1)
            for t in range(TT):
                norm_act(nc, act, m, M, n0 + TT * GH + t + 1)
            for t in range(TT):
                hT_out(nc, act, m, banks, back, new_hT, t)

        @block.vector
        def _(dve):
            step = Chain(M, dve, "dve_step")
            banks.wait_full(dve, hs[2, 1])
            step(nc.vector.memset(glT[0:RANK + 1, :, :], 1.0), "glT_ones")
            for n, (t, j) in enumerate([(t, j) for t in range(tiles) for j in range(2)]):
                where = zs["z", t, j]
                banks.wait_full(dve, where)
                z = m.ps[:, where[0], :]
                step(nc.vector.tensor_copy(low, z))
                a = early_ab[:, n % 2, :]
                ins = nc.vector.scalar_tensor_tensor(out=a, in0=z, scalar=-1.0, in1=low, op0=ALU.mult, op1=ALU.max)
                banks.free_chained(dve, ins, where)
                dve.sem_inc(M("abs_ready"), 1)
                dve.wait_ge(M("log_ready"), n + 1)
                step(nc.vector.scalar_tensor_tensor(out=g[:, t, j, :], in0=low, scalar=0.0, in1=a, op0=ALU.min, op1=ALU.subtract), "g_ready_gla")
            dve.wait_ge(M("gla_proj"), len(jobs))
            dve.wait_ge(M("projected"), 1)
            for n, (j, i) in enumerate([(j, i) for j in range(2) for i in range(2)]):
                for sign, (dst, src) in enumerate(((q_in, qT), (k_in, kT))):
                    dve.wait_ge(M("exp_ready_gla"), 2 * n + sign + 1)
                    step(nc.vector.tensor_tensor(dst[:, j, 2 * i:2 * i + 2, :].rearrange("p a b -> p (a b)"),
                                                 src[:, 2 * i:2 * i + 2, :].rearrange("p a b -> p (a b)"), ab[:, sign, :], ALU.mult), "in_ready")
            for n, (t, j) in enumerate([(t, j) for t in range(tiles) for j in range(2)]):
                dve.wait_ge(M("suffix_ready"), n + 1)
                step(nc.vector.tensor_tensor(k_end[:, t, j, :], k[:, t, :], ab[:, n % 2, :], ALU.mult), "k_end_ready")
            dve.wait_ge(M("decay_ready"), 1)

            def masked(h):
                where = atts["att", h]
                banks.wait_full(dve, where)
                if h >= 2:
                    banks.wait_full(dve, outs["o", h - 2])
                a = att[:, h % 2, :]
                banks.free_chained(dve, nc.vector.tensor_scalar(a, m.ps[:, where[0], :], -LOWEST, LOWEST, ALU.min, ALU.max), where)
                for j in range(2):
                    part = a[:, j * T:(j + 1) * T].rearrange("p (t i) -> p t i", t=TT)
                    mask = m.const(("fwd", "bwd")[j]).rearrange("p (o i) -> p o i", o=1).to_broadcast([P, TT, P])
                    ins = nc.vector.tensor_tensor(part, part, mask, ALU.mult)
                    if j == 0:
                        step(ins)
                    else:
                        step(ins, "att_masked")

            masked(0)
            for h in range(GH):
                if h + 1 < GH:
                    masked(h + 1)
                for s in range(7):
                    for j in range(2):
                        t, c = steps[j][s]
                        there = kv[h, s, j]
                        banks.wait_full(dve, there)
                        if s >= 5:
                            dve.wait_ge(M(f"state_read{j}"), (4 - j) * h + s - 4)
                        elif s <= 1 and h:
                            banks.wait_full(dve, outs["o", h - 1])
                        new, kv_ = S[:, j, s % 2, :], m.ps[:, there[0], 0:DV]
                        if s == 0:
                            ins = nc.vector.tensor_copy(new, kv_)
                        else:
                            col = (j * GH + h) * 8 + 2 * t + c
                            ins = nc.vector.scalar_tensor_tensor(out=new, in0=S[:, j, (s - 1) % 2, :], scalar=decay[:, col:col + 1], in1=kv_,
                                                                 op0=ALU.mult, op1=ALU.add)
                        banks.free_chained(dve, ins, there)
                        dve.sem_inc(M(f"state_ready{j}"), 1)
                where = outs["o", h]
                banks.wait_full(dve, where)
                for t in range(TT):
                    norm_dve(nc, dve, step, m, M, m.ps[:, where[0], t * DV:(t + 1) * DV], n0 + TT * h + t + 1,
                             out=o[:, t, h * DV:(h + 1) * DV])
                banks.free_chained(dve, nc.vector.memset(m.stats[:, 40:41], 0.0), where)
            dve.wait_ge(M("gn_in"), 16)
            for t in range(TT):
                step(nc.vector.tensor_tensor(o[:, t, :], o[:, t, :], gn, ALU.mult))
                step(nc.vector.tensor_tensor(o[:, t, :], o[:, t, :], r[:, t, :], ALU.mult), "y_gla")
            dve.wait_ge(M("rows_in"), m.rows_sent)
            for t in range(TT):
                residual_tile(nc, dve, step, m, M, banks, sums, t, n0 + TT * GH + t + 1, ends[0], ends[1], ends[2])
                modulate_tile(nc, step, m, t, ends[3], ends[4])


LASTING = ("bank_", "chunk_", "dve_step", "rows_in", "variance_ready", "std_ready", "consts_in")



def program(nc, d, out):
    with ExitStack() as ctx:
        m = Memory(nc, ctx)
        d = dict(d, mod=nc.dram_tensor("mod_rows", [2, 2, 6 * D], F32, kind="Internal").ap())
        M = Marks(nc, ctx)
        banks = Banks(M)
        chunks = [("w_in", d["w_in"][n], SLOT) for n in range(N_IN)]
        chunks += [("w_mod", d["w_mod"][n], SLOT) for n in range(24)]
        chunks += [("w_proj_a", d["w_proj_a"], 2 * D)]
        chunks += [("w_proj_b", d["w_proj_b"][n], SLOT) for n in range(2)]
        chunks += [("w_out", d["w_out"][n], SLOT) for n in range(2)]
        chunks += [("moe", d["moe"][n // PER_EXPERT, n % PER_EXPERT], SLOT) for n in range(PER_EXPERT * NE)]
        chunks += [("a_w_in", d["a_w_in"][n], SLOT) for n in range(4)]
        chunks += [("a_w_out", d["a_w_out"][n], SLOT) for n in range(2)]
        chunks += [("w_q0", d["w_q"][0, n], SLOT) for n in range(2)]
        chunks += [("b_w_in", d["b_w_in"][n], SLOT) for n in range(6)]
        chunks += [("b_w_out", d["b_w_out"][n], SLOT) for n in range(2)]
        chunks += [("w_q1", d["w_q"][1, n], SLOT) for n in range(2)]
        ring = Ring(M, m.ring, chunks)
        attention(nc, d, m, M, banks, ring)
        route(nc,d,m,M,banks,ring)
        moe(nc,d,m,M,banks,ring)
        M.retire(LASTING)
        chunk_mlp(nc, d, m, M, banks, ring)
        scores(nc, d, m, M, banks, ring, 0, 4)
        peer(nc, d, m, M, banks, 0, 4, 0)
        gla(nc, d, m, M, banks, ring)
        scores(nc, d, m, M, banks, ring, 1, 2)
        peer(nc, d, m, M, banks, 1, 2, 4, out)


def chunked(w):
    lead = w.shape[:-2]
    n = w.shape[-1] // 512
    w = w.reshape(*lead, KT, P, n, 512)
    k = len(lead)
    return np.ascontiguousarray(w.transpose(*range(k), k + 2, k + 1, k, k + 3)).reshape(*lead, n, P, KT * 512)


def pair_heads(w, axis):
    w = np.moveaxis(w, axis, -1)
    w = w.reshape(*w.shape[:-1], 2, SWA_PAIRS, HD).swapaxes(-3, -2).reshape(*w.shape[:-1], -1)
    return np.moveaxis(w, -1, axis)


def layout(i):
    w = i["w_in"][0]
    qa, ka, va, qb, kb, vb, ga, gb = np.split(w, np.cumsum([768, 768, 768, 1024, 128, 128, 1024]), axis=1)
    w_in = np.concatenate([qa, ka, pair_heads(qb, 1), kb, va, vb, ga, gb], axis=1)
    moe = np.stack([i[n][0] for n in ("w_gate", "w_up", "w_down")], 1).reshape(NE, PER_EXPERT, KT // 2, P, D)
    moe = moe.transpose(0, 1, 3, 2, 4).reshape(NE, PER_EXPERT, P, SLOT)
    out = {
        "x": i["x"][0],
        "xT": i["x"][0].T.reshape(KT, P, T).transpose(1, 0, 2),
        "w_in": chunked(w_in),
        "w_proj_a": i["w_proj_a"][0].reshape(2, P, D).transpose(1, 0, 2).reshape(P, 2 * D),
        "w_proj_b": chunked(pair_heads(i["w_proj_b"][0], 0)),
        "w_out": chunked(i["w_out"][0]),
        "sinks": i["sinks"],
        "moe": moe,
        "lns": np.stack([i["ln1_g"][0], i["ln1_b"][0], i["ln2_g"][0], i["ln2_b"][0]]),
        "router_w": i["router_w"][0].reshape(KT, P, NE).transpose(1, 0, 2),
        "router_b": i["router_b"],
        "b_gate": i["b_gate"][0],
        "b_up": i["b_up"][0],
        "b_down": i["b_down"][0],
        "c": np.stack([i["c_2"][0], i["c_ctx_2"]]).reshape(2, KT, P).transpose(2, 1, 0),
        "ctx": i["ctx_2"][0],
        "w_mod": i["w_mod_2"].reshape(2, 4, 2, P, 3, 2048).transpose(0, 4, 1, 3, 2, 5).reshape(24, P, SLOT),
        "b_mod": i["b_mod_2"].reshape(24, 512),
        "ln_g": i["ln_g_2"].reshape(4, D),
        "ln_b": i["ln_b_2"].reshape(4, D),
        "a_w_in": chunked(np.concatenate([i["a_w_in_2"][0][:, D:], i["a_w_in_2"][0][:, :D]], 1)),
        "a_norm": np.stack([i["a_norm_g_2"][0], i["a_norm_b_2"][0]]),
        "a_w_s": i["a_w_s_2"][0].transpose(2, 0, 1),
        "a_b_s": i["a_b_s_2"][0].T,
        "a_w_out": chunked(i["a_w_out_2"][0]),
        "b_w_in": chunked(np.concatenate([i["b_w_in_2"][0][:, a:b] for a, b in ((512, 1024), (1024, 2048), (0, 512), (2048, 3072))], 1)),
        "b_w_gl": i["b_w_in_2"][0][:, 3072:].reshape(KT, P, 2 * RANK).transpose(1, 0, 2),
        "b_w_gate": np.concatenate([i["b_w_gate_2"][0], i["b_gate_bias_2"][0][:, None, :]], 1).transpose(1, 0, 2),
        "b_gn_g": i["b_gn_g_2"],
        "b_w_out": chunked(i["b_w_out_2"][0]),
        "w_q": chunked(i["p_w_q_2"]),
        "keys": i["p_keys_2"].transpose(0, 1, 3, 2).reshape(2, P, NKEY),
        "u0": i["p_u_2"][0], "u1": i["p_u_2"][1], "v0": i["p_v_2"][0], "v1": i["p_v_2"][1],
    }
    out["consts"] = np.concatenate([np.asarray(a, np.float32) for a in constants().values()], 1)
    out["dist"] = distances()
    return out


def kernel(**inputs):
    import numpy as _np
    import concourse.bacc as _bacc
    from concourse import mybir as _mybir
    from concourse.bass_utils import run_bass_kernel_spmd as _run

    nc = _bacc.Bacc("TRN2", target_bir_lowering=False, num_devices=1)
    arrays, aps = {}, {}
    for name, a in layout({k: _np.asarray(v) for k, v in inputs.items()}).items():
        a = _np.ascontiguousarray(a)
        arrays[f"in_{name}"] = a
        aps[name] = nc.dram_tensor(f"in_{name}", a.shape, _mybir.dt.from_np(a.dtype), kind="ExternalInput").ap()
    out = nc.dram_tensor("out_0", (1, T, D), _mybir.dt.float32, kind="ExternalOutput").ap()
    program(nc, aps, out)
    r = _run(nc, [arrays], core_ids=[0])
    return r.results[0]["out_0"]
```
